# Optimizing a Trainium2 kernel written in Bass

```python
import jax, jax.numpy as jnp
from jax import lax
import numpy as np
import math

D_MODEL = 1024
BATCH = 1
SEQ = 256
DEPTH = 2

MIX_WIDTH = D_MODEL
ATTN_WIDTH = MIX_WIDTH // 2
POOL_WIDTH = MIX_WIDTH - ATTN_WIDTH
HEAD_DIM = 64
N_HEADS = ATTN_WIDTH // HEAD_DIM
N_KV_HEADS = 2
GROUP = N_HEADS // N_KV_HEADS
KV_WIDTH = N_KV_HEADS * HEAD_DIM
WINDOW = 128
BLOCK = 128
ROT_DIM = HEAD_DIM // 4
ROPE_THETA = 500000.0
POOL_WINDOWS = (2, 4, 8, 16)
N_POOL_GROUPS = len(POOL_WINDOWS)
POOL_GROUP_WIDTH = POOL_WIDTH // N_POOL_GROUPS
IN_WIDTH = ATTN_WIDTH + 2 * KV_WIDTH + POOL_WIDTH
D_FF = ((int(np.ceil(8 * D_MODEL / 3)) + 255) // 256) * 256
N_MOD = 6
EPS = 1e-6
NEG_INF = -1e30


def rms_norm(x, g):
    xf = x.astype(jnp.float32)
    y = xf * lax.rsqrt(jnp.mean(xf * xf, axis=-1, keepdims=True) + EPS)
    return (y * g.astype(jnp.float32)).astype(x.dtype)

def partial_rotary(t, positions):
    inv_freq = ROPE_THETA ** (-jnp.arange(0, ROT_DIM, 2, dtype=jnp.float32) / ROT_DIM)
    ang = positions.astype(jnp.float32)[:, :, None] * inv_freq
    cos = jnp.cos(ang)[:, :, None, :]
    sin = jnp.sin(ang)[:, :, None, :]
    tf = t.astype(jnp.float32)
    half = ROT_DIM // 2
    t1, t2, rest = tf[..., :half], tf[..., half:ROT_DIM], tf[..., ROT_DIM:]
    rot = jnp.concatenate([t1 * cos - t2 * sin, t2 * cos + t1 * sin, rest], axis=-1)
    return rot.astype(t.dtype)

def sliding_window_attention_with_sinks(q, k, v, sinks):
    B, S = q.shape[0], q.shape[1]
    nb = S // BLOCK
    qb = q.reshape(B, nb, BLOCK, N_KV_HEADS, GROUP, HEAD_DIM)
    kb = k.reshape(B, nb, BLOCK, N_KV_HEADS, HEAD_DIM)
    vb = v.reshape(B, nb, BLOCK, N_KV_HEADS, HEAD_DIM)
    pad = ((0, 0), (1, 0), (0, 0), (0, 0), (0, 0))
    k_cat = jnp.concatenate([jnp.pad(kb, pad)[:, :-1], kb], axis=2)
    v_cat = jnp.concatenate([jnp.pad(vb, pad)[:, :-1], vb], axis=2)
    scores = jnp.einsum("bnqkgd,bnskd->bnkgqs", qb, k_cat).astype(jnp.float32)
    scores = scores * (HEAD_DIM ** -0.5)
    qi = jnp.arange(BLOCK)[:, None]
    kj = jnp.arange(2 * BLOCK)[None, :]
    diff = qi + BLOCK - kj
    blk = jnp.arange(nb)[:, None, None]
    key_abs = blk * BLOCK + kj[None] - BLOCK
    valid = (diff[None] >= 0) & (diff[None] < WINDOW) & (key_abs >= 0)
    scores = jnp.where(valid[None, :, None, None], scores, NEG_INF)
    sink = jnp.broadcast_to(
        sinks.astype(jnp.float32).reshape(1, 1, N_KV_HEADS, GROUP, 1, 1),
        scores.shape[:-1] + (1,))
    probs = jax.nn.softmax(jnp.concatenate([scores, sink], axis=-1), axis=-1)[..., :-1]
    out = jnp.einsum("bnkgqs,bnskd->bnqkgd", probs.astype(v.dtype), v_cat)
    return out.reshape(B, S, N_HEADS * HEAD_DIM)

def causal_pool_mixer(u, pool_w, pool_scale):
    S = u.shape[1]
    t = jnp.arange(S, dtype=jnp.float32)[None, :, None]
    outs = []
    for gi, w in enumerate(POOL_WINDOWS):
        ug = u[..., gi * POOL_GROUP_WIDTH:(gi + 1) * POOL_GROUP_WIDTH].astype(jnp.float32)
        cs = jnp.pad(jnp.cumsum(ug, axis=1), ((0, 0), (1, 0), (0, 0)))
        upper = cs[:, 1:]
        lower = jnp.pad(cs, ((0, 0), (w - 1, 0), (0, 0)))[:, :S]
        count = jnp.minimum(t + 1.0, float(w))
        pooled = (upper - lower) / count - ug
        outs.append(jnp.einsum("bsc,cd->bsd", pooled.astype(u.dtype), pool_w[gi]))
    return jnp.concatenate(outs, axis=-1) * pool_scale

def first_inputs(seed: int = 0) -> dict:
    key = jax.random.key(seed)
    ks = jax.random.split(key, 20)
    f32 = jnp.float32
    def nrm(k, shape, scale):
        return jax.random.normal(k, shape, f32) * scale
    x = jax.random.normal(ks[0], (BATCH, SEQ, D_MODEL), f32)
    c = jax.random.normal(ks[1], (BATCH, D_MODEL), f32)
    offsets = jax.random.randint(ks[2], (BATCH, 1), 0, 4096, dtype=jnp.int32)
    positions = (offsets + jnp.arange(SEQ, dtype=jnp.int32)[None, :]).astype(jnp.int32)
    return {
        "x": x,
        "c": c,
        "positions": positions,
        "ada_w": nrm(ks[3], (DEPTH, D_MODEL, N_MOD * D_MODEL), D_MODEL ** -0.5),
        "ada_b": nrm(ks[4], (DEPTH, N_MOD * D_MODEL), 0.02),
        "w_in": nrm(ks[5], (DEPTH, D_MODEL, IN_WIDTH), D_MODEL ** -0.5),
        "b_in": nrm(ks[6], (DEPTH, IN_WIDTH), 0.02),
        "sinks": nrm(ks[7], (DEPTH, N_HEADS), 1.0),
        "pool_w": nrm(ks[8], (DEPTH, N_POOL_GROUPS, POOL_GROUP_WIDTH, POOL_GROUP_WIDTH), POOL_GROUP_WIDTH ** -0.5),
        "pool_scale": 1.0 + nrm(ks[9], (DEPTH, POOL_WIDTH), 0.1),
        "w_out": nrm(ks[10], (DEPTH, MIX_WIDTH, D_MODEL), MIX_WIDTH ** -0.5),
        "w_gate": nrm(ks[11], (DEPTH, D_MODEL, D_FF), D_MODEL ** -0.5),
        "w_up": nrm(ks[12], (DEPTH, D_MODEL, D_FF), D_MODEL ** -0.5),
        "w_down": nrm(ks[13], (DEPTH, D_FF, D_MODEL), D_FF ** -0.5),
        "g_pre_mix": 1.0 + nrm(ks[14], (DEPTH, D_MODEL), 0.02),
        "g_post_mix": 1.0 + nrm(ks[15], (DEPTH, D_MODEL), 0.02),
        "g_pre_ffn": 1.0 + nrm(ks[16], (DEPTH, D_MODEL), 0.02),
        "g_post_ffn": 1.0 + nrm(ks[17], (DEPTH, D_MODEL), 0.02),
    }

def first_block(x, c, positions, ada_w, ada_b, w_in, b_in, sinks, pool_w, pool_scale,
              w_out, w_gate, w_up, w_down, g_pre_mix, g_post_mix, g_pre_ffn, g_post_ffn):
    B, S = x.shape[0], x.shape[1]
    c_act = jax.nn.silu(c)
    for l in range(DEPTH):
        mod = c_act @ ada_w[l] + ada_b[l]
        shift_m, scale_m, gate_m, shift_f, scale_f, gate_f = [
            m[:, None, :] for m in jnp.split(mod, N_MOD, axis=-1)]

        h = rms_norm(x, g_pre_mix[l]) * (1.0 + scale_m) + shift_m
        proj = h @ w_in[l] + b_in[l]
        q, k, v, u = jnp.split(
            proj, [ATTN_WIDTH, ATTN_WIDTH + KV_WIDTH, ATTN_WIDTH + 2 * KV_WIDTH], axis=-1)
        q = partial_rotary(q.reshape(B, S, N_HEADS, HEAD_DIM), positions)
        k = partial_rotary(k.reshape(B, S, N_KV_HEADS, HEAD_DIM), positions)
        v = v.reshape(B, S, N_KV_HEADS, HEAD_DIM)
        attn_out = sliding_window_attention_with_sinks(q, k, v, sinks[l])
        pool_out = causal_pool_mixer(u, pool_w[l], pool_scale[l])
        mix = jnp.concatenate([attn_out, pool_out], axis=-1) @ w_out[l]
        x = x + gate_m * rms_norm(mix, g_post_mix[l])

        h = rms_norm(x, g_pre_ffn[l]) * (1.0 + scale_f) + shift_f
        f = (jax.nn.silu(h @ w_gate[l]) * (h @ w_up[l])) @ w_down[l]
        x = x + gate_f * rms_norm(f, g_post_ffn[l])
    return x


MLA_HEADS = 4
MLA_NOPE = 128
MLA_ROPE = 64
MLA_V = 128
MLA_Q_RANK = 384
MLA_KV_RANK = 256
MLA_ROPE_BASE = 10000.0
Q_BLOCK = 128
GLA_HEADS = 4
GLA_DK = 32
GLA_DV = 64
GLA_GATE_RANK = 16
GLA_GATE_NORM = 16.0
GLA_CHUNK = 64
RET_HEADS = 4
RET_DK = 32
RET_DV = 64
RET_CHUNK = 64
RET_ROPE_BASE = 10000.0
D_MIX = MLA_HEADS * MLA_V + GLA_HEADS * GLA_DV + RET_HEADS * RET_DV
IN_SIZES = (MLA_Q_RANK, MLA_KV_RANK, MLA_ROPE,
            GLA_HEADS * GLA_DK, GLA_HEADS * GLA_DK, GLA_HEADS * GLA_DV, GLA_GATE_RANK, GLA_HEADS * GLA_DV,
            RET_HEADS * RET_DK, RET_HEADS * RET_DK, RET_HEADS * RET_DV, RET_HEADS * RET_DV)
D_IN = sum(IN_SIZES)
D_FF_2 = 2816
CONV_W = 3


def rmsnorm(x, gain):
    xf = x.astype(jnp.float32)
    y = xf * lax.rsqrt(jnp.mean(xf * xf, axis=-1, keepdims=True) + EPS)
    return (y * gain.astype(jnp.float32)).astype(x.dtype)

def head_rmsnorm(x, gain):
    H, d = x.shape[-2], x.shape[-1]
    return rmsnorm(x, gain.reshape(H, d))

def rope_tables(S, dim, base):
    inv = base ** (-(jnp.arange(0, dim, 2, dtype=jnp.float32) / dim))
    ang = jnp.arange(S, dtype=jnp.float32)[:, None] * inv[None, :]
    return jnp.cos(ang), jnp.sin(ang)

def apply_rope(x, cos, sin):
    half = x.shape[-1] // 2
    c = cos[None, :, None, :].astype(x.dtype)
    s = sin[None, :, None, :].astype(x.dtype)
    x1, x2 = x[..., :half], x[..., half:]
    return jnp.concatenate([x1 * c - x2 * s, x2 * c + x1 * s], axis=-1)

def mla_attention(q_nope, q_rope, k_nope, k_rope, v):
    B, S, H, dn = q_nope.shape
    dr = q_rope.shape[-1]
    nb = S // Q_BLOCK
    scale = (MLA_NOPE + MLA_ROPE) ** -0.5
    qn = q_nope.reshape(B, nb, Q_BLOCK, H, dn).transpose(1, 0, 2, 3, 4)
    qr = q_rope.reshape(B, nb, Q_BLOCK, H, dr).transpose(1, 0, 2, 3, 4)
    key_pos = jnp.arange(S)

    def one_block(args):
        qn_b, qr_b, start = args
        s = (jnp.einsum('bqhd,bkhd->bhqk', qn_b, k_nope)
             + jnp.einsum('bqhd,bkd->bhqk', qr_b, k_rope)).astype(jnp.float32) * scale
        q_pos = start + jnp.arange(Q_BLOCK)
        mask = key_pos[None, :] <= q_pos[:, None]
        s = jnp.where(mask[None, None], s, jnp.finfo(jnp.float32).min)
        p = jax.nn.softmax(s, axis=-1).astype(v.dtype)
        return jnp.einsum('bhqk,bkhd->bqhd', p, v)

    out = lax.map(one_block, (qn, qr, jnp.arange(nb) * Q_BLOCK))
    return out.transpose(1, 0, 2, 3, 4).reshape(B, S, H, v.shape[-1])

def mla_branch(c_q, c_kv, k_rope, q_norm, w_uq, kv_norm, w_ukv, cos, sin):
    B, S, _ = c_q.shape
    q = (rmsnorm(c_q, q_norm) @ w_uq).reshape(B, S, MLA_HEADS, MLA_NOPE + MLA_ROPE)
    q_nope, q_rope = q[..., :MLA_NOPE], apply_rope(q[..., MLA_NOPE:], cos, sin)
    kv = (rmsnorm(c_kv, kv_norm) @ w_ukv).reshape(B, S, MLA_HEADS, MLA_NOPE + MLA_V)
    k_nope, v = kv[..., :MLA_NOPE], kv[..., MLA_NOPE:]
    k_r = apply_rope(k_rope[:, :, None, :], cos, sin)[:, :, 0, :]
    return mla_attention(q_nope, q_rope, k_nope, k_r, v)

def gla_chunked(q, k, v, log_a):
    B, S, H, dk = q.shape
    dv = v.shape[-1]
    C = GLA_CHUNK
    n = S // C
    to_chunks = lambda t: t.astype(jnp.float32).reshape(B, n, C, H, t.shape[-1]).transpose(1, 0, 3, 2, 4)
    qc, kc, vc, gc = to_chunks(q), to_chunks(k), to_chunks(v), to_chunks(log_a)
    tril = jnp.tril(jnp.ones((C, C), dtype=bool))

    def step(state, inp):
        qb, kb, vb, gb = inp
        b = jnp.cumsum(gb, axis=-2)
        inter = jnp.einsum('bhik,bhkv->bhiv', qb * jnp.exp(b), state)
        diff = b[..., :, None, :] - b[..., None, :, :]
        dec = jnp.where(tril[:, :, None], jnp.exp(jnp.where(tril[:, :, None], diff, 0.0)), 0.0)
        A = jnp.einsum('bhik,bhjk,bhijk->bhij', qb, kb, dec)
        intra = jnp.einsum('bhij,bhjv->bhiv', A, vb)
        b_end = b[..., -1:, :]
        new_state = state * jnp.exp(b_end)[..., 0, :, None] + jnp.einsum(
            'bhjk,bhjv->bhkv', kb * jnp.exp(b_end - b), vb)
        return new_state, inter + intra

    state0 = jnp.zeros((B, H, dk, dv), jnp.float32)
    _, out = lax.scan(step, state0, (qc, kc, vc, gc))
    return out.transpose(1, 0, 3, 2, 4).reshape(B, S, H, dv).astype(v.dtype)

def gla_branch(q, k, v, gate_lr, g, w_gate, b_gate, out_norm):
    B, S, _ = q.shape
    qh = q.reshape(B, S, GLA_HEADS, GLA_DK) * (GLA_DK ** -0.5)
    kh = k.reshape(B, S, GLA_HEADS, GLA_DK)
    vh = v.reshape(B, S, GLA_HEADS, GLA_DV)
    gk = (gate_lr @ w_gate + b_gate).astype(jnp.float32)
    log_a = (jax.nn.log_sigmoid(gk) / GLA_GATE_NORM).reshape(B, S, GLA_HEADS, GLA_DK)
    o = gla_chunked(qh, kh, vh, log_a)
    o = head_rmsnorm(o, out_norm).reshape(B, S, GLA_HEADS * GLA_DV)
    return o * jax.nn.silu(g)

def retention_chunked(q, k, v):
    B, S, H, dk = q.shape
    dv = v.shape[-1]
    C = RET_CHUNK
    n = S // C
    to_chunks = lambda t: t.astype(jnp.float32).reshape(B, n, C, H, t.shape[-1]).transpose(0, 3, 1, 2, 4)
    qc, kc, vc = to_chunks(q), to_chunks(k), to_chunks(v)
    log_g = jnp.log(1.0 - 2.0 ** (-5.0 - jnp.arange(H, dtype=jnp.float32)))
    idx = jnp.arange(C, dtype=jnp.float32)
    diff = idx[:, None] - idx[None, :]
    D = jnp.where(diff >= 0, jnp.exp(log_g[:, None, None] * jnp.maximum(diff, 0.0)), 0.0)
    scores = jnp.einsum('bhnid,bhnjd->bhnij', qc, kc) * D[None, :, None]
    intra = jnp.einsum('bhnij,bhnjv->bhniv', scores, vc)
    k_dec = kc * jnp.exp(log_g[:, None] * (C - 1 - idx)[None, :])[None, :, None, :, None]
    U = jnp.einsum('bhnjd,bhnjv->nbhdv', k_dec, vc)
    chunk_decay = jnp.exp(log_g * C)[None, :, None, None]

    def step(R, u):
        return R * chunk_decay + u, R

    _, R_prev = lax.scan(step, jnp.zeros((B, H, dk, dv), jnp.float32), U)
    q_dec = qc * jnp.exp(log_g[:, None] * (idx + 1.0)[None, :])[None, :, None, :, None]
    inter = jnp.einsum('bhnid,nbhdv->bhniv', q_dec, R_prev)
    out = (intra + inter).transpose(0, 2, 3, 1, 4).reshape(B, S, H, dv)
    return out.astype(v.dtype)

def retention_branch(q, k, v, g, out_norm, cos, sin):
    B, S, _ = q.shape
    qh = apply_rope(q.reshape(B, S, RET_HEADS, RET_DK), cos, sin)
    kh = apply_rope(k.reshape(B, S, RET_HEADS, RET_DK), cos, sin) * (RET_DK ** -0.5)
    vh = v.reshape(B, S, RET_HEADS, RET_DV)
    o = retention_chunked(qh, kh, vh)
    o = head_rmsnorm(o, out_norm).reshape(B, S, RET_HEADS * RET_DV)
    return o * jax.nn.silu(g)

def causal_dwconv(a, w, b):
    S = a.shape[1]
    p = jnp.pad(a, ((0, 0), (CONV_W - 1, 0), (0, 0)))
    out = b
    for kk in range(CONV_W):
        out = out + p[:, kk:kk + S] * w[kk]
    return out

def second_inputs(seed: int = 0) -> dict:
    key = jax.random.key(seed)
    ks = jax.random.split(key, 19)
    f32 = jnp.float32
    nrm = lambda k, shape, scale: jax.random.normal(k, shape, f32) * scale
    gain = lambda k, shape: 1.0 + 0.02 * jax.random.normal(k, shape, f32)
    return {
        "x": nrm(ks[0], (BATCH, SEQ, D_MODEL), 1.0),
        "attn_norm": gain(ks[1], (DEPTH, D_MODEL)),
        "w_in": nrm(ks[2], (DEPTH, D_MODEL, D_IN), D_MODEL ** -0.5),
        "mla_q_norm": gain(ks[3], (DEPTH, MLA_Q_RANK)),
        "mla_w_uq": nrm(ks[4], (DEPTH, MLA_Q_RANK, MLA_HEADS * (MLA_NOPE + MLA_ROPE)), MLA_Q_RANK ** -0.5),
        "mla_kv_norm": gain(ks[5], (DEPTH, MLA_KV_RANK)),
        "mla_w_ukv": nrm(ks[6], (DEPTH, MLA_KV_RANK, MLA_HEADS * (MLA_NOPE + MLA_V)), MLA_KV_RANK ** -0.5),
        "mla_out_norm": gain(ks[7], (DEPTH, MLA_HEADS * MLA_V)),
        "gla_w_gate": nrm(ks[8], (DEPTH, GLA_GATE_RANK, GLA_HEADS * GLA_DK), GLA_GATE_RANK ** -0.5),
        "gla_b_gate": nrm(ks[9], (DEPTH, GLA_HEADS * GLA_DK), 0.02),
        "gla_out_norm": gain(ks[10], (DEPTH, GLA_HEADS * GLA_DV)),
        "ret_out_norm": gain(ks[11], (DEPTH, RET_HEADS * RET_DV)),
        "w_out": nrm(ks[12], (DEPTH, D_MIX, D_MODEL), D_MIX ** -0.5),
        "ffn_norm": gain(ks[13], (DEPTH, D_MODEL)),
        "ffn_w_up": nrm(ks[14], (DEPTH, D_MODEL, 2 * D_FF_2), D_MODEL ** -0.5),
        "ffn_conv_w": nrm(ks[15], (DEPTH, CONV_W, D_FF_2), CONV_W ** -0.5),
        "ffn_conv_b": nrm(ks[16], (DEPTH, D_FF_2), 0.02),
        "ffn_w_down": nrm(ks[17], (DEPTH, D_FF_2, D_MODEL), D_FF_2 ** -0.5),
        "final_norm": gain(ks[18], (D_MODEL,)),
    }

def second_block(x, attn_norm, w_in, mla_q_norm, mla_w_uq, mla_kv_norm, mla_w_ukv, mla_out_norm,
              gla_w_gate, gla_b_gate, gla_out_norm, ret_out_norm, w_out, ffn_norm, ffn_w_up,
              ffn_conv_w, ffn_conv_b, ffn_w_down, final_norm):
    B, S, _ = x.shape
    mla_cos, mla_sin = rope_tables(S, MLA_ROPE, MLA_ROPE_BASE)
    ret_cos, ret_sin = rope_tables(S, RET_DK, RET_ROPE_BASE)
    split_points = []
    acc = 0
    for sz in IN_SIZES[:-1]:
        acc += sz
        split_points.append(acc)

    for l in range(DEPTH):
        h = rmsnorm(x, attn_norm[l])
        z = h @ w_in[l]
        (c_q, c_kv, k_rope, g_q, g_k, g_v, g_lr, g_g, r_q, r_k, r_v, r_g) = jnp.split(z, split_points, axis=-1)
        y_a = mla_branch(c_q, c_kv, k_rope, mla_q_norm[l], mla_w_uq[l], mla_kv_norm[l], mla_w_ukv[l],
                         mla_cos, mla_sin)
        y_a = head_rmsnorm(y_a, mla_out_norm[l]).reshape(B, S, MLA_HEADS * MLA_V)
        y_b = gla_branch(g_q, g_k, g_v, g_lr, g_g, gla_w_gate[l], gla_b_gate[l], gla_out_norm[l])
        y_c = retention_branch(r_q, r_k, r_v, r_g, ret_out_norm[l], ret_cos, ret_sin)
        x = x + jnp.concatenate([y_a, y_b, y_c], axis=-1) @ w_out[l]
        h = rmsnorm(x, ffn_norm[l])
        u = h @ ffn_w_up[l]
        a, bv = u[..., :D_FF_2], u[..., D_FF_2:]
        a = causal_dwconv(a, ffn_conv_w[l], ffn_conv_b[l])
        x = x + (jax.nn.silu(a) * bv) @ ffn_w_down[l]

    return rmsnorm(x, final_norm)


def setup_inputs(seed=0):
    out = dict(first_inputs(seed))
    for name, value in second_inputs(seed + 1).items():
        if name != "x":
            out[name + "_2"] = value
    return out


def reference(
    x, c, positions, ada_w, ada_b, w_in, b_in, sinks, pool_w, pool_scale, w_out, w_gate, w_up,
    w_down, g_pre_mix, g_post_mix, g_pre_ffn, g_post_ffn, attn_norm_2, w_in_2, mla_q_norm_2,
    mla_w_uq_2, mla_kv_norm_2, mla_w_ukv_2, mla_out_norm_2, gla_w_gate_2, gla_b_gate_2,
    gla_out_norm_2, ret_out_norm_2, w_out_2, ffn_norm_2, ffn_w_up_2, ffn_conv_w_2, ffn_conv_b_2,
    ffn_w_down_2, final_norm_2,
):
    x = first_block(
        x, c, positions, ada_w, ada_b, w_in, b_in, sinks, pool_w, pool_scale, w_out, w_gate,
        w_up, w_down, g_pre_mix, g_post_mix, g_pre_ffn, g_post_ffn,
    )
    return second_block(
        x, attn_norm_2, w_in_2, mla_q_norm_2, mla_w_uq_2, mla_kv_norm_2, mla_w_ukv_2,
        mla_out_norm_2, gla_w_gate_2, gla_b_gate_2, gla_out_norm_2, ret_out_norm_2, w_out_2,
        ffn_norm_2, ffn_w_up_2, ffn_conv_w_2, ffn_conv_b_2, ffn_w_down_2, final_norm_2,
    )


_drawn_inputs = setup_inputs


def setup_inputs(seed=0):
    import zlib

    import numpy as np

    out = dict(_drawn_inputs(seed))
    spreads = {}
    factors = {'g_pre_mix': 3.156,
     'g_pre_ffn': 2.994,
     'mla_q_norm_2': 8.0,
     'mla_kv_norm_2': 4.106,
     'mla_out_norm_2': 4.298,
     'gla_b_gate_2': 8.0,
     'gla_out_norm_2': 8.0,
     'ret_out_norm_2': 8.0,
     'ffn_norm_2': 4.291,
     'ffn_conv_b_2': 6.21,
     'final_norm_2': 2.802}
    for name, (base, spread) in spreads.items():
        noise = np.random.default_rng([zlib.crc32(name.encode()), seed]).standard_normal(out[name].shape)
        drawn = base * np.exp(spread * noise) if base else spread * noise
        out[name] = __import__('jax').numpy.asarray(drawn.astype(out[name].dtype))
    for name, factor in factors.items():
        out[name] = (out[name] * factor).astype(out[name].dtype)
    return out
```

```python
from contextlib import ExitStack

import numpy as np

import concourse.bass as bass
from concourse import mybir

F32 = mybir.dt.float32
I32 = mybir.dt.int32
ALU = mybir.AluOpType
ACT = mybir.ActivationFunctionType
AX_X = mybir.AxisListType.X

P = 128
S = 256
D = 1024
KT = D // P
NL = 4
FF = 2816
FT = FF // P
NU = FT // 2
EPS = 1e-6
NEG = -1e30
HEADS = 8
HEAD_DIM = 64
ROT = 16
POOLS = (2, 4, 8, 16)
SLOT = 5632
NSLOT = 4


def const_table():
    parts, at = [], {}

    def put(name, a):
        a = np.asarray(a, np.float32).reshape(P, -1)
        start = sum(b.shape[1] for b in parts)
        at[name] = (start, start + a.shape[1])
        parts.append(a)

    def rot_matrix(period, half):
        r = np.zeros((P, P))
        for m in range(P):
            o = m % period
            if o < half:
                r[m + half, m] = -1.0
            elif o < 2 * half:
                r[m - half, m] = 1.0
        return r

    def rope(dim, base, copies):
        inv = base ** (-(np.arange(0, dim, 2, dtype=np.float32) / dim))
        ang = (np.arange(S, dtype=np.float32)[:, None] * inv[None, :].astype(np.float32)).astype(np.float32)
        c, s = np.cos(ang).T, np.sin(ang).T
        return np.tile(np.concatenate([c, c]), (copies, 1)), np.tile(np.concatenate([s, s]), (copies, 1))

    i = np.arange(P)
    put("ident", np.eye(P))
    put("ones", np.ones((P, P)))
    put("ones64", (i[:, None] // 64 == i[None, :] // 64))
    put("rot16", rot_matrix(HEAD_DIM, ROT // 2))
    put("rot64", rot_matrix(64, 32))
    put("rot32", rot_matrix(32, 16))
    k2 = np.arange(2 * P)
    diff = i[:, None] + P - k2[None, :]
    put("window", np.where((diff >= 0) & (diff < P), 0.0, NEG))
    put("causal2", np.where(diff >= 0, 0.0, NEG))
    t = np.arange(S)
    band = []
    for w in POOLS:
        full = ((t[None, :] - t[:, None] >= 0) & (t[None, :] - t[:, None] < w)) / np.minimum(t + 1.0, w)[None, :] - np.eye(S)
        band += [full[:P, :], full[P:, P:]]
    put("band", np.concatenate(band, 1))
    lower = (t[None, :] >= i[:, None]).astype(float)
    put("glamask", np.concatenate([lower, lower[:, :P]], 1))
    decay = []
    for h in range(4):
        g = np.log(1.0 - 2.0 ** (-5.0 - h))
        d = np.where(t[None, :] >= i[:, None], np.exp(g * np.maximum(t[None, :] - i[:, None], 0)), 0.0)
        decay.append(d)
    put("decay", np.concatenate(decay, 1))
    for name, (c, s) in (("mla", rope(64, 10000.0, 2)), ("ret", rope(32, 10000.0, 4))):
        put(name + "cos", c)
        put(name + "sin", s)
    put("headmask", (i[:, None] // 32 == np.arange(4)[None, :]))
    inv = np.float32(500000.0) ** (-np.arange(0, ROT, 2, dtype=np.float32) / np.float32(ROT))
    freq = np.zeros(P)
    for m in range(P):
        if m % HEAD_DIM < ROT:
            freq[m] = inv[m % HEAD_DIM % (ROT // 2)]
    put("freq", freq)
    put("eps", np.full(P, EPS))
    return np.concatenate(parts, 1), at


VECTORS = []
for _l in range(2):
    VECTORS += [(f"ada_b{_l}", 48), (f"g_pre_mix{_l}", 8), (f"g_post_mix{_l}", 8), (f"g_pre_ffn{_l}", 8),
                (f"g_post_ffn{_l}", 8), (f"b_qk{_l}", 5), (f"pool_scale{_l}", 4)]
for _l in range(2):
    VECTORS += [(f"attn_norm{_l}", 8), (f"q_norm{_l}", 3), (f"kv_norm{_l}", 2), (f"mla_out{_l}", 4),
                (f"gla_b{_l}", 1), (f"gla_out{_l}", 2), (f"ret_out{_l}", 2), (f"ffn_norm{_l}", 8),
                (f"conv_w{_l}", 66), (f"conv_b{_l}", 22)]
VECTORS += [("final", 8), ("c", 8)]
COL, _n = {}, 0
for _name, _t in VECTORS:
    COL[_name] = _n
    _n += _t
NVEC = (_n + P - 1) // P


def unit_list():
    units = []
    for L in range(2):
        ada = [(("ada", L, i), 8, 512) for i in range(12)]
        units += ada[:4] + [(("qk", L), 8, 640), (("vu", L), 8, 640)]
        units += ada[4:6] + [(("poolw", L), 4, 128)] + ada[6:] + [(("wo", L, 0), 8, 512), (("wo", L, 1), 8, 512)]
        units += [(("gu", L, i), 8, 512) for i in range(NU)]
        units += [(("wd", L, i), FT, 256) for i in range(4)]
    for L in range(2, 4):
        units += [(("z0", L), 8, 640), (("z1", L), 8, 640), (("z2", L), 8, 528), (("z3", L), 8, 512),
                  (("uq", L), 3, 768), (("ukv", L), 2, 1024), (("wo", L, 0), 8, 512), (("wo", L, 1), 8, 512)]
        units += [(("gu", L, i), 8, 512) for i in range(NU)]
        units += [(("wd", L, i), FT, 256) for i in range(4)]
    return units


UNITS = unit_list()


def tiled(w):
    rows, cols = w.shape
    return w.reshape(rows // P, P, cols).transpose(1, 0, 2).reshape(P, -1)


def pack_weights(a):
    heads = [h for j in range(4) for h in (j, j + 4)]
    out = []
    for (kind, L, *i), kt, cols in UNITS:
        l = L % 2
        if kind == "ada":
            w = a["ada_w"][l][:, 512 * i[0]:512 * (i[0] + 1)]
        elif kind == "qk":
            q = a["w_in"][l][:, :512].reshape(D, HEADS, HEAD_DIM)[:, heads].reshape(D, 512)
            w = np.concatenate([q, a["w_in"][l][:, 512:640]], 1)
        elif kind == "vu":
            w = a["w_in"][l][:, 640:1280]
        elif kind == "poolw":
            w = a["pool_w"][l].reshape(512, P)
        elif kind == "wo" and L < 2:
            w = a["w_out"][l]
            att = w[:512].reshape(HEADS, HEAD_DIM, D)[heads].reshape(512, D)
            w = np.concatenate([att, w[512:]], 0)[:, 512 * i[0]:512 * (i[0] + 1)]
        elif kind == "wo":
            w = a["w_out_2"][l][:, 512 * i[0]:512 * (i[0] + 1)]
        elif kind == "gu":
            one, two = (a["w_gate"][l], a["w_up"][l]) if L < 2 else (a["ffn_w_up_2"][l][:, :FF], a["ffn_w_up_2"][l][:, FF:])
            c = slice(256 * i[0], 256 * (i[0] + 1))
            w = np.concatenate([one[:, c], two[:, c]], 1)
        elif kind == "wd":
            w = (a["w_down"] if L < 2 else a["ffn_w_down_2"])[l][:, 256 * i[0]:256 * (i[0] + 1)]
        elif kind in ("z0", "z1", "z2", "z3"):
            w = a["w_in_2"][l]
            sizes = (384, 256, 64, 128, 128, 256, 16, 256, 128, 128, 256, 256)
            cq, ckv, kr, gq, gk, gv, glr, gg, rq, rk, rv, rg = np.split(w, np.cumsum(sizes)[:-1], 1)
            w = np.concatenate({"z0": [cq, ckv], "z1": [kr, kr, gq, gk, rq, rk], "z2": [gg, rg, glr],
                                "z3": [gv, rv]}[kind], 1)
        elif kind == "uq":
            w = a["mla_w_uq_2"][l].reshape(384, 4, 192)
            w = np.concatenate([w[:, :, :128].reshape(384, 512), w[:, :, 128:].reshape(384, 256)], 1)
        elif kind == "ukv":
            w = a["mla_w_ukv_2"][l].reshape(256, 4, 256)
            w = np.concatenate([w[:, :, :128].reshape(256, 512), w[:, :, 128:].reshape(256, 512)], 1)
        w = tiled(w)
        assert w.shape == (P, kt * cols), (kind, w.shape)
        out.append(w.ravel())
    return np.concatenate(out)


def pack_vectors(a):
    heads = [h for j in range(4) for h in (j, j + 4)]
    rows = []
    for name, tiles in VECTORS:
        base, l = (name[:-1], int(name[-1])) if name[-1].isdigit() else (name, 0)
        v = {
            "ada_b": lambda: a["ada_b"][l], "b_qk": lambda: np.concatenate(
                [a["b_in"][l][:512].reshape(HEADS, HEAD_DIM)[heads].ravel(), a["b_in"][l][512:640]]),
            "attn_norm": lambda: a["attn_norm_2"][l], "q_norm": lambda: a["mla_q_norm_2"][l],
            "kv_norm": lambda: a["mla_kv_norm_2"][l], "mla_out": lambda: a["mla_out_norm_2"][l],
            "gla_b": lambda: a["gla_b_gate_2"][l], "gla_out": lambda: a["gla_out_norm_2"][l],
            "ret_out": lambda: a["ret_out_norm_2"][l], "ffn_norm": lambda: a["ffn_norm_2"][l],
            "conv_w": lambda: a["ffn_conv_w_2"][l], "conv_b": lambda: a["ffn_conv_b_2"][l],
            "final": lambda: a["final_norm_2"], "c": lambda: a["c"],
        }.get(base, lambda: a[base][l])()
        rows.append(np.asarray(v).reshape(tiles, P))
    rows = np.concatenate(rows)
    rows = np.concatenate([rows, np.zeros((NVEC * P - len(rows), P), rows.dtype)])
    return np.ascontiguousarray(rows.reshape(NVEC, P, P).transpose(1, 0, 2).reshape(P, NVEC * P))


class Counts:

    def __init__(self):
        self.value = {}
        self.freed_by = {}
        self.last_use = {}


def build(nc, counts, a_x, a_pos, a_const, const_at, a_vec, a_w, a_bias, a_sinks, a_gatew, out):
    ctx = ExitStack()
    with ctx:
        def sb(name, shape, dt=F32):
            return ctx.enter_context(nc.sbuf_tensor(name, shape, dt))

        psum = [ctx.enter_context(nc.psum_tensor(f"bank{b}", [P, 512], F32)) for b in range(8)]

        sems, so_far = {}, {}

        def sem(name):
            if name not in sems:
                sems[name] = ctx.enter_context(nc.semaphore(name))
                so_far[name] = 0
            return sems[name]

        def sig(name, *key, frees=None, by=1):
            s = sem(name)
            so_far[name] += by
            counts.value[(name, *key)] = so_far[name]
            if frees is not None:
                counts.freed_by[frees] = (name, *key)
            return s, by

        def due(name, *key):
            return sem(name), counts.value.get((name, *key), 1)

        ring = sb("ring", [P, NSLOT, SLOT])
        const = sb("const", [P, a_const.shape[1]])
        vcol = sb("vcol", [P, NVEC * P])
        x = sb("x", [P, KT, S])
        h = sb("h", [P, KT, S])
        cat = sb("cat", [P, KT, S])
        o_sb = cat
        act = sb("act", [P, FT, S])
        silu = sb("silu", [P, 2, S])
        shared = sb("shared", [P, 1536])
        bias_vu = shared[:, 0:1280].rearrange("p (l n) -> p l n", l=2)
        gates = shared[:, 0:1024].rearrange("p (t s) -> p t s", t=4)
        conv = shared[:, 1024:1536].rearrange("p (b s) -> p b s", b=2)
        rstd = sb("rstd", [P, 2, 512])
        c_act = sb("c_act", [P, KT])
        mods = sb("mods", [P, 48])
        gains = sb("gains", [P, 4, KT])
        start = act[:, :, :].rearrange("p t s -> p (t s)")
        vrow = start[:, 0:NVEC * P]
        pos_i = start[:, 1024:1280].bitcast(I32)
        ang = start[:, 1280:1536]
        turns = start[:, 1536:2048].rearrange("p (i s) -> p i s", i=2)
        rope1 = sb("rope1", [P, 2, S])
        sinks = sb("sinks", [P, 2, HEADS])
        gatew = sb("gatew", [16, 2, P])
        tmp = sb("tmp", [P, 512])
        work = sb("work", [P, 7936])
        at = [0]

        def part(n, *shape):
            v = work[:, at[0]:at[0] + n]
            at[0] += n
            return v

        qk = part(1280).rearrange("p (t s) -> p t s", t=5)
        tok = part(1280).rearrange("p (b n) -> p b n", b=2)
        prob = part(2 * 516).rearrange("p (b n) -> p b n", b=2)
        probT = part(6 * 512).rearrange("p (b n) -> p b n", b=6)
        pooled = part(1024).rearrange("p (g s) -> p g s", g=4)
        first_end = at[0]
        at[0] = 0
        cqkv = part(1280).rearrange("p (t s) -> p t s", t=5)
        cnorm = part(1280).rearrange("p (t s) -> p t s", t=5)
        prob2 = work[:, 1280:2304].rearrange("p (b n) -> p b n", b=2)
        probT2 = part(3 * 512).rearrange("p (b n) -> p b n", b=3)
        qh = part(1792).rearrange("p (t s) -> p t s", t=7)
        kn = work[:, 0:1024].rearrange("p (t s) -> p t s", t=4)
        vm = part(1024).rearrange("p (b n) -> p b n", b=2)
        vgr = part(1024).rearrange("p (b n) -> p b n", b=2)
        assert max(first_end, at[0]) <= 7936, (first_end, at[0])
        gr = act[:, :, :].rearrange("p t s -> p (t s)")
        gq, gk, rq, rk = (gr[:, 256 * n:256 * (n + 1)] for n in range(4))
        lsum = gr[:, 1024:1280]
        expq = gr[:, 1280:2304].rearrange("p (j s) -> p j s", j=4)
        kbd = gr[:, 2304:3328].rearrange("p (h s) -> p h s", h=4)
        attT = gr[:, 3328:4864].rearrange("p (h n) -> p h n", h=4)
        expk = gr[:, 4864:5120]
        glr = gr[0:16, 5120:5376]
        mid = gr[:, 5376:5384]
        kr2 = silu
        smax = sb("smax", [P, 2, 4])
        ssum = sb("ssum", [P, 2, 4])

        def k(name, a=0, b=None):
            lo, hi = const_at[name]
            return const[:, lo + a:(hi if b is None else lo + b)]

        def v(name, i=0, n=1):
            return vcol[:, COL[name] + i:COL[name] + i + n]

        def bcast(ap, n):
            return ap.rearrange("p (o s) -> p o s", o=1).to_broadcast([ap.shape[0], n, ap.shape[1]])

        unit_no = {u[0]: n for n, u in enumerate(UNITS)}

        block = ctx.enter_context(nc.Block())

        bank_of, occupant = {}, [None] * 8

        def ps(job):
            return psum[bank_of[job]]

        @block.tensor
        def _(pe):
            n_jobs = [0]

            def take(job):
                b = n_jobs[0] % 8
                n_jobs[0] += 1
                if occupant[b] is not None and occupant[b] in counts.freed_by:
                    pe.wait_ge(*due(*counts.freed_by[occupant[b]]))
                occupant[b] = job
                bank_of[job] = b
                return psum[b]

            def weights(unit, job):
                n = unit_no[unit]
                pe.wait_ge(*due(f"slot{n % NSLOT}", unit))
                counts.last_use[unit] = job
                _, kt, cols = UNITS[n]
                return ring[:, n % NSLOT, 0:kt * cols].rearrange("p (t c) -> p t c", t=kt)

            def group(o, pairs):
                for i, (w, r) in enumerate(pairs):
                    last = nc.tensor.matmul(o, w, r, start=(i == 0), stop=(i == len(pairs) - 1))
                return last

            def half(bank, i):
                return bank[:, 256 * i:256 * (i + 1)]

            def sums(N, tiles, ones, src, wait):
                job = ("sums", *N)
                b = take(job)
                for i, t in enumerate(tiles):
                    wait(t)
                    last = nc.tensor.matmul(b[:, 0:256], ones, src[:, t, :], start=(i == 0), stop=(i == len(tiles) - 1))
                last.then_inc(*sig(*job))

            def norm_sums(N):
                sums(N, range(KT), k("ones"), h, lambda t: pe.wait_ge(*due("squared", N, t // 2)) if t % 2 == 0 else None)

            def pair_job(job, unit, c0, src, wait=None, kts=KT, n=2):
                w = weights(unit, job)
                b = take(job)
                for i in range(n):
                    for t in range(kts):
                        if i == 0 and wait is not None:
                            wait(t)
                        last = nc.tensor.matmul(half(b, i), w[:, t, c0 + P * i:c0 + P * (i + 1)], src[:, t, :],
                                                start=(t == 0), stop=(t == kts - 1))
                last.then_inc(*sig(*job))

            def ada(L, part_, comps):
                b = take(("ada", L, part_))
                for comp in comps:
                    for u in (2 * comp, 2 * comp + 1):
                        w = weights(("ada", L, u), ("ada_unit", L, u))
                        for f in range(4):
                            col = 4 * u + f
                            last = group(b[:, col:col + 1], [(w[:, t, P * f:P * (f + 1)], c_act[:, t:t + 1]) for t in range(KT)])
                        last.then_inc(*sig("ada_unit", L, u))

            def transposes(job, srcs):
                b = take(job)
                for i, s_ in enumerate(srcs):
                    last = nc.tensor.transpose(b[:, P * i:P * (i + 1)], s_, k("ident"))
                last.then_inc(*sig(*job))

            pe.wait_ge(*due("const_in", 0))
            pe.wait_ge(*due("vec_in", 0))
            transposes(("vec",), [vrow[:, P * g:P * (g + 1)] for g in range(NVEC)])
            pe.wait_ge(*due("c_act", 0))

            for L in range(NL):
                h_wait = lambda t: pe.wait_ge(*due("h", ("mix", L), t))
                if L < 2:
                    ada(L, 0, (0, 1))
                    norm_sums(("mix", L))
                    for i in range(3):
                        pair_job(("qk", L, i), ("qk", L), 256 * i, h, h_wait if i == 0 else None, n=2 if i < 2 else 1)
                    job = ("val", L)
                    w = weights(("vu", L), job)
                    b = take(job)
                    for tb in range(2):
                        last = group(b[:, P * tb:P * (tb + 1)], [(h[:, t, P * tb:P * (tb + 1)], w[:, t, 0:128]) for t in range(KT)])
                    last.then_inc(*sig(*job))
                    for tb in range(2):
                        job = ("stream", L, tb)
                        weights(("vu", L), job)
                        b = take(job)
                        group(b[:, :], [(h[:, t, P * tb:P * (tb + 1)], w[:, t, 128:640]) for t in range(KT)]).then_inc(*sig(*job))
                    for i in range(3):
                        pe.wait_ge(*due("qk_raw", L, i))
                        n = 512 if i < 2 else 256
                        b = take(("qk_rot", L, i))
                        nc.tensor.matmul(b[:, 0:n], k("rot16"), qk[:, 2 * i:2 * i + n // 256, :], start=True, stop=True).then_inc(*sig("qk_rot", L, i))
                    for i in range(2):
                        pe.wait_ge(*due("tok", L, 2))
                        job = ("pool", L, i)
                        b = take(job)
                        for g in range(2):
                            gi = 2 * i + g
                            o = half(b, g)
                            nc.tensor.matmul(o, tok[:, 0, 128 + P * gi:256 + P * gi], k("band", 384 * gi, 384 * gi + 256), start=True, stop=False)
                            last = nc.tensor.matmul(o[:, P:2 * P], tok[:, 1, 128 + P * gi:256 + P * gi], k("band", 384 * gi + 256, 384 * gi + 384), start=False, stop=True)
                        last.then_inc(*sig(*job))
                    ada(L, 1, (2,))
                    w = weights(("poolw", L), ("poolw", L, 1))
                    for i in range(2):
                        job = ("poolw", L, i)
                        pe.wait_ge(*due("pooled", L, i))
                        b = take(job)
                        for g in range(2):
                            last = group(half(b, g), [(w[:, 2 * i + g, :], pooled[:, 2 * i + g, :])])
                        last.then_inc(*sig(*job))
                    pe.wait_ge(*due("qk_done", L, 2))
                    for g in range(2):
                        rows = slice(64 * g, 64 * g + 64)
                        for jp in range(2):
                            pe.wait_ge(*due("qk_done", L, jp))
                            job = ("score", L, 2 * g + jp)
                            b = take(job)
                            for j in range(2):
                                last = group(half(b, j), [(qk[rows, 2 * jp + j, P:2 * P], qk[rows, 4, :])])
                            last.then_inc(*sig(*job))
                    for g in range(2):
                        rows = slice(64 * g, 64 * g + 64)
                        job = ("score", L, 4 + g)
                        b = take(job)
                        for j in range(4):
                            last = group(b[:, P * j:P * (j + 1)], [(qk[rows, j, 0:P], qk[rows, 4, 0:P])])
                        last.then_inc(*sig(*job))
                    for n in range(6):
                        pe.wait_ge(*due("prob", L, n))
                        p_ = prob[:, n % 2, :]
                        cut = (lambda i: p_[:, 257 * (i // 2) + P * (i % 2):][:, 0:P]) if n < 4 else (lambda i: p_[:, 128 * i + i:][:, 0:P])
                        transposes(("probT", L, n), [cut(i) for i in range(4)])
                    for jp in range(2):
                        job = ("attn", L, jp)
                        b = take(job)
                        for n in (jp, 2 + jp, 4, 5):
                            pe.wait_ge(*due("probT_in", L, n))
                        for j in range(2):
                            for g in range(2):
                                val = lambda kb: tok[:, kb, 64 * g:64 * g + 64]
                                o = b[64 * g:64 * g + 64, 256 * j:256 * (j + 1)]
                                t1 = probT[:, 2 * g + jp, 256 * j:256 * (j + 1)]
                                t0 = probT[:, 4 + g, P * (2 * jp + j):P * (2 * jp + j + 1)]
                                group(o[:, 0:P], [(val(0), t0)])
                                last = group(o[:, P:2 * P], [(val(0), t1[:, 0:P]), (val(1), t1[:, P:2 * P])])
                        last.then_inc(*sig(*job))
                    ada(L, 2, (3, 4, 5))
                    cat_wait = lambda t: pe.wait_ge(*(due("cat", L, t // 2) if t < 4 else due("cat_pool", L, t // 2 - 2)))
                else:
                    norm_sums(("mix", L))
                    pair_job(("z0", L, 0), ("z0", L), 0, h, h_wait)
                    pair_job(("z0", L, 1), ("z0", L), 256, h)
                    pair_job(("z0", L, 2), ("z0", L), 512, h, n=1)
                    pair_job(("z1", L, 0), ("z1", L), 0, h, n=1)
                    pair_job(("z1", L, 1), ("z1", L), 128, h)
                    pair_job(("z1", L, 2), ("z1", L), 384, h)
                    for n, tiles in enumerate(((0, 1, 2), (3, 4))):
                        sums(("c", L, n), tiles, k("ones"), o_sb, lambda t: pe.wait_ge(*due("csq", L, t // 2)))
                    job = ("glr", L)
                    w = weights(("z2", L), job)
                    b = take(job)
                    group(b[0:16, 0:256], [(w[:, t, 512:528], h[:, t, :]) for t in range(KT)]).then_inc(*sig(*job))
                    pair_job(("z2", L, 0), ("z2", L), 0, h)
                    pair_job(("z2", L, 1), ("z2", L), 256, h)
                    for tb in range(2):
                        job = ("vgr", L, tb)
                        w = weights(("z3", L), job)
                        b = take(job)
                        group(b[:, :], [(h[:, t, P * tb:P * (tb + 1)], w[:, t, :]) for t in range(KT)]).then_inc(*sig(*job))
                    pe.wait_ge(*due("gatew_in", 0))
                    pe.wait_ge(*due("glr_in", L))
                    b = take(("ggate", L))
                    nc.tensor.matmul(b[:, 0:256], gatew[:, L - 2, :], glr, start=True, stop=True).then_inc(*sig("ggate", L))
                    pe.wait_ge(*due("kr_raw", L))
                    b = take(("kr_rot", L))
                    nc.tensor.matmul(b[:, 0:256], k("rot64"), qh[:, 6, :], start=True, stop=True).then_inc(*sig("kr_rot", L))
                    pe.wait_ge(*due("rqk_raw", L))
                    b = take(("rqk_rot", L))
                    nc.tensor.matmul(b[:, :], k("rot32"), gr[:, 512:1024], start=True, stop=True).then_inc(*sig("rqk_rot", L))
                    cw = lambda t: pe.wait_ge(*due("cnorm", L, t))
                    pair_job(("qr", L), ("uq", L), 512, cnorm, cw, kts=3)
                    pair_job(("qn", L, 0), ("uq", L), 0, cnorm, kts=3)
                    pair_job(("qn", L, 1), ("uq", L), 256, cnorm, kts=3)
                    cw = lambda t: pe.wait_ge(*due("cnorm", L, 3 + t))
                    pair_job(("kn", L, 0), ("ukv", L), 0, cnorm[:, 3:5, :], cw, kts=2)
                    pair_job(("kn", L, 1), ("ukv", L), 256, cnorm[:, 3:5, :], kts=2)
                    for tb in range(2):
                        job = ("vm", L, tb)
                        w = weights(("ukv", L), job)
                        b = take(job)
                        group(b[:, :], [(cnorm[:, 3 + t, P * tb:P * (tb + 1)], w[:, t, 512:1024]) for t in range(2)]).then_inc(*sig(*job))
                    pe.wait_ge(*due("qr_raw", L))
                    b = take(("qr_rot", L))
                    nc.tensor.matmul(b[:, :], k("rot64"), qh[:, 4:6, :], start=True, stop=True).then_inc(*sig("qr_rot", L))
                    pe.wait_ge(*due("rkbd", L))
                    for hd in range(4):
                        job = ("rscore", L, hd)
                        b = take(job)
                        group(b[:, 0:256], [(kbd[:, hd, 0:P], rq)])
                        group(b[:, 256:384], [(kbd[:, hd, P:2 * P], rq[:, P:2 * P])]).then_inc(*sig(*job))
                    pe.wait_ge(*due("kn_in", L, 1))
                    pe.wait_ge(*due("qn_in", L, 1))
                    pe.wait_ge(*due("qr_in", L))
                    pe.wait_ge(*due("kr2", L))
                    for n in range(3):
                        job = ("score", L, n)
                        b = take(job)
                        for i in range(2 if n < 2 else 4):
                            hd = 2 * n + i if n < 2 else i
                            qs, ks, o = (slice(P, 2 * P), slice(0, 256), half(b, i)) if n < 2 else (slice(0, P), slice(0, P), b[:, P * i:P * (i + 1)])
                            last = group(o, [(qh[:, hd, qs], kn[:, hd, ks]), (qh[:, 4 + hd // 2, qs], kr2[:, hd % 2, ks])])
                        last.then_inc(*sig(*job))
                    pe.wait_ge(*due("vgr_in", L, 1))
                    job = ("rout", L)
                    b = take(job)
                    for hd in range(4):
                        pe.wait_ge(*due("ratt", L, hd))
                        o = b[64 * (hd % 2):64 * (hd % 2) + 64, 256 * (hd // 2):256 * (hd // 2) + 256]
                        val = lambda jb: vgr[:, jb, 256 + 64 * hd:256 + 64 * hd + 64]
                        nc.tensor.matmul(o, val(0), attT[:, hd, 0:256], start=True, stop=False)
                        last = nc.tensor.matmul(o[:, P:2 * P], val(1), attT[:, hd, 256:384], start=False, stop=True)
                    last.then_inc(*sig(*job))
                    pe.wait_ge(*due("gkbd", L))
                    for hd in range(4):
                        job = ("gscore", L, hd)
                        b = take(job)
                        for J in range(4):
                            o = b[64 * (J % 2):64 * (J % 2) + 64, 0:256] if J < 2 else b[64 * (J % 2):64 * (J % 2) + 64, 256:384]
                            last = group(o, [(kbd[:, hd, 64 * J:64 * J + 64], expq[:, J, P * (J // 2):])])
                        last.then_inc(*sig(*job))
                    for n in range(3):
                        pe.wait_ge(*due("prob", L, n))
                        transposes(("probT", L, n), [prob2[:, n % 2, P * i:P * (i + 1)] for i in range(4)])
                    job = ("gout", L)
                    b = take(job)
                    for hd in range(4):
                        pe.wait_ge(*due("gatt", L, hd))
                        o = b[64 * (hd % 2):64 * (hd % 2) + 64, 256 * (hd // 2):256 * (hd // 2) + 256]
                        val = lambda jb: vgr[:, jb, 64 * hd:64 * hd + 64]
                        nc.tensor.matmul(o, val(0), attT[:, hd, 0:256], start=True, stop=False)
                        last = nc.tensor.matmul(o[:, P:2 * P], val(1), attT[:, hd, 256:384], start=False, stop=True)
                    last.then_inc(*sig(*job))
                    pe.wait_ge(*due("vm_in", L, 1))
                    for n in range(2):
                        job = ("attn", L, n)
                        b = take(job)
                        for m in (n, 2):
                            pe.wait_ge(*due("probT_in", L, m))
                        for i in range(2):
                            hd = 2 * n + i
                            val = lambda kb: vm[:, kb, P * hd:P * (hd + 1)]
                            t1 = probT2[:, n, 256 * i:256 * (i + 1)]
                            t0 = probT2[:, 2, P * hd:P * (hd + 1)]
                            group(half(b, i)[:, 0:P], [(val(0), t0)])
                            last = group(half(b, i)[:, P:2 * P], [(val(0), t1[:, 0:P]), (val(1), t1[:, P:2 * P])])
                        last.then_inc(*sig(*job))
                    for n, ones in ((3, "ones64"), (2, "ones64"), (0, "ones"), (1, "ones")):
                        pe.wait_ge(*due("hsq", L, n))
                        b = take(("hsum", L, n))
                        nc.tensor.matmul(b[:, :], k(ones), h[:, 2 * n:2 * n + 2, :], start=True, stop=True).then_inc(*sig("hsum", L, n))
                    cat_wait = lambda t: pe.wait_ge(*due("cat", L, t // 2))
                for p_ in range(4):
                    pair_job(("y", L, 0, p_), ("wo", L, p_ // 2), 256 * (p_ % 2), cat, cat_wait if p_ == 0 else None)
                if L < 2:
                    norm_sums(("post_mix", L))
                norm_sums(("ffn", L))
                for f in range(FT):
                    job = ("gu", L, f)
                    unit = ("gu", L, f // 2)
                    w = weights(unit, job)
                    b = take(job)
                    for i in range(2):
                        for t in range(KT):
                            if f == 0 and i == 0:
                                pe.wait_ge(*due("h", ("ffn", L), t))
                            last = nc.tensor.matmul(half(b, i), w[:, t, 256 * i + P * (f % 2):256 * i + P * (f % 2) + P], h[:, t, :],
                                                    start=(t == 0), stop=(t == KT - 1))
                    last.then_inc(*sig(*job))
                for p_ in range(4):
                    pair_job(("y", L, 1, p_), ("wd", L, p_), 0, act, (lambda t: pe.wait_ge(*due("act", L, t))) if p_ == 0 else None, kts=FT)
                if L < 2:
                    norm_sums(("post_ffn", L))
            norm_sums(("final", 0))

        @block.sync
        def _(sp):
            off = 0
            occupied = {}
            for n, (unit, kt, cols) in enumerate(UNITS):
                slot = n % NSLOT
                if slot in occupied:
                    sp.wait_ge(*due(*counts.last_use[occupied[slot]]))
                occupied[slot] = unit
                width = kt * cols
                sp.dma_start(ring[:, slot, 0:width], a_w[off:off + P * width].rearrange("(p w) -> p w", w=width)).then_inc(
                    *sig(f"slot{slot}", unit, by=16))
                off += P * width
            sp.wait_ge(*due("out_ready", 3))
            sp.dma_start(out, h[:, :, :]).then_inc(*sig("stored", 0, by=16))
            sp.wait_ge(*due("stored", 0))

        @block.gpsimd
        def _(pool):
            pool.dma_start(bias_vu[:, :, :], a_bias.rearrange("(o l) n -> o l n", o=1).to_broadcast([P, 2, 640])).then_inc(*sig("bias_in", 0, by=16))
            pool.dma_start(sinks[:, :, :], a_sinks.rearrange("(o l) n -> o l n", o=1).to_broadcast([P, 2, HEADS])).then_inc(*sig("sinks_in", 0, by=16))
            pool.dma_start(gatew[:, :, :], a_gatew.rearrange("l g n -> g l n")).then_inc(*sig("gatew_in", 0, by=16))

        @block.scalar
        def _(sc):
            sc.dma_start(vrow[:, :], a_vec).then_inc(*sig("vec_in", 0, by=16))
            sc.dma_start(const[:, :], a_const).then_inc(*sig("const_in", 0, by=16))
            sc.dma_start(x[:, :, :], a_x).then_inc(*sig("x_in", 0, by=16))
            sc.dma_start(pos_i[:, :], a_pos.to_broadcast([P, S])).then_inc(*sig("pos_in", 0, by=16))
            sc.preload_act_table_set("trig_and_small")
            sc.wait_ge(*due("turns", 1))
            nc.scalar.activation(rope1[:, :, :], turns[:, :, :], ACT.Sin).then_inc(*sig("rope1", 0))
            sc.wait_ge(*due("vcol", 0))
            nc.scalar.activation(c_act[:, :], v("c", 0, 8), ACT.Silu).then_inc(*sig("c_act", 0))
            n_rstd = [0]

            def square(N, p_, src_due):
                sc.wait_ge(*src_due)
                if N[0] in ("post_mix", "post_ffn"):
                    src = ps(("y", N[1], 0 if N[0] == "post_mix" else 1, p_))[:, :]
                    dst = h[:, 2 * p_:2 * p_ + 2, :].rearrange("p t s -> p (t s)")
                else:
                    src, dst = x[:, 2 * p_:2 * p_ + 2, :], h[:, 2 * p_:2 * p_ + 2, :]
                nc.scalar.activation(dst, src, ACT.Square).then_inc(*sig("squared", N, p_))

            def root(job, name, key, scale, width, dst):
                sc.wait_ge(*due(*job))
                nc.scalar.activation(dst, ps(job)[:, 0:width], ACT.Ln, bias=k("eps"), scale=scale).then_inc(*sig("mean_log", job, frees=job))
                sc.wait_ge(*due("mean_log", job))
                nc.scalar.activation(dst, dst, ACT.Exp, scale=-0.5).then_inc(*sig(name, *key))

            def norm(N, src_due):
                for p_ in range(4):
                    square(N, p_, src_due(p_))
                root(("sums", *N), "rstd", (N,), 1.0 / D, 256, rstd[:, 0, 0:256])

            def shift(N, col0):
                for t in range(KT):
                    sc.wait_ge(*due("scaled", N, t))
                    nc.scalar.activation(h[:, t, :], h[:, t, :], ACT.Identity, bias=mods[:, col0 + t:col0 + t + 1]).then_inc(*sig("h", N, t))

            def copy(job, dst, src, name, *key, **kw):
                sc.wait_ge(*due(*job))
                return nc.scalar.activation(dst, src, ACT.Identity, **kw).then_inc(*sig(name, *key, frees=job))

            sc.preload_act_table_set("natural_log_exp_and_others")
            for L in range(NL):
                l = L % 2
                norm(("mix", L), (lambda p_: due("x_in", 0)) if L == 0 else (lambda p_: due("x", L - 1, 1, p_)))
                if L < 2:
                    shift(("mix", L), 0)
                    for i in range(3):
                        for j in range(2 if i < 2 else 1):
                            sc.wait_ge(*due("qk", L, i))
                            last = nc.scalar.activation(qk[:, 2 * i + j, :], ps(("qk", L, i))[:, 256 * j:256 * (j + 1)], ACT.Identity,
                                                        bias=v(f"b_qk{l}", 2 * i + j))
                        last.then_inc(*sig("qk_raw", L, i, frees=("qk", L, i)))
                    for i in range(2):
                        copy(("pool", L, i), pooled[:, 2 * i:2 * i + 2, :].rearrange("p t s -> p (t s)"), ps(("pool", L, i))[:, :], "pooled", L, i)
                    for n in range(6):
                        nh = 2 if n < 4 else 4
                        w = 257 if n < 4 else 129
                        sc.wait_ge(*due("smax", L, n))
                        for i in range(nh):
                            last = nc.scalar.activation(prob[:, n % 2, w * i:w * i + w - 0], prob[:, n % 2, w * i:w * i + w], ACT.Exp,
                                                        bias=smax[:, n % 2, i:i + 1], accum_out=ssum[:, n % 2, i:i + 1])
                        last.then_inc(*sig("exp", L, n))
                        if n >= 1:
                            copy(("probT", L, n - 1), probT[:, n - 1, :], ps(("probT", L, n - 1))[:, :], "probT_in", L, n - 1)
                    copy(("probT", L, 5), probT[:, 5, :], ps(("probT", L, 5))[:, :], "probT_in", L, 5)
                    for jp in range(2):
                        copy(("attn", L, jp), cat[:, 2 * jp:2 * jp + 2, :].rearrange("p t s -> p (t s)"), ps(("attn", L, jp))[:, :], "cat", L, jp)
                else:
                    for i in range(3):
                        n = 2 if i < 2 else 1
                        copy(("z0", L, i), cqkv[:, 2 * i:2 * i + n, :].rearrange("p t s -> p (t s)"), ps(("z0", L, i))[:, 0:256 * n], "c_raw", L, i)
                    copy(("z1", L, 0), qh[:, 6, :], ps(("z1", L, 0))[:, 0:256], "kr_raw", L)
                    sc.wait_ge(*due("z1", L, 1))
                    nc.scalar.activation(gq, ps(("z1", L, 1))[:, 0:256], ACT.Identity, scale=32.0 ** -0.5)
                    nc.scalar.activation(gk, ps(("z1", L, 1))[:, 256:512], ACT.Identity).then_inc(*sig("gqk_raw", L, frees=("z1", L, 1)))
                    copy(("z1", L, 2), gr[:, 512:1024], ps(("z1", L, 2))[:, :], "rqk_raw", L)
                    root(("sums", "c", L, 0), "c_rstd", (L, 0), 1.0 / 384, 256, rstd[:, 1, 0:256])
                    root(("sums", "c", L, 1), "c_rstd", (L, 1), 1.0 / 256, 256, rstd[:, 1, 256:512])
                    copy(("glr", L), glr, ps(("glr", L))[0:16, 0:256], "glr_in", L)
                    for i in range(2):
                        sc.wait_ge(*due("z2", L, i))
                        nc.scalar.activation(gates[:, 2 * i:2 * i + 2, :].rearrange("p t s -> p (t s)"), ps(("z2", L, i))[:, :], ACT.Silu).then_inc(
                            *sig("gates", L, i, frees=("z2", L, i)))
                    sc.preload_act_table_set("natural_log_exp_and_others")
                    for tb in range(2):
                        copy(("vgr", L, tb), vgr[:, tb, :], ps(("vgr", L, tb))[:, :], "vgr_in", L, tb)
                    sc.wait_ge(*due("ggate_in", L))
                    nc.scalar.activation(expk, lsum, ACT.Abs).then_inc(*sig("lsig", L, 0))
                    sc.wait_ge(*due("lsig", L, 0))
                    nc.scalar.activation(expk, expk, ACT.Exp, scale=-1.0).then_inc(*sig("lsig", L, 1))
                    sc.wait_ge(*due("lsig", L, 1))
                    nc.scalar.activation(expk, expk, ACT.Ln, bias=1.0).then_inc(*sig("lsig", L, 2))
                    copy(("qr", L), qh[:, 4:6, :].rearrange("p t s -> p (t s)"), ps(("qr", L))[:, :], "qr_raw", L)
                    for i in range(2):
                        copy(("qn", L, i), qh[:, 2 * i:2 * i + 2, :].rearrange("p t s -> p (t s)"), ps(("qn", L, i))[:, :], "qn_in", L, i)
                    for i in range(2):
                        copy(("kn", L, i), kn[:, 2 * i:2 * i + 2, :].rearrange("p t s -> p (t s)"), ps(("kn", L, i))[:, :], "kn_in", L, i)
                    for tb in range(2):
                        copy(("vm", L, tb), vm[:, tb, :], ps(("vm", L, tb))[:, :], "vm_in", L, tb)
                    sc.wait_ge(*due("gmid", L))
                    for J in range(4):
                        nc.scalar.activation(expq[:, J, 64 * J:256], lsum[:, 64 * J:256], ACT.Exp, bias=mid[:, 4 + J:5 + J], scale=1.0 / 16)
                        last = nc.scalar.activation(expk[:, 64 * J:64 * J + 64], lsum[:, 64 * J:64 * J + 64], ACT.Exp, bias=mid[:, J:J + 1], scale=-1.0 / 16)
                    last.then_inc(*sig("gexp", L))
                    for n in range(3):
                        nh, w = (2, 256) if n < 2 else (4, 128)
                        sc.wait_ge(*due("smax", L, n))
                        for i in range(nh):
                            last = nc.scalar.activation(prob2[:, n % 2, w * i:w * (i + 1)], prob2[:, n % 2, w * i:w * (i + 1)], ACT.Exp,
                                                        bias=smax[:, n % 2, i:i + 1], accum_out=ssum[:, n % 2, i:i + 1])
                        last.then_inc(*sig("exp", L, n))
                        if n == 2:
                            copy(("probT", L, 0), probT2[:, 0, :], ps(("probT", L, 0))[:, :], "probT_in", L, 0)
                    copy(("rout", L), o_sb[:, 6:8, :].rearrange("p t s -> p (t s)"), ps(("rout", L))[:, :], "o_in", L, 3)
                    for n in range(1, 3):
                        copy(("probT", L, n), probT2[:, n, :], ps(("probT", L, n))[:, :], "probT_in", L, n)
                    copy(("gout", L), o_sb[:, 4:6, :].rearrange("p t s -> p (t s)"), ps(("gout", L))[:, :], "o_in", L, 2)
                    for n in range(2):
                        copy(("attn", L, n), o_sb[:, 2 * n:2 * n + 2, :].rearrange("p t s -> p (t s)"), ps(("attn", L, n))[:, :], "o_in", L, n)
                    for n in (3, 2, 0, 1):
                        sc.wait_ge(*due("o_in", L, n))
                        nc.scalar.activation(h[:, 2 * n:2 * n + 2, :], o_sb[:, 2 * n:2 * n + 2, :], ACT.Square).then_inc(*sig("hsq", L, n))
                    for m, n in enumerate((3, 2, 0, 1)):
                        if m >= 2:
                            sc.wait_ge(*due("cat", L, (3, 2)[m - 2]))
                        root(("hsum", L, n), "h_rstd", (L, n), 1.0 / (64 if n >= 2 else 128), 512, rstd[:, m % 2, :])
                if L < 2:
                    norm(("post_mix", L), lambda p_: due("y", L, 0, p_))
                norm(("ffn", L), lambda p_: due("x", L, 0, p_))
                if L < 2:
                    shift(("ffn", L), 24)
                sc.preload_act_table_set("silu_and_others")
                for f in range(FT + 1):
                    if f < FT and L >= 2:
                        job = ("gu", L, f)
                        sc.wait_ge(*due(*job))
                        if f >= 2:
                            sc.wait_ge(*due("silu", L, f - 2))
                        nc.scalar.activation(conv[:, f % 2, :], ps(job)[:, 0:256], ACT.Identity, bias=v(f"conv_b{l}", f),
                                             scale=v(f"conv_w{l}", 44 + f)).then_inc(*sig("conv0", L, f))
                    if f >= 1:
                        g = f - 1
                        sc.wait_ge(*due(*(("gu", L, g) if L < 2 else ("conv", L, g))))
                        if g >= 2:
                            sc.wait_ge(*due("act", L, g - 2))
                        src = ps(("gu", L, g))[:, 0:256] if L < 2 else conv[:, g % 2, :]
                        nc.scalar.activation(silu[:, g % 2, :], src, ACT.Silu).then_inc(*sig("silu", L, g))
                sc.preload_act_table_set("natural_log_exp_and_others")
                if L < 2:
                    norm(("post_ffn", L), lambda p_: due("y", L, 1, p_))
            norm(("final", 0), lambda p_: due("x", 3, 1, p_))

        @block.vector
        def _(ve):
            steps = [0]

            def step(ins):
                steps[0] += 1
                ins.then_inc(*sig("ve_step", steps[0]))
                ve.wait_ge(*due("ve_step", steps[0]))

            def apply(N, g, has_shift):
                ve.wait_ge(*due("rstd", N))
                for t in range(KT):
                    nc.vector.scalar_tensor_tensor(h[:, t, :], x[:, t, :], g(t), rstd[:, 0, 0:256], ALU.mult, ALU.mult).then_inc(
                        *sig("scaled" if has_shift else "h", N, t))

            def update_post(L, which, gain):
                N = ("post_mix" if which == 0 else "post_ffn", L)
                ve.wait_ge(*due("rstd", N))
                for p_ in range(4):
                    for j in range(2):
                        t = 2 * p_ + j
                        step(nc.vector.scalar_tensor_tensor(tmp[:, 0:256], ps(("y", L, which, p_))[:, 256 * j:256 * (j + 1)],
                                                            gains[:, gain, t:t + 1], rstd[:, 0, 0:256], ALU.mult, ALU.mult))
                        last = nc.vector.tensor_tensor(x[:, t, :], x[:, t, :], tmp[:, 0:256], ALU.add)
                        if j == 0:
                            step(last)
                    last.then_inc(*sig("x", L, which, p_, frees=("y", L, which, p_)))
                    ve.wait_ge(*due("x", L, which, p_))

            def softmax(L, n, nh, w, w1, scale, mask, buf, sink):
                job = ("score", L, n)
                ve.wait_ge(*due(*job))
                if n >= 2:
                    ve.wait_ge(*due("probT", L, n - 2))
                pr = buf[:, n % 2, 0:nh * w1].rearrange("p (h k) -> p h k", h=nh)
                if sink is not None:
                    nc.vector.tensor_copy(pr[:, :, w], sink)
                nc.vector.scalar_tensor_tensor(pr[:, :, 0:w], ps(job)[:, 0:nh * w].rearrange("p (h k) -> p h k", h=nh), scale,
                                               bcast(mask, nh), ALU.mult, ALU.add).then_inc(*sig("scored", L, n, frees=job))
                ve.wait_ge(*due("scored", L, n))
                step(nc.vector.tensor_reduce(smax[:, n % 2, 0:nh], pr, AX_X, ALU.max))
                nc.vector.tensor_scalar(smax[:, n % 2, 0:nh], smax[:, n % 2, 0:nh], -1.0, None, ALU.mult).then_inc(*sig("smax", L, n))

            def normalize(L, n, nh, w, w1, buf):
                ve.wait_ge(*due("exp", L, n))
                step(nc.vector.reciprocal(ssum[:, n % 2, 0:nh], ssum[:, n % 2, 0:nh]))
                pr = buf[:, n % 2, 0:nh * w1].rearrange("p (h k) -> p h k", h=nh)
                nc.vector.tensor_tensor(pr[:, :, 0:w], pr[:, :, 0:w], ssum[:, n % 2, 0:nh].rearrange("p (h o) -> p h o", o=1).to_broadcast([P, nh, w]),
                                        ALU.mult).then_inc(*sig("prob", L, n))

            def rotate(raw, rot, cos, sin, n, name, *key, frees):
                w = 256 * n
                r3 = raw.rearrange("p (t s) -> p t s", t=n)
                step(nc.vector.tensor_tensor(tmp[:, 0:w].rearrange("p (t s) -> p t s", t=n), rot.rearrange("p (t s) -> p t s", t=n),
                                             bcast(sin, n), ALU.mult))
                step(nc.vector.tensor_tensor(r3, r3, bcast(cos, n), ALU.mult))
                nc.vector.tensor_tensor(raw, raw, tmp[:, 0:w], ALU.add).then_inc(*sig(name, *key, frees=frees))
                ve.wait_ge(*due(name, *key))

            magic, two_pi = 12582912.0, 6.283185307179586
            parts = (6.28125, 0.0019350051879882812, 3.019915982e-07)
            ve.wait_ge(*due("pos_in", 0))
            ve.wait_ge(*due("const_in", 0))
            step(nc.vector.tensor_copy(ang[:, :], pos_i[:, :]))
            step(nc.vector.tensor_scalar(ang[:, :], ang[:, :], k("freq"), None, ALU.mult))
            for i, quarter in ((0, 0.25), (1, 0.0)):
                step(nc.vector.tensor_scalar(tmp[:, 0:256], ang[:, :], 1.0 / two_pi, quarter, ALU.mult, ALU.add))
                step(nc.vector.tensor_scalar(tmp[:, 0:256], tmp[:, 0:256], magic, None, ALU.add))
                step(nc.vector.tensor_scalar(tmp[:, 0:256], tmp[:, 0:256], magic, None, ALU.subtract))
                step(nc.vector.scalar_tensor_tensor(turns[:, i, :], tmp[:, 0:256], -parts[0], ang[:, :], ALU.mult, ALU.add))
                for c in parts[1:]:
                    step(nc.vector.scalar_tensor_tensor(turns[:, i, :], tmp[:, 0:256], -c, turns[:, i, :], ALU.mult, ALU.add))
                step(nc.vector.tensor_scalar(turns[:, i, :], turns[:, i, :], quarter * two_pi, -3.1415925, ALU.add, ALU.max))
                nc.vector.tensor_scalar(turns[:, i, :], turns[:, i, :], 3.1415925, None, ALU.min).then_inc(*sig("turns", i))
            ve.wait_ge(*due("vec"))
            nc.vector.tensor_copy(vcol[:, :], ps(("vec",))[:, 0:NVEC * P]).then_inc(*sig("vcol", 0, frees=("vec",)))
            ve.wait_ge(*due("vcol", 0))

            def mod_part(L, i, c0, c1):
                l = L % 2
                ve.wait_ge(*due("ada_unit", L, c1 // 4 - 1))
                nc.vector.tensor_tensor(mods[:, c0:c1], ps(("ada", L, i))[:, c0:c1], v(f"ada_b{l}", c0, c1 - c0), ALU.add).then_inc(
                    *sig("mods", L, i, frees=("ada", L, i)))
                ve.wait_ge(*due("mods", L, i))
                if i == 0:
                    step(nc.vector.scalar_tensor_tensor(gains[:, 0, :], mods[:, 8:16], 1.0, v(f"g_pre_mix{l}", 0, 8), ALU.add, ALU.mult))
                elif i == 1:
                    step(nc.vector.tensor_tensor(gains[:, 1, :], mods[:, 16:24], v(f"g_post_mix{l}", 0, 8), ALU.mult))
                else:
                    step(nc.vector.scalar_tensor_tensor(gains[:, 2, :], mods[:, 32:40], 1.0, v(f"g_pre_ffn{l}", 0, 8), ALU.add, ALU.mult))
                    step(nc.vector.tensor_tensor(gains[:, 3, :], mods[:, 40:48], v(f"g_post_ffn{l}", 0, 8), ALU.mult))

            flat = lambda ap: ap.rearrange("p t s -> p (t s)")
            for L in range(NL):
                l = L % 2
                if L < 2:
                    mod_part(L, 0, 0, 16)
                    if L == 0:
                        ve.wait_ge(*due("x_in", 0))
                    apply(("mix", L), lambda t: gains[:, 0, t:t + 1], True)
                    ve.wait_ge(*due("bias_in", 0))
                    ve.wait_ge(*due("val", L))
                    nc.vector.tensor_tensor(tok[:, :, 0:128], ps(("val", L))[:, 0:256].rearrange("p (b n) -> p b n", b=2),
                                            bcast(bias_vu[:, l, 0:128], 2), ALU.add).then_inc(*sig("tok", L, 0, frees=("val", L)))
                    for tb in range(2):
                        ve.wait_ge(*due("stream", L, tb))
                        nc.vector.tensor_tensor(tok[:, tb, 128:640], ps(("stream", L, tb))[:, :], bias_vu[:, l, 128:640],
                                                ALU.add).then_inc(*sig("tok", L, 1 + tb, frees=("stream", L, tb)))
                    if L == 0:
                        ve.wait_ge(*due("rope1", 0))
                    for i in range(3):
                        n = 2 if i < 2 else 1
                        ve.wait_ge(*due("qk_rot", L, i))
                        rotate(flat(qk[:, 2 * i:2 * i + n, :]), ps(("qk_rot", L, i))[:, 0:256 * n], rope1[:, 0, :], rope1[:, 1, :], n,
                               "qk_done", L, i, frees=("qk_rot", L, i))
                    mod_part(L, 1, 16, 24)
                    for i in range(2):
                        for g in range(2):
                            ve.wait_ge(*due("poolw", L, i))
                            last = nc.vector.tensor_scalar(cat[:, 4 + 2 * i + g, :], ps(("poolw", L, i))[:, 256 * g:256 * (g + 1)],
                                                           v(f"pool_scale{l}", 2 * i + g), None, ALU.mult)
                        last.then_inc(*sig("cat_pool", L, i, frees=("poolw", L, i)))
                    ve.wait_ge(*due("sinks_in", 0))
                    for n in range(7):
                        if n < 6:
                            if n < 4:
                                g, jp = n // 2, n % 2
                                softmax(L, n, 2, 256, 257, 0.125, k("window"), prob, sinks[:, l, 4 * g + 2 * jp:4 * g + 2 * jp + 2])
                            else:
                                softmax(L, n, 4, 128, 129, 0.125, k("causal2", P, 2 * P), prob, sinks[:, l, 4 * (n - 4):4 * (n - 4) + 4])
                        if n >= 1:
                            m = n - 1
                            normalize(L, m, *((2, 256, 257) if m < 4 else (4, 128, 129)), prob)
                    mod_part(L, 2, 24, 48)
                    update_post(L, 0, 1)
                    apply(("ffn", L), lambda t: gains[:, 2, t:t + 1], True)
                else:
                    apply(("mix", L), lambda t: v(f"attn_norm{l}", t), False)
                    for i in range(3):
                        n = 2 if i < 2 else 1
                        ve.wait_ge(*due("c_raw", L, i))
                        c = cqkv[:, 2 * i:2 * i + n, :]
                        nc.vector.tensor_tensor(o_sb[:, 2 * i:2 * i + n, :], c, c, ALU.mult).then_inc(*sig("csq", L, i))
                    for n, tiles in enumerate(((0, 1, 2), (3, 4))):
                        ve.wait_ge(*due("c_rstd", L, n))
                        for t in tiles:
                            g = v(f"q_norm{l}", t) if n == 0 else v(f"kv_norm{l}", t - 3)
                            nc.vector.scalar_tensor_tensor(cnorm[:, t, :], cqkv[:, t, :], g, rstd[:, 1, 256 * n:256 * n + 256],
                                                           ALU.mult, ALU.mult).then_inc(*sig("cnorm", L, t))
                    ve.wait_ge(*due("ggate", L))
                    nc.vector.tensor_scalar(lsum, ps(("ggate", L))[:, 0:256], v(f"gla_b{l}"), None, ALU.add).then_inc(*sig("ggate_in", L, frees=("ggate", L)))
                    ve.wait_ge(*due("kr_rot", L))
                    rotate(qh[:, 6, :], ps(("kr_rot", L))[:, 0:256], k("mlacos"), k("mlasin"), 1, "kr_in", L, frees=("kr_rot", L))
                    for i in range(2):
                        last = nc.vector.tensor_scalar(kr2[:, i, :], qh[:, 6, :], k("ones64", 127 * i, 127 * i + 1), None, ALU.mult)
                    last.then_inc(*sig("kr2", L))
                    ve.wait_ge(*due("rqk_rot", L))
                    rotate(gr[:, 512:1024], ps(("rqk_rot", L))[:, :], k("retcos"), k("retsin"), 2, "rqk_in", L, frees=("rqk_rot", L))
                    for hd in range(4):
                        last = nc.vector.tensor_scalar(kbd[:, hd, :], rk, k("headmask", hd, hd + 1), 32.0 ** -0.5, ALU.mult, ALU.mult)
                    last.then_inc(*sig("rkbd", L))
                    ve.wait_ge(*due("lsig", L, 2))
                    step(nc.vector.scalar_tensor_tensor(tmp[:, 0:256], lsum, 0.0, expk, ALU.min, ALU.subtract))
                    step(nc.vector.tensor_tensor_scan(lsum, k("ones", 0, 1).to_broadcast([P, S]), tmp[:, 0:256], 0.0, ALU.mult, ALU.add))
                    middle = lsum.rearrange("p (j s) -> p j s", j=4)[:, :, 31]
                    nc.vector.tensor_scalar(mid[:, 0:4], middle, 1.0 / 16, None, ALU.mult)
                    nc.vector.tensor_scalar(mid[:, 4:8], middle, -1.0 / 16, None, ALU.mult).then_inc(*sig("gmid", L))
                    ve.wait_ge(*due("qr_rot", L))
                    rotate(flat(qh[:, 4:6, :]), ps(("qr_rot", L))[:, :], k("mlacos"), k("mlasin"), 2, "qr_in", L, frees=("qr_rot", L))
                    for hd in range(4):
                        ve.wait_ge(*due("rscore", L, hd))
                        nc.vector.tensor_tensor(attT[:, hd, 0:256], ps(("rscore", L, hd))[:, 0:256], k("decay", 256 * hd, 256 * hd + 256), ALU.mult)
                        nc.vector.tensor_tensor(attT[:, hd, 256:384], ps(("rscore", L, hd))[:, 256:384], k("decay", 256 * hd, 256 * hd + 128),
                                                ALU.mult).then_inc(*sig("ratt", L, hd, frees=("rscore", L, hd)))
                    args = lambda n: (2, 256, 256) if n < 2 else (4, 128, 128)
                    sc_ = 192.0 ** -0.5
                    softmax(L, 0, *args(0), sc_, k("causal2"), prob2, None)
                    softmax(L, 1, *args(1), sc_, k("causal2"), prob2, None)
                    ve.wait_ge(*due("gexp", L))
                    ve.wait_ge(*due("gqk_raw", L))
                    for J in range(4):
                        nc.vector.tensor_tensor(expq[:, J, 64 * J:256], expq[:, J, 64 * J:256], gq[:, 64 * J:256], ALU.mult)
                        if J % 2:
                            nc.vector.memset(expq[:, J, 64 * J - 64:64 * J], 0.0)
                    for hd in range(4):
                        if hd == 0:
                            ve.wait_ge(*due("rscore", L, 3))
                        last = nc.vector.scalar_tensor_tensor(kbd[:, hd, :], gk, k("headmask", hd, hd + 1), expk, ALU.mult, ALU.mult)
                    last.then_inc(*sig("gkbd", L))
                    normalize(L, 0, *args(0), prob2)
                    softmax(L, 2, *args(2), sc_, k("causal2", P, 2 * P), prob2, None)
                    normalize(L, 1, *args(1), prob2)
                    ve.wait_ge(*due("rout", L))
                    for hd in range(4):
                        ve.wait_ge(*due("gscore", L, hd))
                        nc.vector.tensor_tensor(attT[:, hd, :], ps(("gscore", L, hd))[:, 0:384], k("glamask"),
                                                ALU.mult).then_inc(*sig("gatt", L, hd, frees=("gscore", L, hd)))
                    normalize(L, 2, *args(2), prob2)
                    for m, n in enumerate((3, 2, 0, 1)):
                        ve.wait_ge(*due("h_rstd", L, n))
                        for j in range(2):
                            t = 2 * n + j
                            g = v(f"ret_out{l}", j) if n == 3 else v(f"gla_out{l}", j) if n == 2 else v(f"mla_out{l}", t)
                            last = nc.vector.scalar_tensor_tensor(cat[:, t, :], o_sb[:, t, :], g, rstd[:, m % 2, 256 * j:256 * (j + 1)],
                                                                  ALU.mult, ALU.mult)
                        if n < 2:
                            last.then_inc(*sig("cat", L, n))
                        else:
                            step(last)
                            ve.wait_ge(*due("gates", L, 1))
                            nc.vector.tensor_tensor(cat[:, 2 * n:2 * n + 2, :], cat[:, 2 * n:2 * n + 2, :], gates[:, 2 * (n - 2):2 * (n - 2) + 2, :],
                                                    ALU.mult).then_inc(*sig("cat", L, n))
                    for p_ in range(4):
                        ve.wait_ge(*due("y", L, 0, p_))
                        xs = flat(x[:, 2 * p_:2 * p_ + 2, :])
                        nc.vector.tensor_tensor(xs, xs, ps(("y", L, 0, p_))[:, :], ALU.add).then_inc(*sig("x", L, 0, p_, frees=("y", L, 0, p_)))
                    apply(("ffn", L), lambda t: v(f"ffn_norm{l}", t), False)
                for f in range(FT + 1):
                    if f < FT and L >= 2:
                        bank = ps(("gu", L, f))
                        ve.wait_ge(*due("conv0", L, f))
                        step(nc.vector.scalar_tensor_tensor(conv[:, f % 2, 1:S], bank[:, 0:S - 1], v(f"conv_w{l}", 22 + f), conv[:, f % 2, 1:S],
                                                            ALU.mult, ALU.add))
                        nc.vector.scalar_tensor_tensor(conv[:, f % 2, 2:S], bank[:, 0:S - 2], v(f"conv_w{l}", f), conv[:, f % 2, 2:S],
                                                       ALU.mult, ALU.add).then_inc(*sig("conv", L, f))
                    if f >= 1:
                        g = f - 1
                        ve.wait_ge(*due("silu", L, g))
                        nc.vector.tensor_tensor(act[:, g, :], silu[:, g % 2, :], ps(("gu", L, g))[:, 256:512], ALU.mult).then_inc(
                            *sig("act", L, g, frees=("gu", L, g)))
                if L < 2:
                    update_post(L, 1, 3)
                else:
                    for p_ in range(4):
                        ve.wait_ge(*due("y", L, 1, p_))
                        xs = flat(x[:, 2 * p_:2 * p_ + 2, :])
                        nc.vector.tensor_tensor(xs, xs, ps(("y", L, 1, p_))[:, :], ALU.add).then_inc(*sig("x", L, 1, p_, frees=("y", L, 1, p_)))
            ve.wait_ge(*due("rstd", ("final", 0)))
            for t in range(KT):
                last = nc.vector.scalar_tensor_tensor(h[:, t, :], x[:, t, :], v("final", t), rstd[:, 0, 0:256], ALU.mult, ALU.mult)
                if t % 2:
                    last.then_inc(*sig("out_ready", t // 2))


def kernel(**inputs):
    import concourse.bacc as bacc
    from concourse.bass_utils import run_bass_kernel_spmd as run

    a = {n: np.asarray(v) for n, v in inputs.items()}
    const, const_at = const_table()
    arrays = {
        "x_t": np.ascontiguousarray(a["x"][0].T.reshape(KT, P, S).transpose(1, 0, 2)),
        "positions": np.ascontiguousarray(a["positions"]),
        "const_table": np.ascontiguousarray(const),
        "vectors": pack_vectors(a),
        "weights": pack_weights(a),
        "bias_rows": np.ascontiguousarray(a["b_in"][:, 640:1280]),
        "sink_rows": np.ascontiguousarray(a["sinks"]),
        "gate_w": np.ascontiguousarray(a["gla_w_gate_2"]),
    }
    counts = Counts()
    for _ in range(2):
        nc = bacc.Bacc("TRN2", target_bir_lowering=False, num_devices=1)
        t = {n: nc.dram_tensor(n, v.shape, mybir.dt.from_np(v.dtype), kind="ExternalInput").ap() for n, v in arrays.items()}
        out = nc.dram_tensor("out_t", (P, KT, S), F32, kind="ExternalOutput").ap()
        build(nc, counts, t["x_t"], t["positions"], t["const_table"], const_at, t["vectors"], t["weights"], t["bias_rows"],
              t["sink_rows"], t["gate_w"], out)
    r = run(nc, [arrays], core_ids=[0])
    got = r.results[0]["out_t"]
    return got.transpose(1, 0, 2).reshape(D, S).T.reshape(1, S, D)
```

```python
from contextlib import ExitStack

import numpy as np

import concourse.bass as bass
from concourse import mybir

F32 = mybir.dt.float32
F32R = mybir.dt.float32r
I32 = mybir.dt.int32
ALU = mybir.AluOpType
ACT = mybir.ActivationFunctionType
AX_X = mybir.AxisListType.X

P = 128
S = 256
D = 1024
KT = D // P
NL = 4
FF = 2816
FT = FF // P
EPS = 1e-6
NEG = -1e30
HEADS = 8
HEAD_DIM = 64
ROT = 16
POOLS = (2, 4, 8, 16)
SLOT = FF
NRAW = 3
NSPLIT = 2
NADA = 24


def const_table():
    parts, at = [], {}

    def put(name, a):
        a = np.asarray(a, np.float32).reshape(P, -1)
        start = sum(b.shape[1] for b in parts)
        at[name] = (start, start + a.shape[1])
        parts.append(a)

    def rot_matrix(period, half):
        r = np.zeros((P, P))
        for m in range(P):
            o = m % period
            if o < half:
                r[m + half, m] = -1.0
            elif o < 2 * half:
                r[m - half, m] = 1.0
        return r

    def rope(dim, base, copies):
        inv = base ** (-(np.arange(0, dim, 2, dtype=np.float32) / dim))
        ang = (np.arange(S, dtype=np.float32)[:, None] * inv[None, :].astype(np.float32)).astype(np.float32)
        c, s = np.cos(ang).T, np.sin(ang).T
        return np.tile(np.concatenate([c, c]), (copies, 1)), np.tile(np.concatenate([s, s]), (copies, 1))

    i = np.arange(P)
    put("ident", np.eye(P))
    put("ones", np.ones((P, P)))
    put("ones64", (i[:, None] // 64 == i[None, :] // 64))
    put("rot16", rot_matrix(HEAD_DIM, ROT // 2))
    put("rot64", rot_matrix(64, 32))
    put("rot32", rot_matrix(32, 16))
    k2 = np.arange(2 * P)
    diff = i[:, None] + P - k2[None, :]
    put("window", np.where((diff >= 0) & (diff < P), 0.0, NEG))
    put("causal2", np.where(diff >= 0, 0.0, NEG))
    t = np.arange(S)
    band = []
    for w in POOLS:
        full = ((t[None, :] - t[:, None] >= 0) & (t[None, :] - t[:, None] < w)) / np.minimum(t + 1.0, w)[None, :] - np.eye(S)
        band += [full[:P, :], full[P:, P:]]
    put("band", np.concatenate(band, 1))
    lower = (t[None, :] >= i[:, None]).astype(float)
    put("glamask", lower)
    decay = []
    for h in range(4):
        g = np.log(1.0 - 2.0 ** (-5.0 - h))
        d = np.where(t[None, :] >= i[:, None], np.exp(g * np.maximum(t[None, :] - i[:, None], 0)), 0.0)
        decay.append(d)
    put("decay", np.concatenate(decay, 1))
    for name, (c, s) in (("mla", rope(64, 10000.0, 2)), ("ret", rope(32, 10000.0, 4))):
        put(name + "cos", c)
        put(name + "sin", s)
    put("headmask", (i[:, None] // 32 == np.arange(4)[None, :]))
    inv = np.float32(500000.0) ** (-np.arange(0, ROT, 2, dtype=np.float32) / np.float32(ROT))
    freq = np.zeros(P)
    for m in range(P):
        if m % HEAD_DIM < ROT:
            freq[m] = inv[m % HEAD_DIM % (ROT // 2)]
    put("freq", freq)
    put("eps", np.full(P, EPS))
    return np.concatenate(parts, 1), at


VECTORS = []
for _l in range(2):
    VECTORS += [(f"ada_b{_l}", 48), (f"g_pre_mix{_l}", 8), (f"g_post_mix{_l}", 8), (f"g_pre_ffn{_l}", 8),
                (f"g_post_ffn{_l}", 8), (f"b_qk{_l}", 5), (f"pool_scale{_l}", 4)]
for _l in range(2):
    VECTORS += [(f"attn_norm{_l}", 8), (f"q_norm{_l}", 3), (f"kv_norm{_l}", 2), (f"mla_out{_l}", 4),
                (f"gla_b{_l}", 1), (f"gla_out{_l}", 2), (f"ret_out{_l}", 2), (f"ffn_norm{_l}", 8),
                (f"conv_w{_l}", 66), (f"conv_b{_l}", 22)]
VECTORS += [("final", 8), ("c", 8)]
COL, _n = {}, 0
for _name, _t in VECTORS:
    COL[_name] = _n
    _n += _t
NVEC = (_n + P - 1) // P


def unit_list():
    units = []

    def add(kind, L, i, kt, cols, *ada):
        units.append(((kind, L, i), kt, cols))
        units.extend((("ada", l, n), KT, 256) for l, n in ada)

    units += [(("ada", 0, n), KT, 256) for n in range(8)]
    for L in range(2):
        for i, cols in enumerate((256, 256, 128)):
            add("qk", L, i, KT, cols)
        add("val", L, 0, KT, 128)
        for i in range(2):
            add("st", L, i, KT, 256, *([(0, 8 + 2 * i), (0, 9 + 2 * i)] if L == 0 else [(1, 16 + i)]))
        for i in range(4):
            add("wo", L, i, KT, 256, *([(0, 12 + 2 * i), (0, 13 + 2 * i)] if L == 0 else [(1, 18 + i)] if i < 2 else []))
        for f in range(FT):
            add("gu", L, f, KT, 256, *([(L, 20 + f)] if f < 4 else [(1, f - 4)] if L == 0 and f < 20 else []))
        for m in range(KT):
            add("wd", L, m, FT, 128)
    for L in range(2, 4):
        for kind, i, cols in (("z0", 0, 256), ("z0", 1, 256), ("z0", 2, 128), ("kr", 0, 128), ("gqk", 0, 256), ("rqk", 0, 256),
                              ("glr", 0, 128), ("gg", 0, 256), ("rg", 0, 256), ("gv", 0, 256), ("rv", 0, 256)):
            add(kind, L, i, KT, cols)
        add("uq", L, 0, 3, 768)
        add("ukv", L, 0, 2, 1024)
        for i in range(4):
            add("wo", L, i, KT, 256)
        for f in range(FT):
            add("gu", L, f, KT, 256)
        for m in range(KT):
            add("wd", L, m, FT, 128)
    return units


UNITS = unit_list()
UNIT_NO = {u[0]: n for n, u in enumerate(UNITS)}
SPLITS = [u[0] for u in UNITS if u[0][0] != "ada"]
SPLIT_NO = {u: n for n, u in enumerate(SPLITS)}


def ada_groups(n):
    run = []
    while n < len(UNITS) and UNITS[n][0][0] == "ada":
        run.append(UNITS[n][0])
        n += 1
    return [run[i:i + 2] for i in range(0, len(run), 2)]


def tiled(w):
    rows, cols = w.shape
    return w.reshape(rows // P, P, cols).transpose(1, 0, 2).reshape(P, -1)


def pack_weights(a):
    heads = [h for j in range(4) for h in (j, j + 4)]
    out = []
    sizes = (384, 256, 64, 128, 128, 256, 16, 256, 128, 128, 256, 256)
    for (kind, L, i), kt, cols in UNITS:
        l = L % 2
        c = slice(256 * i, 256 * (i + 1))
        if kind == "ada":
            w = a["ada_w"][l][:, c]
        elif kind == "qk":
            q = a["w_in"][l][:, :512].reshape(D, HEADS, HEAD_DIM)[:, heads].reshape(D, 512)
            w = np.concatenate([q, a["w_in"][l][:, 512:640]], 1)[:, 256 * i:256 * i + cols]
        elif kind == "val":
            w = a["w_in"][l][:, 640:768]
        elif kind == "st":
            w = a["w_in"][l][:, 768:][:, c]
        elif kind == "wo" and L < 2:
            att = a["w_out"][l][:512].reshape(HEADS, HEAD_DIM, D)[heads].reshape(512, D)
            w = np.concatenate([att, a["w_out"][l][512:]], 0)[:, c]
        elif kind == "wo":
            w = a["w_out_2"][l][:, c]
        elif kind == "gu":
            one, two = (a["w_gate"][l], a["w_up"][l]) if L < 2 else (a["ffn_w_up_2"][l][:, :FF], a["ffn_w_up_2"][l][:, FF:])
            w = np.concatenate([one[:, P * i:P * (i + 1)], two[:, P * i:P * (i + 1)]], 1)
        elif kind == "wd":
            w = (a["w_down"] if L < 2 else a["ffn_w_down_2"])[l][:, P * i:P * (i + 1)]
        elif kind == "uq":
            w = a["mla_w_uq_2"][l].reshape(384, 4, 192)
            w = np.concatenate([w[:, :, :128].reshape(384, 512), w[:, :, 128:].reshape(384, 256)], 1)
        elif kind == "ukv":
            w = a["mla_w_ukv_2"][l].reshape(256, 4, 256)
            w = np.concatenate([w[:, :, :128].reshape(256, 512), w[:, :, 128:].reshape(256, 512)], 1)
        else:
            cq, ckv, kr, gq, gk, gv, glr, gg, rq, rk, rv, rg = np.split(a["w_in_2"][l], np.cumsum(sizes)[:-1], 1)
            w = {"z0": lambda: np.concatenate([cq, ckv], 1)[:, 256 * i:256 * i + cols], "kr": lambda: np.concatenate([kr, kr], 1),
                 "gqk": lambda: np.concatenate([gq, gk], 1), "rqk": lambda: np.concatenate([rq, rk], 1),
                 "glr": lambda: np.concatenate([glr, np.zeros((D, P - 16), glr.dtype)], 1), "gg": lambda: gg, "rg": lambda: rg,
                 "gv": lambda: gv, "rv": lambda: rv}[kind]()
        w = tiled(w)
        assert w.shape == (P, kt * cols), (kind, w.shape)
        out.append(w.ravel())
    return np.concatenate(out)


def pack_vectors(a):
    heads = [h for j in range(4) for h in (j, j + 4)]
    rows = []
    for name, tiles in VECTORS:
        base, l = (name[:-1], int(name[-1])) if name[-1].isdigit() else (name, 0)
        v = {
            "ada_b": lambda: a["ada_b"][l], "b_qk": lambda: np.concatenate(
                [a["b_in"][l][:512].reshape(HEADS, HEAD_DIM)[heads].ravel(), a["b_in"][l][512:640]]),
            "attn_norm": lambda: a["attn_norm_2"][l], "q_norm": lambda: a["mla_q_norm_2"][l],
            "kv_norm": lambda: a["mla_kv_norm_2"][l], "mla_out": lambda: a["mla_out_norm_2"][l],
            "gla_b": lambda: a["gla_b_gate_2"][l], "gla_out": lambda: a["gla_out_norm_2"][l],
            "ret_out": lambda: a["ret_out_norm_2"][l], "ffn_norm": lambda: a["ffn_norm_2"][l],
            "conv_w": lambda: a["ffn_conv_w_2"][l], "conv_b": lambda: a["ffn_conv_b_2"][l],
            "final": lambda: a["final_norm_2"], "c": lambda: a["c"],
        }.get(base, lambda: a[base][l])()
        rows.append(np.asarray(v).reshape(tiles, P))
    rows = np.concatenate(rows)
    rows = np.concatenate([rows, np.zeros((NVEC * P - len(rows), P), rows.dtype)])
    return np.ascontiguousarray(rows.reshape(NVEC, P, P).transpose(1, 0, 2).reshape(P, NVEC * P))


class Counts:

    def __init__(self):
        self.value = {}
        self.freed_by = {}
        self.last_use = {}


def build(nc, counts, a_x, a_pos, a_const, const_at, a_vec, a_w, a_bias, a_sinks, a_gatew, a_poolw, out):
    ctx = ExitStack()
    with ctx:
        def sb(name, shape, dt=F32):
            return ctx.enter_context(nc.sbuf_tensor(name, shape, dt))

        psum = [ctx.enter_context(nc.psum_tensor(f"bank{b}", [P, 512], F32)) for b in range(8)]

        sems, so_far = {}, {}

        def sem(name):
            if name not in sems:
                sems[name] = ctx.enter_context(nc.semaphore(name))
                so_far[name] = 0
            return sems[name]

        def sig(name, *key, frees=None, by=1):
            s = sem(name)
            so_far[name] += by
            counts.value[(name, *key)] = so_far[name]
            if frees is not None:
                counts.freed_by[frees] = (name, *key)
            return s, by

        def due(name, *key):
            return sem(name), counts.value.get((name, *key), 1)

        raw_w = sb("raw_w", [P, NRAW, SLOT])
        hi_w = sb("hi_w", [P, NSPLIT, SLOT], F32R)
        lo_w = sb("lo_w", [P, NSPLIT, SLOT], F32R)
        const = sb("const", [P, a_const.shape[1]])
        vcol = sb("vcol", [P, NVEC * P])
        x = sb("x", [P, KT, S])
        raw = sb("raw", [P, KT, S])
        in_hi = sb("in_hi", [P, KT, S], F32R)
        in_lo = sb("in_lo", [P, KT, S], F32R)
        silu = sb("silu", [P, 2, S])
        hidden = sb("hidden", [P, 2, S])
        shared = sb("shared", [P, 1536])
        bias_vu = shared[:, 0:1280].rearrange("p (l n) -> p l n", l=2)
        gates = shared[:, 0:1024].rearrange("p (t s) -> p t s", t=4)
        conv = shared[:, 1024:1536].rearrange("p (b s) -> p b s", b=2)
        rstd = sb("rstd", [P, 2, 512])
        ada_sum = sb("ada_sum", [P, 4, 256])
        c_act = sb("c_act", [P, KT])
        mods = sb("mods", [P, 2, 48])
        gains = sb("gains", [P, 2, 4, KT])
        rope1 = sb("rope1", [P, 2, S])
        sinks = sb("sinks", [P, 2, HEADS])
        gatew = sb("gatew", [16, 2, P])
        poolw = sb("poolw", [P, 2, 4, P])
        tmp = sb("tmp", [P, 512])
        smax = sb("smax", [P, 3, 4])
        ssum = sb("ssum", [P, 3, 4])

        def overlay(*tensors):
            with ExitStack() as own:
                return [own.enter_context(nc.sbuf_tensor(name, [P, n], dt)) for name, n, dt in tensors]

        start, = overlay(("start", 2048, F32))
        vrow = start[:, 0:NVEC * P]
        pos_i = start[:, 1024:1280].bitcast(I32)
        ang = start[:, 1280:1536]
        turns = start[:, 1536:2048].rearrange("p (i s) -> p i s", i=2)

        hid_hi, hid_lo = (t[:, :].rearrange("p (t s) -> p t s", t=FT) for t in overlay(("hid_hi", FT * S, F32R), ("hid_lo", FT * S, F32R)))

        qk, tok, prob, probT, pooled = overlay(("qk", 1280, F32), ("tok", 1280, F32), ("prob", 3 * 516, F32),
                                               ("probT", 6 * 512, F32), ("pooled", 1024, F32))
        qk = qk[:, :].rearrange("p (t s) -> p t s", t=5)
        tok = tok[:, :].rearrange("p (b n) -> p b n", b=2)
        prob = prob[:, :].rearrange("p (b n) -> p b n", b=3)
        probT = probT[:, :].rearrange("p (b n) -> p b n", b=6)
        pooled = pooled[:, :].rearrange("p (g s) -> p g s", g=4)

        cqkv, cn_hi, cn_lo, qh, vm, vgr, gr = overlay(("cqkv", 1280, F32), ("cn_hi", 1280, F32R), ("cn_lo", 1280, F32R), ("qh", 1792, F32),
                                                      ("vm", 1024, F32), ("vgr", 1024, F32), ("gr", 3336, F32))
        _, prob2, probT2 = overlay(("cqkv_under", 1280, F32), ("prob2", 1024, F32), ("probT2", 1536, F32))
        kn = cqkv[:, 0:1024].rearrange("p (t s) -> p t s", t=4)
        cqkv = cqkv[:, :].rearrange("p (t s) -> p t s", t=5)
        cn_hi = cn_hi[:, :].rearrange("p (t s) -> p t s", t=5)
        cn_lo = cn_lo[:, :].rearrange("p (t s) -> p t s", t=5)
        prob2 = prob2[:, :].rearrange("p (b n) -> p b n", b=2)
        probT2 = probT2[:, :].rearrange("p (b n) -> p b n", b=3)
        head_sq = qh[:, 0:1024].rearrange("p (b n) -> p b n", b=2)
        qh = qh[:, :].rearrange("p (t s) -> p t s", t=7)
        vm = vm[:, :].rearrange("p (b n) -> p b n", b=2)
        vgr = vgr[:, :].rearrange("p (b n) -> p b n", b=2)
        gq, gk, rq, rk = (gr[:, 256 * n:256 * (n + 1)] for n in range(4))
        lsum = gr[:, 1024:1280]
        attT = gr[:, 1280:2816].rearrange("p (h n) -> p h n", h=4)
        expk = gr[:, 2816:3072]
        glr = gr[0:16, 3072:3328]
        mid = gr[:, 3328:3336]
        expq = poolw[:, :, :, :].rearrange("p l g d -> p (l g d)").rearrange("p (j s) -> p j s", j=4)
        kbd = ada_sum[:, :, :]
        kr2 = silu
        def k(name, a=0, b=None):
            lo, hi = const_at[name]
            return const[:, lo + a:(hi if b is None else lo + b)]

        def v(name, i=0, n=1):
            return vcol[:, COL[name] + i:COL[name] + i + n]

        def bcast(ap, n):
            return ap.rearrange("p (o s) -> p o s", o=1).to_broadcast([ap.shape[0], n, ap.shape[1]])

        def raw_view(unit):
            n = UNIT_NO[unit]
            return raw_w[:, n % NRAW, 0:UNITS[n][1] * UNITS[n][2]]

        def halves(unit):
            _, kt, cols = UNITS[UNIT_NO[unit]]
            w = kt * cols // 2
            return [slice(0, w), slice(w, 2 * w)]

        block = ctx.enter_context(nc.Block())

        bank_of, occupant = {}, [None] * 8

        def ps(job):
            return psum[bank_of[job]]

        @block.tensor
        def _(pe):
            n_jobs = [0]

            def take(job):
                b = n_jobs[0] % 8
                n_jobs[0] += 1
                if occupant[b] is not None and occupant[b] in counts.freed_by:
                    pe.wait_ge(*due(*counts.freed_by[occupant[b]]))
                occupant[b] = job
                bank_of[job] = b
                return psum[b]

            stream, current = [0], [None]

            def weights(unit, job):
                if unit != current[0]:
                    for units in ada_groups(stream[0]):
                        ada_reduce(units)
                        stream[0] += len(units)
                    assert UNITS[stream[0]][0] == unit, unit
                    stream[0] += 1
                    current[0] = unit
                pe.wait_ge(*due("lo_w", unit, 1))
                counts.last_use[unit] = job
                _, kt, cols = UNITS[UNIT_NO[unit]]
                n = SPLIT_NO[unit] % NSPLIT
                return tuple(w[:, n, 0:kt * cols].rearrange("p (t c) -> p t c", t=kt) for w in (hi_w, lo_w))

            def ada_reduce(units):
                job = ("ada", units[-1])
                b = take(job)
                for i, unit in enumerate(units):
                    pe.wait_ge(*due("ada_sum", unit))
                    for f in range(2):
                        last = nc.tensor.matmul(b[:, 2 * i + f:2 * i + f + 1], ada_sum[:, unit[2] % 4, P * f:P * (f + 1)], k("ones", 0, 1),
                                                start=True, stop=True)
                last.then_inc(*sig(*job))

            def exact(o, st, mv, start, stop, **kw):
                nc.tensor.matmul(o, st[1], mv[0], start=start, stop=False, **kw)
                nc.tensor.matmul(o, st[0], mv[1], start=False, stop=False, **kw)
                return nc.tensor.matmul(o, st[0], mv[0], start=False, stop=stop, **kw)

            def group(o, pairs):
                for i, (w, r) in enumerate(pairs):
                    last = nc.tensor.matmul(o, w, r, start=(i == 0), stop=(i == len(pairs) - 1))
                return last

            def half(bank, i):
                return bank[:, 256 * i:256 * (i + 1)]

            def sums(N, tiles, ones, src, wait):
                job = ("sums", *N)
                b = take(job)
                for i, t in enumerate(tiles):
                    wait(t)
                    last = nc.tensor.matmul(b[:, 0:256], ones, src[:, t, :], start=(i == 0), stop=(i == len(tiles) - 1))
                last.then_inc(*sig(*job))

            def norm_sums(N):
                sums(N, range(KT), k("ones"), raw, lambda t: pe.wait_ge(*due("squared", N, t // 2)) if t % 2 == 0 else None)

            both = (in_hi, in_lo)

            def product(job, unit, src, wait=None, c0=0, n=2, at=0, first=True, last=True):
                w = weights(unit, job)
                kts = UNITS[UNIT_NO[unit]][1]
                b = take(job) if first else ps(job)
                order = [(i, t) for i in range(n) for t in range(kts)] if wait is None else [(i, t) for t in range(kts) for i in range(n)]
                for i, t in order:
                    if wait is not None and i == 0:
                        wait(t)
                    c = c0 + P * i
                    kw = {} if wait is None or n == 1 else {"skip_group_check": True}
                    done = exact(half(b, at + i), [v_[:, t, c:c + P] for v_ in w], [v_[:, t, :] for v_ in src],
                                 start=(t == 0 and (i == 0 or wait is None)), stop=(t == kts - 1), **kw)
                if last:
                    done.then_inc(*sig(*job))
                else:
                    done.then_inc(*sig("part", unit))
                    counts.last_use[unit] = ("part", unit)

            def token_product(job, unit, src, tb, c0, cols, o0, last, tiles):
                w = weights(unit, job)
                for n, t in enumerate(tiles):
                    done = exact(ps(job)[:, o0:o0 + cols], [v_[:, t, P * tb:P * (tb + 1)] for v_ in src],
                                 [v_[:, n, c0:c0 + cols] for v_ in w], start=(n == 0), stop=(n == len(tiles) - 1))
                if last:
                    done.then_inc(*sig(*job))
                elif tb == 1:
                    done.then_inc(*sig("part", unit))
                    counts.last_use[unit] = ("part", unit)

            def transposes(job, srcs):
                b = take(job)
                for i, s_ in enumerate(srcs):
                    last = nc.tensor.transpose(b[:, P * i:P * (i + 1)], s_, k("ident"))
                last.then_inc(*sig(*job))

            pe.wait_ge(*due("const_in", 0))
            pe.wait_ge(*due("vec_in", 0))
            transposes(("vec",), [vrow[:, P * g:P * (g + 1)] for g in range(NVEC)])
            pe.wait_ge(*due("c_act", 0))

            for L in range(NL):
                h_wait = lambda t: pe.wait_ge(*due("in_lo", ("mix", L), t))
                if L == 0:
                    norm_sums(("mix", L))
                if L < 2:
                    for i in range(3):
                        product(("qk", L, i), ("qk", L, i), both, h_wait if i == 0 else None, n=2 if i < 2 else 1)
                    job = ("val", L)
                    take(job)
                    token_product(job, ("val", L, 0), both, 0, 0, 128, 0, False, range(KT))
                    token_product(job, ("val", L, 0), both, 1, 0, 128, 128, True, range(KT))
                    for tb in range(2):
                        take(("stream", L, tb))
                    for u in range(2):
                        for tb in range(2):
                            token_product(("stream", L, tb), ("st", L, u), both, tb, 0, 256, 256 * u, u == 1, range(KT))
                    for i in range(3):
                        pe.wait_ge(*due("qk_raw", L, i))
                        n = 512 if i < 2 else 256
                        b = take(("qk_rot", L, i))
                        nc.tensor.matmul(b[:, 0:n], k("rot16"), qk[:, 2 * i:2 * i + n // 256, :], start=True, stop=True).then_inc(*sig("qk_rot", L, i))
                    pe.wait_ge(*due("poolw_in", 0))
                    for i in range(2):
                        pe.wait_ge(*due("tok", L, 2))
                        job = ("pool", L, i)
                        b = take(job)
                        for g in range(2):
                            gi = 2 * i + g
                            o = half(b, g)
                            nc.tensor.matmul(o, tok[:, 0, 128 + P * gi:256 + P * gi], k("band", 384 * gi, 384 * gi + 256), start=True, stop=False)
                            last = nc.tensor.matmul(o[:, P:2 * P], tok[:, 1, 128 + P * gi:256 + P * gi], k("band", 384 * gi + 256, 384 * gi + 384), start=False, stop=True)
                        last.then_inc(*sig(*job))
                    for i in range(2):
                        job = ("poolw", L, i)
                        pe.wait_ge(*due("pooled", L, i))
                        b = take(job)
                        for g in range(2):
                            last = group(half(b, g), [(poolw[:, L, 2 * i + g, :], pooled[:, 2 * i + g, :])])
                        last.then_inc(*sig(*job))
                    pe.wait_ge(*due("qk_done", L, 2))
                    for g in range(2):
                        rows = slice(64 * g, 64 * g + 64)
                        for jp in range(2):
                            pe.wait_ge(*due("qk_done", L, jp))
                            job = ("score", L, 2 * g + jp)
                            b = take(job)
                            for j in range(2):
                                last = group(half(b, j), [(qk[rows, 2 * jp + j, P:2 * P], qk[rows, 4, :])])
                            last.then_inc(*sig(*job))
                    for g in range(2):
                        rows = slice(64 * g, 64 * g + 64)
                        job = ("score", L, 4 + g)
                        b = take(job)
                        for j in range(4):
                            last = group(b[:, P * j:P * (j + 1)], [(qk[rows, j, 0:P], qk[rows, 4, 0:P])])
                        last.then_inc(*sig(*job))
                    for n in range(6):
                        pe.wait_ge(*due("prob", L, n))
                        p_ = prob[:, n % 3, :]
                        cut = (lambda i: p_[:, 257 * (i // 2) + P * (i % 2):][:, 0:P]) if n < 4 else (lambda i: p_[:, 128 * i + i:][:, 0:P])
                        transposes(("probT", L, n), [cut(i) for i in range(4)])
                    for jp in range(2):
                        job = ("attn", L, jp)
                        b = take(job)
                        for n in (jp, 2 + jp, 4, 5):
                            pe.wait_ge(*due("probT_in", L, n))
                        for j in range(2):
                            for g in range(2):
                                val = lambda kb: tok[:, kb, 64 * g:64 * g + 64]
                                o = b[64 * g:64 * g + 64, 256 * j:256 * (j + 1)]
                                t1 = probT[:, 2 * g + jp, 256 * j:256 * (j + 1)]
                                t0 = probT[:, 4 + g, P * (2 * jp + j):P * (2 * jp + j + 1)]
                                group(o[:, 0:P], [(val(0), t0)])
                                last = group(o[:, P:2 * P], [(val(0), t1[:, 0:P]), (val(1), t1[:, P:2 * P])])
                        last.then_inc(*sig(*job))
                else:
                    product(("z0", L, 0), ("z0", L, 0), both, h_wait)
                    product(("z0", L, 1), ("z0", L, 1), both)
                    product(("z0", L, 2), ("z0", L, 2), both, n=1)
                    product(("kr", L), ("kr", L, 0), both, n=1)
                    product(("gqk", L), ("gqk", L, 0), both)
                    for n, tiles in enumerate(((0, 1, 2), (3, 4))):
                        sums(("c", L, n), tiles, k("ones"), raw, lambda t: pe.wait_ge(*due("csq", L, t // 2)))
                    product(("rqk", L), ("rqk", L, 0), both)
                    product(("glr", L), ("glr", L, 0), both, n=1)
                    product(("gate", L, 0), ("gg", L, 0), both)
                    product(("gate", L, 1), ("rg", L, 0), both)
                    for tb in range(2):
                        take(("vgr", L, tb))
                    for u, unit in enumerate(("gv", "rv")):
                        for tb in range(2):
                            token_product(("vgr", L, tb), (unit, L, 0), both, tb, 0, 256, 256 * u, u == 1, range(KT))
                    pe.wait_ge(*due("gatew_in", 0))
                    pe.wait_ge(*due("glr_in", L))
                    b = take(("ggate", L))
                    nc.tensor.matmul(b[:, 0:256], gatew[:, L - 2, :], glr, start=True, stop=True).then_inc(*sig("ggate", L))
                    pe.wait_ge(*due("kr_raw", L))
                    b = take(("kr_rot", L))
                    nc.tensor.matmul(b[:, 0:256], k("rot64"), qh[:, 6, :], start=True, stop=True).then_inc(*sig("kr_rot", L))
                    pe.wait_ge(*due("rqk_raw", L))
                    b = take(("rqk_rot", L))
                    nc.tensor.matmul(b[:, :], k("rot32"), gr[:, 512:1024], start=True, stop=True).then_inc(*sig("rqk_rot", L))
                    cn = (cn_hi, cn_lo)
                    product(("qr", L), ("uq", L, 0), cn, lambda t: pe.wait_ge(*due("cn_lo", L, t)), c0=512)
                    product(("qn", L, 0), ("uq", L, 0), cn, c0=0)
                    product(("qn", L, 1), ("uq", L, 0), cn, c0=256)
                    ckv = tuple(v_[:, 3:5, :] for v_ in cn)
                    product(("kn", L, 0), ("ukv", L, 0), ckv, lambda t: pe.wait_ge(*due("cn_lo", L, 3 + t)), c0=0)
                    product(("kn", L, 1), ("ukv", L, 0), ckv, c0=256)
                    for tb in range(2):
                        take(("vm", L, tb))
                        token_product(("vm", L, tb), ("ukv", L, 0), ckv, tb, 512, 512, 0, True, range(2))
                    pe.wait_ge(*due("qr_raw", L))
                    b = take(("qr_rot", L))
                    nc.tensor.matmul(b[:, :], k("rot64"), qh[:, 4:6, :], start=True, stop=True).then_inc(*sig("qr_rot", L))
                    pe.wait_ge(*due("rkbd", L))
                    for hd in range(4):
                        job = ("rscore", L, hd)
                        b = take(job)
                        group(b[:, 0:256], [(kbd[:, hd, 0:P], rq)])
                        group(b[:, 256:384], [(kbd[:, hd, P:2 * P], rq[:, P:2 * P])]).then_inc(*sig(*job))
                    pe.wait_ge(*due("kn_in", L, 1))
                    pe.wait_ge(*due("qn_in", L, 1))
                    pe.wait_ge(*due("qr_in", L))
                    pe.wait_ge(*due("kr2", L))
                    for n in range(3):
                        job = ("score", L, n)
                        b = take(job)
                        for i in range(2 if n < 2 else 4):
                            hd = 2 * n + i if n < 2 else i
                            qs, ks, o = (slice(P, 2 * P), slice(0, 256), half(b, i)) if n < 2 else (slice(0, P), slice(0, P), b[:, P * i:P * (i + 1)])
                            last = group(o, [(qh[:, hd, qs], kn[:, hd, ks]), (qh[:, 4 + hd // 2, qs], kr2[:, hd % 2, ks])])
                        last.then_inc(*sig(*job))
                    pe.wait_ge(*due("vgr_in", L, 1))
                    job = ("rout", L)
                    b = take(job)
                    for hd in range(4):
                        pe.wait_ge(*due("ratt", L, hd))
                        o = b[64 * (hd % 2):64 * (hd % 2) + 64, 256 * (hd // 2):256 * (hd // 2) + 256]
                        val = lambda jb: vgr[:, jb, 256 + 64 * hd:256 + 64 * hd + 64]
                        nc.tensor.matmul(o, val(0), attT[:, hd, 0:256], start=True, stop=False)
                        last = nc.tensor.matmul(o[:, P:2 * P], val(1), attT[:, hd, 256:384], start=False, stop=True)
                    last.then_inc(*sig(*job))
                    pe.wait_ge(*due("gkbd", L))
                    for hd in range(4):
                        job = ("gscore", L, hd)
                        b = take(job)
                        for J in range(4):
                            o = b[64 * (J % 2):64 * (J % 2) + 64, 0:256] if J < 2 else b[64 * (J % 2):64 * (J % 2) + 64, 256:384]
                            last = group(o, [(kbd[:, hd, 64 * J:64 * J + 64], expq[:, J, P * (J // 2):])])
                        last.then_inc(*sig(*job))
                    for n in range(3):
                        pe.wait_ge(*due("prob", L, n))
                        transposes(("probT", L, n), [prob2[:, n % 2, P * i:P * (i + 1)] for i in range(4)])
                    job = ("gout", L)
                    b = take(job)
                    for hd in range(4):
                        pe.wait_ge(*due("gatt", L, hd))
                        o = b[64 * (hd % 2):64 * (hd % 2) + 64, 256 * (hd // 2):256 * (hd // 2) + 256]
                        val = lambda jb: vgr[:, jb, 64 * hd:64 * hd + 64]
                        nc.tensor.matmul(o, val(0), attT[:, hd, 0:256], start=True, stop=False)
                        last = nc.tensor.matmul(o[:, P:2 * P], val(1), attT[:, hd, 256:384], start=False, stop=True)
                    last.then_inc(*sig(*job))
                    pe.wait_ge(*due("vm_in", L, 1))
                    for n in range(2):
                        job = ("attn", L, n)
                        b = take(job)
                        for m in (n, 2):
                            pe.wait_ge(*due("probT_in", L, m))
                        for i in range(2):
                            hd = 2 * n + i
                            val = lambda kb: vm[:, kb, P * hd:P * (hd + 1)]
                            t1 = probT2[:, n, 256 * i:256 * (i + 1)]
                            t0 = probT2[:, 2, P * hd:P * (hd + 1)]
                            group(half(b, i)[:, 0:P], [(val(0), t0)])
                            last = group(half(b, i)[:, P:2 * P], [(val(0), t1[:, 0:P]), (val(1), t1[:, P:2 * P])])
                        last.then_inc(*sig(*job))
                    for m, (n, ones) in enumerate(((3, "ones64"), (2, "ones64"), (0, "ones"), (1, "ones"))):
                        pe.wait_ge(*due("hsq", L, n))
                        b = take(("hsum", L, n))
                        nc.tensor.matmul(b[:, :], k(ones), head_sq[:, m % 2, :], start=True, stop=True).then_inc(*sig("hsum", L, n))

                def summed(N, jobs):
                    job = ("sums", *N)
                    for p_ in range(4):
                        jobs(p_)
                        if p_ == 1:
                            b = take(job)
                        if p_ >= 1:
                            square_sums(N, b, p_ - 1)
                    square_sums(N, b, 3).then_inc(*sig(*job))

                def square_sums(N, b, p_):
                    pe.wait_ge(*due("squared", N, p_))
                    for t in (2 * p_, 2 * p_ + 1):
                        done = nc.tensor.matmul(b[:, 0:256], k("ones"), raw[:, t, :], start=(t == 0), stop=(t == KT - 1))
                    return done

                cat_wait = lambda t: pe.wait_ge(*due("cat_lo", L, t))
                summed(("post_mix" if L < 2 else "ffn", L),
                       lambda p_: product(("y", L, 0, p_), ("wo", L, p_), both, cat_wait if p_ == 0 else None))
                if L < 2:
                    norm_sums(("ffn", L))
                for f in range(FT):
                    product(("gu", L, f), ("gu", L, f), both, (lambda t: pe.wait_ge(*due("in_lo", ("ffn", L), t))) if f == 0 else None)

                def down(p_):
                    hid = (hid_hi, hid_lo)
                    product(("y", L, 1, p_), ("wd", L, 2 * p_), hid, (lambda t: pe.wait_ge(*due("hid_lo", L, t))) if p_ == 0 else None,
                            n=1, last=False)
                    product(("y", L, 1, p_), ("wd", L, 2 * p_ + 1), hid, n=1, at=1, first=False)

                summed(("post_ffn", L) if L < 2 else ("mix", L + 1) if L + 1 < NL else ("final", 0), down)
                if L < 2:
                    norm_sums(("mix", L + 1))

        @block.sync
        def _(sp):
            off = 0
            for n, (unit, kt, cols) in enumerate(UNITS):
                if n >= NRAW:
                    old = UNITS[n - NRAW][0]
                    sp.wait_ge(*due(*(("ada_sum", old) if old[0] == "ada" else ("lo_w", old, 1))))
                sp.dma_start(raw_view(unit), a_w[off:off + P * kt * cols].rearrange("(p w) -> p w", p=P)).then_inc(
                    *sig(f"raw_w{n % NRAW}", unit, by=16))
                off += P * kt * cols
            sp.wait_ge(*due("out_ready", 3))
            sp.dma_start(out, raw[:, :, :]).then_inc(*sig("stored", 0, by=16))
            sp.wait_ge(*due("stored", 0))

        @block.gpsimd
        def _(pool):
            pool.dma_start(bias_vu[:, :, :], a_bias.rearrange("(o l) n -> o l n", o=1).to_broadcast([P, 2, 640])).then_inc(*sig("bias_in", 0, by=16))
            pool.dma_start(sinks[:, :, :], a_sinks.rearrange("(o l) n -> o l n", o=1).to_broadcast([P, 2, HEADS])).then_inc(*sig("sinks_in", 0, by=16))
            pool.dma_start(poolw[:, :, :, :], a_poolw.rearrange("l g c d -> c l g d")).then_inc(*sig("poolw_in", 0, by=16))
            pool.dma_start(gatew[:, :, :], a_gatew.rearrange("l g n -> g l n")).then_inc(*sig("gatew_in", 0, by=16))

        @block.scalar
        def _(sc):
            sc.dma_start(vrow[:, :], a_vec).then_inc(*sig("vec_in", 0, by=16))
            sc.dma_start(const[:, :], a_const).then_inc(*sig("const_in", 0, by=16))
            sc.dma_start(x[:, :, :], a_x).then_inc(*sig("x_in", 0, by=16))
            sc.dma_start(pos_i[:, :], a_pos.to_broadcast([P, S])).then_inc(*sig("pos_in", 0, by=16))
            sc.preload_act_table_set("trig_and_small")
            sc.wait_ge(*due("turns", 1))
            nc.scalar.activation(rope1[:, :, :], turns[:, :, :], ACT.Sin).then_inc(*sig("rope1", 0))
            sc.wait_ge(*due("vcol", 0))
            nc.scalar.activation(c_act[:, :], v("c", 0, 8), ACT.Silu).then_inc(*sig("c_act", 0))
            splits = [0]

            def prepare(n=1):
                for unit in SPLITS[splits[0]:splits[0] + n]:
                    m = splits[0]
                    splits[0] += 1
                    sc.wait_ge(*due(f"raw_w{UNIT_NO[unit] % NRAW}", unit))
                    if m >= NSPLIT:
                        sc.wait_ge(*due(*counts.last_use.get(SPLITS[m - NSPLIT], ("none",))))
                    for i, cut in enumerate(halves(unit)):
                        nc.scalar.activation(hi_w[:, m % NSPLIT, cut], raw_view(unit)[:, cut], ACT.Identity).then_inc(*sig("hi_w", unit, i))

            def square(N, p_, src_due):
                sc.wait_ge(*src_due)
                if N[0] in ("post_mix", "post_ffn"):
                    src = ps(("y", N[1], 0 if N[0] == "post_mix" else 1, p_))[:, :]
                    dst = raw[:, 2 * p_:2 * p_ + 2, :].rearrange("p t s -> p (t s)")
                else:
                    src, dst = x[:, 2 * p_:2 * p_ + 2, :], raw[:, 2 * p_:2 * p_ + 2, :]
                nc.scalar.activation(dst, src, ACT.Square).then_inc(*sig("squared", N, p_))

            def root(job, name, key, scale, width, dst):
                sc.wait_ge(*due(*job))
                nc.scalar.activation(dst, ps(job)[:, 0:width], ACT.Ln, bias=k("eps"), scale=scale).then_inc(*sig("mean_log", job, frees=job))
                sc.wait_ge(*due("mean_log", job))
                nc.scalar.activation(dst, dst, ACT.Exp, scale=-0.5).then_inc(*sig(name, *key))

            def norm(N, src_due, before=(0, 0, 0, 0), after=(0, 0, 0, 0)):
                for p_ in range(4):
                    prepare(before[p_])
                    square(N, p_, src_due(p_))
                    if p_ == 3:
                        root(("sums", *N), "rstd", (N,), 1.0 / D, 256, rstd[:, 0, 0:256])
                    prepare(after[p_])

            def round_in(N, shift=None):
                for t in range(KT):
                    sc.wait_ge(*due("scaled", N, t))
                    kw = {} if shift is None else {"bias": shift[:, t:t + 1]}
                    nc.scalar.activation(in_hi[:, t, :], raw[:, t, :], ACT.Identity, **kw).then_inc(*sig("in_hi", N, t))

            def round_cat(L, tiles):
                for t in tiles:
                    sc.wait_ge(*due("cat_raw", L, t))
                    nc.scalar.activation(in_hi[:, t, :], raw[:, t, :], ACT.Identity).then_inc(*sig("cat_hi", L, t))

            def copy(job, dst, src, name, *key, **kw):
                sc.wait_ge(*due(*job))
                return nc.scalar.activation(dst, src, ACT.Identity, **kw).then_inc(*sig(name, *key, frees=job))

            def head_root(L, m, n):
                if m >= 2:
                    sc.wait_ge(*due("cat_raw", L, 2 * (3, 2, 0, 1)[m - 2] + 1))
                root(("hsum", L, n), "h_rstd", (L, n), 1.0 / (64 if n >= 2 else 128), 512, rstd[:, m % 2, :])

            sc.preload_act_table_set("natural_log_exp_and_others")
            for L in range(NL):
                l = L % 2
                if L == 0:
                    norm(("mix", L), lambda p_: due("x_in", 0), after=(0, 0, 0, 2))
                if L < 2:
                    round_in(("mix", L), mods[:, L, 0:8])
                    for i in range(3):
                        for j in range(2 if i < 2 else 1):
                            sc.wait_ge(*due("qk", L, i))
                            last = nc.scalar.activation(qk[:, 2 * i + j, :], ps(("qk", L, i))[:, 256 * j:256 * (j + 1)], ACT.Identity,
                                                        bias=v(f"b_qk{l}", 2 * i + j))
                        last.then_inc(*sig("qk_raw", L, i, frees=("qk", L, i)))
                        prepare()
                    prepare()
                    for i in range(2):
                        copy(("pool", L, i), pooled[:, 2 * i:2 * i + 2, :].rearrange("p t s -> p (t s)"), ps(("pool", L, i))[:, :], "pooled", L, i)
                    prepare(2)
                    for n in range(6):
                        nh = 2 if n < 4 else 4
                        w = 257 if n < 4 else 129
                        sc.wait_ge(*due("smax", L, n))
                        for i in range(nh):
                            last = nc.scalar.activation(prob[:, n % 3, w * i:w * i + w], prob[:, n % 3, w * i:w * i + w], ACT.Exp,
                                                        bias=smax[:, n % 3, i:i + 1], accum_out=ssum[:, n % 3, i:i + 1])
                        last.then_inc(*sig("exp", L, n))
                        if n >= 1:
                            copy(("probT", L, n - 1), probT[:, n - 1, :], ps(("probT", L, n - 1))[:, :], "probT_in", L, n - 1)
                    copy(("probT", L, 5), probT[:, 5, :], ps(("probT", L, 5))[:, :], "probT_in", L, 5)
                    for jp in range(2):
                        sc.wait_ge(*due("attn", L, jp))
                        nc.scalar.activation(in_hi[:, 2 * jp:2 * jp + 2, :], ps(("attn", L, jp))[:, :], ACT.Identity).then_inc(*sig("attn_hi", L, jp))
                    for t in range(4, 8):
                        sc.wait_ge(*due("cat_raw", L, t))
                        nc.scalar.activation(in_hi[:, t, :], raw[:, t, :], ACT.Identity).then_inc(*sig("cat_hi", L, t))
                else:
                    round_in(("mix", L))
                    for i in range(3):
                        n = 2 if i < 2 else 1
                        copy(("z0", L, i), cqkv[:, 2 * i:2 * i + n, :].rearrange("p t s -> p (t s)"), ps(("z0", L, i))[:, 0:256 * n], "c_raw", L, i)
                        prepare()
                    copy(("kr", L), qh[:, 6, :], ps(("kr", L))[:, 0:256], "kr_raw", L)
                    prepare()
                    sc.wait_ge(*due("gqk", L))
                    nc.scalar.activation(gq, ps(("gqk", L))[:, 0:256], ACT.Identity, scale=32.0 ** -0.5)
                    nc.scalar.activation(gk, ps(("gqk", L))[:, 256:512], ACT.Identity).then_inc(*sig("gqk_raw", L, frees=("gqk", L)))
                    prepare()
                    root(("sums", "c", L, 0), "c_rstd", (L, 0), 1.0 / 384, 256, rstd[:, 1, 0:256])
                    root(("sums", "c", L, 1), "c_rstd", (L, 1), 1.0 / 256, 256, rstd[:, 1, 256:512])
                    copy(("rqk", L), gr[:, 512:1024], ps(("rqk", L))[:, :], "rqk_raw", L)
                    prepare()
                    copy(("glr", L), glr, ps(("glr", L))[0:16, 0:256], "glr_in", L)
                    prepare()
                    for n in range(2):
                        for t in ((0, 1, 2), (3, 4))[n]:
                            sc.wait_ge(*due("cn_raw", L, t))
                            nc.scalar.activation(cn_hi[:, t, :], cqkv[:, t, :], ACT.Identity).then_inc(*sig("cn_hi", L, t))
                    for i in range(2):
                        sc.wait_ge(*due("gate", L, i))
                        nc.scalar.activation(gates[:, 2 * i:2 * i + 2, :].rearrange("p t s -> p (t s)"), ps(("gate", L, i))[:, :], ACT.Silu).then_inc(
                            *sig("gates", L, i, frees=("gate", L, i)))
                        prepare()
                    prepare()
                    sc.preload_act_table_set("natural_log_exp_and_others")
                    for tb in range(2):
                        copy(("vgr", L, tb), vgr[:, tb, :], ps(("vgr", L, tb))[:, :], "vgr_in", L, tb)
                    prepare()
                    sc.wait_ge(*due("ggate_in", L))
                    nc.scalar.activation(expk, lsum, ACT.Abs).then_inc(*sig("lsig", L, 0))
                    sc.wait_ge(*due("lsig", L, 0))
                    nc.scalar.activation(expk, expk, ACT.Exp, scale=-1.0).then_inc(*sig("lsig", L, 1))
                    sc.wait_ge(*due("lsig", L, 1))
                    nc.scalar.activation(expk, expk, ACT.Ln, bias=1.0).then_inc(*sig("lsig", L, 2))
                    copy(("qr", L), qh[:, 4:6, :].rearrange("p t s -> p (t s)"), ps(("qr", L))[:, :], "qr_raw", L)
                    for i in range(2):
                        copy(("qn", L, i), qh[:, 2 * i:2 * i + 2, :].rearrange("p t s -> p (t s)"), ps(("qn", L, i))[:, :], "qn_in", L, i)
                    for i in range(2):
                        copy(("kn", L, i), kn[:, 2 * i:2 * i + 2, :].rearrange("p t s -> p (t s)"), ps(("kn", L, i))[:, :], "kn_in", L, i)
                    for tb in range(2):
                        copy(("vm", L, tb), vm[:, tb, :], ps(("vm", L, tb))[:, :], "vm_in", L, tb)
                    prepare(2)
                    sc.wait_ge(*due("gmid", L))
                    for J in range(4):
                        nc.scalar.activation(expq[:, J, 64 * J:256], lsum[:, 64 * J:256], ACT.Exp, bias=mid[:, 4 + J:5 + J], scale=1.0 / 16)
                        last = nc.scalar.activation(expk[:, 64 * J:64 * J + 64], lsum[:, 64 * J:64 * J + 64], ACT.Exp, bias=mid[:, J:J + 1], scale=-1.0 / 16)
                    last.then_inc(*sig("gexp", L))
                    for n in range(3):
                        nh, w = (2, 256) if n < 2 else (4, 128)
                        sc.wait_ge(*due("smax", L, n))
                        for i in range(nh):
                            last = nc.scalar.activation(prob2[:, n % 2, w * i:w * (i + 1)], prob2[:, n % 2, w * i:w * (i + 1)], ACT.Exp,
                                                        bias=smax[:, n % 2, i:i + 1], accum_out=ssum[:, n % 2, i:i + 1])
                        last.then_inc(*sig("exp", L, n))
                        if n == 2:
                            copy(("probT", L, 0), probT2[:, 0, :], ps(("probT", L, 0))[:, :], "probT_in", L, 0)
                    copy(("rout", L), raw[:, 6:8, :].rearrange("p t s -> p (t s)"), ps(("rout", L))[:, :], "o_in", L, 3)
                    for n in range(1, 3):
                        copy(("probT", L, n), probT2[:, n, :], ps(("probT", L, n))[:, :], "probT_in", L, n)
                    copy(("gout", L), raw[:, 4:6, :].rearrange("p t s -> p (t s)"), ps(("gout", L))[:, :], "o_in", L, 2)
                    for n in range(2):
                        copy(("attn", L, n), raw[:, 2 * n:2 * n + 2, :].rearrange("p t s -> p (t s)"), ps(("attn", L, n))[:, :], "o_in", L, n)
                    order = (3, 2, 0, 1)
                    for m, n in enumerate(order):
                        sc.wait_ge(*due("o_in", L, n))
                        if m >= 2:
                            sc.wait_ge(*due("hsum", L, order[m - 2]))
                        nc.scalar.activation(head_sq[:, m % 2, :], raw[:, 2 * n:2 * n + 2, :], ACT.Square).then_inc(*sig("hsq", L, n))
                        if m >= 1:
                            head_root(L, m - 1, order[m - 1])
                            round_cat(L, (2 * order[m - 2], 2 * order[m - 2] + 1) if m >= 2 else ())
                    head_root(L, 3, 1)
                    round_cat(L, (0, 1))
                    round_cat(L, (2, 3))
                if L < 2:
                    norm(("post_mix", L), lambda p_: due("y", L, 0, p_), after=(1, 1, 1, 0))
                    norm(("ffn", L), lambda p_: due("x", L, 0, p_), after=(0, 0, 0, 1))
                    round_in(("ffn", L), mods[:, L, 24:32])
                else:
                    norm(("ffn", L), lambda p_: due("x", L, 0, p_), after=(1, 1, 1, 1))
                    round_in(("ffn", L))
                sc.preload_act_table_set("silu_and_others")
                lag = 1 if L < 2 else 2
                for f in range(1, FT + lag + 2):
                    if L >= 2 and f - 1 < FT:
                        g = f - 1
                        sc.wait_ge(*due("gu", L, g))
                        if g >= 2:
                            sc.wait_ge(*due("silu", L, g - 2))
                        nc.scalar.activation(conv[:, g % 2, :], ps(("gu", L, g))[:, 0:256], ACT.Identity, bias=v(f"conv_b{l}", g),
                                             scale=v(f"conv_w{l}", 44 + g)).then_inc(*sig("conv0", L, g))
                    g = f - lag
                    if 0 <= g < FT:
                        sc.wait_ge(*due(*(("gu", L, g) if L < 2 else ("conv", L, g))))
                        if g >= 2:
                            sc.wait_ge(*due("hidden", L, g - 2))
                        src = ps(("gu", L, g))[:, 0:256] if L < 2 else conv[:, g % 2, :]
                        nc.scalar.activation(silu[:, g % 2, :], src, ACT.Silu).then_inc(*sig("silu", L, g))
                    g = f - lag - 1
                    if 0 <= g < FT:
                        sc.wait_ge(*due("hidden", L, g))
                        nc.scalar.activation(hid_hi[:, g, :], hidden[:, g % 2, :], ACT.Identity).then_inc(*sig("hid_hi", L, g))
                    if f <= FT:
                        prepare()
                sc.preload_act_table_set("natural_log_exp_and_others")
                N, src = (("post_ffn", L), (lambda p_: due("y", L, 1, p_))) if L < 2 else \
                    (("mix", L + 1) if L + 1 < NL else ("final", 0), lambda p_: due("x", L, 1, p_))
                norm(N, src, before=(1, 1, 1, 1), after=(1, 1, 1, 1))
                if L < 2:
                    norm(("mix", L + 1), lambda p_: due("x", L, 1, p_))

        @block.vector
        def _(ve):
            steps = [0]

            def step(ins):
                steps[0] += 1
                ins.then_inc(*sig("ve_step", steps[0]))
                ve.wait_ge(*due("ve_step", steps[0]))

            flat = lambda ap: ap.rearrange("p t s -> p (t s)")
            splits = [0]
            ada_todo, ada_pending = ada_groups(0), []

            def prepare(n=1, ada=True):
                for unit in SPLITS[splits[0]:splits[0] + n]:
                    m = splits[0]
                    splits[0] += 1
                    for i, cut in enumerate(halves(unit)):
                        ve.wait_ge(*due("hi_w", unit, i))
                        nc.vector.tensor_tensor(lo_w[:, m % NSPLIT, cut], raw_view(unit)[:, cut], hi_w[:, m % NSPLIT, cut].bitcast(F32),
                                                ALU.subtract).then_inc(*sig("lo_w", unit, i))
                    ada_todo.extend(ada_groups(UNIT_NO[unit] + 1))
                    if ada:
                        ada_work()

            def ada_work():
                while ada_todo:
                    units = ada_todo.pop(0)
                    while len(ada_pending) >= 2:
                        ada_finish()
                    for unit in units:
                        acc = ada_sum[:, unit[2] % 4, :]
                        ve.wait_ge(*due(f"raw_w{UNIT_NO[unit] % NRAW}", unit))
                        w = raw_view(unit).rearrange("p (t c) -> p t c", t=KT)
                        step(nc.vector.tensor_scalar(acc, w[:, 0, :], c_act[:, 0:1], None, ALU.mult))
                        for t in range(1, KT - 1):
                            step(nc.vector.scalar_tensor_tensor(acc, w[:, t, :], c_act[:, t:t + 1], acc, ALU.mult, ALU.add))
                        nc.vector.scalar_tensor_tensor(acc, w[:, KT - 1, :], c_act[:, KT - 1:KT], acc, ALU.mult, ALU.add).then_inc(
                            *sig("ada_sum", unit))
                    ada_pending.append((splits[0], units))
                ada_drain(2)

            def ada_drain(behind):
                while ada_pending and ada_pending[0][0] + behind <= splits[0]:
                    ada_finish()

            def ada_finish():
                _, units = ada_pending.pop(0)
                _, l, n = units[0]
                job, w = ("ada", units[-1]), 2 * len(units)
                ve.wait_ge(*due(*job))
                nc.vector.tensor_tensor(mods[:, l, 2 * n:2 * n + w], ps(job)[:, 0:w], v(f"ada_b{l}", 2 * n, w), ALU.add).then_inc(
                    *sig("mods", units[-1], frees=job))

            def ready_mods(L, n):
                while ada_pending and ada_pending[0][1][-1] <= ("ada", L, n):
                    ada_finish()
                ve.wait_ge(*due("mods", ("ada", L, n)))

            def apply(N, g, shift=None):
                ve.wait_ge(*due("rstd", N))
                for t in range(KT + 2):
                    if t < KT:
                        nc.vector.scalar_tensor_tensor(raw[:, t, :], x[:, t, :], g(t), rstd[:, 0, 0:256], ALU.mult, ALU.mult).then_inc(
                            *sig("scaled", N, t))
                    if t >= 2:
                        u = t - 2
                        ve.wait_ge(*due("in_hi", N, u))
                        hi = in_hi[:, u, :].bitcast(F32)
                        if shift is None:
                            ins = nc.vector.tensor_tensor(in_lo[:, u, :], raw[:, u, :], hi, ALU.subtract)
                        else:
                            ins = nc.vector.scalar_tensor_tensor(in_lo[:, u, :], raw[:, u, :], shift[:, u:u + 1], hi, ALU.add, ALU.subtract)
                        ins.then_inc(*sig("in_lo", N, u))

            def cat_lo(L, tiles):
                for t in tiles:
                    ve.wait_ge(*due("cat_hi", L, t))
                    nc.vector.tensor_tensor(in_lo[:, t, :], raw[:, t, :], in_hi[:, t, :].bitcast(F32), ALU.subtract).then_inc(
                        *sig("cat_lo", L, t))

            def add_residual(L, which, p_):
                ve.wait_ge(*due("y", L, which, p_))
                xs = flat(x[:, 2 * p_:2 * p_ + 2, :])
                nc.vector.tensor_tensor(xs, xs, ps(("y", L, which, p_))[:, :], ALU.add).then_inc(
                    *sig("x", L, which, p_, frees=("y", L, which, p_)))

            def update_post(L, which, gain):
                N = ("post_mix" if which == 0 else "post_ffn", L)
                ve.wait_ge(*due("rstd", N))
                for p_ in range(4):
                    for j in range(2):
                        t = 2 * p_ + j
                        step(nc.vector.scalar_tensor_tensor(tmp[:, 0:256], ps(("y", L, which, p_))[:, 256 * j:256 * (j + 1)],
                                                            gains[:, L, gain, t:t + 1], rstd[:, 0, 0:256], ALU.mult, ALU.mult))
                        last = nc.vector.tensor_tensor(x[:, t, :], x[:, t, :], tmp[:, 0:256], ALU.add)
                        if j == 0:
                            step(last)
                    last.then_inc(*sig("x", L, which, p_, frees=("y", L, which, p_)))
                    ve.wait_ge(*due("x", L, which, p_))

            def softmax(L, n, nh, w, w1, scale, mask, buf, sink, bufs):
                job = ("score", L, n)
                ve.wait_ge(*due(*job))
                if n >= bufs:
                    ve.wait_ge(*due("probT", L, n - bufs))
                pr = buf[:, n % bufs, 0:nh * w1].rearrange("p (h k) -> p h k", h=nh)
                if sink is not None:
                    nc.vector.tensor_copy(pr[:, :, w], sink)
                nc.vector.scalar_tensor_tensor(pr[:, :, 0:w], ps(job)[:, 0:nh * w].rearrange("p (h k) -> p h k", h=nh), scale,
                                               bcast(mask, nh), ALU.mult, ALU.add).then_inc(*sig("scored", L, n, frees=job))
                ve.wait_ge(*due("scored", L, n))
                step(nc.vector.tensor_reduce(smax[:, n % bufs, 0:nh], pr, AX_X, ALU.max))
                nc.vector.tensor_scalar(smax[:, n % bufs, 0:nh], smax[:, n % bufs, 0:nh], -1.0, None, ALU.mult).then_inc(*sig("smax", L, n))

            def normalize(L, n, nh, w, w1, buf, bufs):
                ve.wait_ge(*due("exp", L, n))
                step(nc.vector.reciprocal(ssum[:, n % bufs, 0:nh], ssum[:, n % bufs, 0:nh]))
                pr = buf[:, n % bufs, 0:nh * w1].rearrange("p (h k) -> p h k", h=nh)
                nc.vector.tensor_tensor(pr[:, :, 0:w], pr[:, :, 0:w], ssum[:, n % bufs, 0:nh].rearrange("p (h o) -> p h o", o=1).to_broadcast([P, nh, w]),
                                        ALU.mult).then_inc(*sig("prob", L, n))

            def rotate(q, rot, cos, sin, n, name, *key, frees):
                w = 256 * n
                r3 = q.rearrange("p (t s) -> p t s", t=n)
                step(nc.vector.tensor_tensor(tmp[:, 0:w].rearrange("p (t s) -> p t s", t=n), rot.rearrange("p (t s) -> p t s", t=n),
                                             bcast(sin, n), ALU.mult))
                step(nc.vector.tensor_tensor(r3, r3, bcast(cos, n), ALU.mult))
                nc.vector.tensor_tensor(q, q, tmp[:, 0:w], ALU.add).then_inc(*sig(name, *key, frees=frees))
                ve.wait_ge(*due(name, *key))

            magic, two_pi = 12582912.0, 6.283185307179586
            parts = (6.28125, 0.0019350051879882812, 3.019915982e-07)
            ve.wait_ge(*due("pos_in", 0))
            ve.wait_ge(*due("const_in", 0))
            step(nc.vector.tensor_copy(ang[:, :], pos_i[:, :]))
            step(nc.vector.tensor_scalar(ang[:, :], ang[:, :], k("freq"), None, ALU.mult))
            for i, quarter in ((0, 0.25), (1, 0.0)):
                step(nc.vector.tensor_scalar(tmp[:, 0:256], ang[:, :], 1.0 / two_pi, quarter, ALU.mult, ALU.add))
                step(nc.vector.tensor_scalar(tmp[:, 0:256], tmp[:, 0:256], magic, None, ALU.add))
                step(nc.vector.tensor_scalar(tmp[:, 0:256], tmp[:, 0:256], magic, None, ALU.subtract))
                step(nc.vector.scalar_tensor_tensor(turns[:, i, :], tmp[:, 0:256], -parts[0], ang[:, :], ALU.mult, ALU.add))
                for c in parts[1:]:
                    step(nc.vector.scalar_tensor_tensor(turns[:, i, :], tmp[:, 0:256], -c, turns[:, i, :], ALU.mult, ALU.add))
                step(nc.vector.tensor_scalar(turns[:, i, :], turns[:, i, :], quarter * two_pi, -3.1415925, ALU.add, ALU.max))
                nc.vector.tensor_scalar(turns[:, i, :], turns[:, i, :], 3.1415925, None, ALU.min).then_inc(*sig("turns", i))
            ve.wait_ge(*due("vec"))
            nc.vector.tensor_copy(vcol[:, :], ps(("vec",))[:, 0:NVEC * P]).then_inc(*sig("vcol", 0, frees=("vec",)))
            ve.wait_ge(*due("vcol", 0))

            def gain(L, which):
                n, col, g, op = ((7, 8, "g_pre_mix", None), (11, 16, "g_post_mix", ALU.mult), (19, 32, "g_pre_ffn", None),
                                 (23, 40, "g_post_ffn", ALU.mult))[which]
                ready_mods(L, n)
                m, o, w = mods[:, L, col:col + 8], gains[:, L, which, :], v(f"{g}{L}", 0, 8)
                if op is None:
                    step(nc.vector.scalar_tensor_tensor(o, m, 1.0, w, ALU.add, ALU.mult))
                else:
                    step(nc.vector.tensor_tensor(o, m, w, op))

            ve.wait_ge(*due("c_act", 0))
            ada_work()
            for L in range(NL):
                l = L % 2
                if L == 0:
                    prepare(2)
                if L < 2:
                    gain(L, 0)
                    if L == 0:
                        ve.wait_ge(*due("x_in", 0))
                    apply(("mix", L), lambda t: gains[:, L, 0, t:t + 1], mods[:, L, 0:8])
                    prepare(3)
                    ve.wait_ge(*due("bias_in", 0))
                    ve.wait_ge(*due("val", L))
                    nc.vector.tensor_tensor(tok[:, :, 0:128], ps(("val", L))[:, 0:256].rearrange("p (b n) -> p b n", b=2),
                                            bcast(bias_vu[:, l, 0:128], 2), ALU.add).then_inc(*sig("tok", L, 0, frees=("val", L)))
                    prepare()
                    for tb in range(2):
                        ve.wait_ge(*due("stream", L, tb))
                        nc.vector.tensor_tensor(tok[:, tb, 128:640], ps(("stream", L, tb))[:, :], bias_vu[:, l, 128:640],
                                                ALU.add).then_inc(*sig("tok", L, 1 + tb, frees=("stream", L, tb)))
                    ada_drain(1)
                    if L == 0:
                        ve.wait_ge(*due("rope1", 0))
                    for i in range(3):
                        n = 2 if i < 2 else 1
                        ve.wait_ge(*due("qk_rot", L, i))
                        rotate(flat(qk[:, 2 * i:2 * i + n, :]), ps(("qk_rot", L, i))[:, 0:256 * n], rope1[:, 0, :], rope1[:, 1, :], n,
                               "qk_done", L, i, frees=("qk_rot", L, i))
                    ve.wait_ge(*due("sinks_in", 0))
                    for n in range(7):
                        if n < 6:
                            if n < 4:
                                g, jp = n // 2, n % 2
                                softmax(L, n, 2, 256, 257, 0.125, k("window"), prob, sinks[:, l, 4 * g + 2 * jp:4 * g + 2 * jp + 2], 3)
                            else:
                                softmax(L, n, 4, 128, 129, 0.125, k("causal2", P, 2 * P), prob, sinks[:, l, 4 * (n - 4):4 * (n - 4) + 4], 3)
                        if n == 0:
                            prepare(1)
                        if n == 1:
                            for i in range(2):
                                ve.wait_ge(*due("poolw", L, i))
                                for g in range(2):
                                    t = 4 + 2 * i + g
                                    nc.vector.tensor_scalar(raw[:, t, :], ps(("poolw", L, i))[:, 256 * g:256 * (g + 1)],
                                                            v(f"pool_scale{l}", 2 * i + g), None, ALU.mult).then_inc(
                                        *sig("cat_raw", L, t, frees=("poolw", L, i)))
                        if n >= 1:
                            m = n - 1
                            normalize(L, m, *((2, 256, 257) if m < 4 else (4, 128, 129)), prob, 3)
                    prepare(1)
                    for jp in range(2):
                        ve.wait_ge(*due("attn_hi", L, jp))
                        for j in range(2):
                            t = 2 * jp + j
                            nc.vector.tensor_tensor(in_lo[:, t, :], ps(("attn", L, jp))[:, 256 * j:256 * (j + 1)], in_hi[:, t, :].bitcast(F32),
                                                    ALU.subtract).then_inc(*sig("cat_lo", L, t, frees=("attn", L, jp)))
                    cat_lo(L, range(4, 8))
                    prepare()
                    prepare(2, ada=False)
                    gain(L, 1)
                    update_post(L, 0, 1)
                    ada_work()
                    prepare()
                    gain(L, 2)
                    apply(("ffn", L), lambda t: gains[:, L, 2, t:t + 1], mods[:, L, 24:32])
                else:
                    apply(("mix", L), lambda t: v(f"attn_norm{l}", t))
                    for i in range(3):
                        n = 2 if i < 2 else 1
                        ve.wait_ge(*due("c_raw", L, i))
                        c = cqkv[:, 2 * i:2 * i + n, :]
                        nc.vector.tensor_tensor(raw[:, 2 * i:2 * i + n, :], c, c, ALU.mult).then_inc(*sig("csq", L, i))
                        prepare()
                    prepare(2)
                    for n, tiles in enumerate(((0, 1, 2), (3, 4))):
                        ve.wait_ge(*due("c_rstd", L, n))
                        for t in tiles:
                            g = v(f"q_norm{l}", t) if n == 0 else v(f"kv_norm{l}", t - 3)
                            nc.vector.scalar_tensor_tensor(cqkv[:, t, :], cqkv[:, t, :], g, rstd[:, 1, 256 * n:256 * n + 256],
                                                           ALU.mult, ALU.mult).then_inc(*sig("cn_raw", L, t))
                    prepare(2)
                    for t in range(5):
                        ve.wait_ge(*due("cn_hi", L, t))
                        nc.vector.tensor_tensor(cn_lo[:, t, :], cqkv[:, t, :], cn_hi[:, t, :].bitcast(F32), ALU.subtract).then_inc(
                            *sig("cn_lo", L, t))
                    prepare(3)
                    ve.wait_ge(*due("ggate", L))
                    nc.vector.tensor_scalar(lsum, ps(("ggate", L))[:, 0:256], v(f"gla_b{l}"), None, ALU.add).then_inc(*sig("ggate_in", L, frees=("ggate", L)))
                    prepare()
                    ve.wait_ge(*due("kr_rot", L))
                    rotate(qh[:, 6, :], ps(("kr_rot", L))[:, 0:256], k("mlacos"), k("mlasin"), 1, "kr_in", L, frees=("kr_rot", L))
                    for i in range(2):
                        last = nc.vector.tensor_scalar(kr2[:, i, :], qh[:, 6, :], k("ones64", 127 * i, 127 * i + 1), None, ALU.mult)
                    last.then_inc(*sig("kr2", L))
                    ve.wait_ge(*due("rqk_rot", L))
                    rotate(gr[:, 512:1024], ps(("rqk_rot", L))[:, :], k("retcos"), k("retsin"), 2, "rqk_in", L, frees=("rqk_rot", L))
                    for hd in range(4):
                        last = nc.vector.tensor_scalar(kbd[:, hd, :], rk, k("headmask", hd, hd + 1), 32.0 ** -0.5, ALU.mult, ALU.mult)
                    last.then_inc(*sig("rkbd", L))
                    ve.wait_ge(*due("lsig", L, 2))
                    step(nc.vector.scalar_tensor_tensor(tmp[:, 0:256], lsum, 0.0, expk, ALU.min, ALU.subtract))
                    step(nc.vector.tensor_tensor_scan(lsum, k("ones", 0, 1).to_broadcast([P, S]), tmp[:, 0:256], 0.0, ALU.mult, ALU.add))
                    middle = lsum.rearrange("p (j s) -> p j s", j=4)[:, :, 31]
                    nc.vector.tensor_scalar(mid[:, 0:4], middle, 1.0 / 16, None, ALU.mult)
                    nc.vector.tensor_scalar(mid[:, 4:8], middle, -1.0 / 16, None, ALU.mult).then_inc(*sig("gmid", L))
                    ve.wait_ge(*due("qr_rot", L))
                    rotate(flat(qh[:, 4:6, :]), ps(("qr_rot", L))[:, :], k("mlacos"), k("mlasin"), 2, "qr_in", L, frees=("qr_rot", L))
                    for hd in range(4):
                        ve.wait_ge(*due("rscore", L, hd))
                        nc.vector.tensor_tensor(attT[:, hd, 0:256], ps(("rscore", L, hd))[:, 0:256], k("decay", 256 * hd, 256 * hd + 256), ALU.mult)
                        nc.vector.tensor_tensor(attT[:, hd, 256:384], ps(("rscore", L, hd))[:, 256:384], k("decay", 256 * hd, 256 * hd + 128),
                                                ALU.mult).then_inc(*sig("ratt", L, hd, frees=("rscore", L, hd)))
                    args = lambda n: (2, 256, 256) if n < 2 else (4, 128, 128)
                    sc_ = 192.0 ** -0.5
                    softmax(L, 0, *args(0), sc_, k("causal2"), prob2, None, 2)
                    softmax(L, 1, *args(1), sc_, k("causal2"), prob2, None, 2)
                    ve.wait_ge(*due("gexp", L))
                    ve.wait_ge(*due("gqk_raw", L))
                    for J in range(4):
                        nc.vector.tensor_tensor(expq[:, J, 64 * J:256], expq[:, J, 64 * J:256], gq[:, 64 * J:256], ALU.mult)
                        if J % 2:
                            nc.vector.memset(expq[:, J, 64 * J - 64:64 * J], 0.0)
                    for hd in range(4):
                        if hd == 0:
                            ve.wait_ge(*due("rscore", L, 3))
                        last = nc.vector.scalar_tensor_tensor(kbd[:, hd, :], gk, k("headmask", hd, hd + 1), expk, ALU.mult, ALU.mult)
                    last.then_inc(*sig("gkbd", L))
                    normalize(L, 0, *args(0), prob2, 2)
                    softmax(L, 2, *args(2), sc_, k("causal2", P, 2 * P), prob2, None, 2)
                    normalize(L, 1, *args(1), prob2, 2)
                    ve.wait_ge(*due("rout", L))
                    for hd in range(4):
                        ve.wait_ge(*due("gscore", L, hd))
                        nc.vector.tensor_tensor(attT[:, hd, 0:256], ps(("gscore", L, hd))[:, 0:256], k("glamask"), ALU.mult)
                        nc.vector.tensor_tensor(attT[:, hd, 256:384], ps(("gscore", L, hd))[:, 256:384], k("glamask", 0, P),
                                                ALU.mult).then_inc(*sig("gatt", L, hd, frees=("gscore", L, hd)))
                    normalize(L, 2, *args(2), prob2, 2)
                    prepare(2)
                    order = (3, 2, 0, 1)
                    for m, n in enumerate(order):
                        ve.wait_ge(*due("h_rstd", L, n))
                        for j in range(2):
                            t = 2 * n + j
                            g = v(f"ret_out{l}", j) if n == 3 else v(f"gla_out{l}", j) if n == 2 else v(f"mla_out{l}", t)
                            last = nc.vector.scalar_tensor_tensor(raw[:, t, :], raw[:, t, :], g, rstd[:, m % 2, 256 * j:256 * (j + 1)],
                                                                  ALU.mult, ALU.mult)
                            if n >= 2:
                                step(last)
                                ve.wait_ge(*due("gates", L, 1))
                                last = nc.vector.tensor_tensor(raw[:, t, :], raw[:, t, :], gates[:, t - 4, :], ALU.mult)
                            last.then_inc(*sig("cat_raw", L, t))
                        if m >= 1:
                            cat_lo(L, (2 * order[m - 1], 2 * order[m - 1] + 1))
                    cat_lo(L, (2, 3))
                    for p_ in range(4):
                        add_residual(L, 0, p_)
                        prepare()
                    apply(("ffn", L), lambda t: v(f"ffn_norm{l}", t))
                lag = 1 if L < 2 else 2
                for f in range(1, FT + lag + 2):
                    if L >= 2 and f - 1 < FT:
                        g = f - 1
                        bank, c = ps(("gu", L, g)), conv[:, g % 2, :]
                        ve.wait_ge(*due("conv0", L, g))
                        step(nc.vector.scalar_tensor_tensor(c[:, 1:S], bank[:, 0:S - 1], v(f"conv_w{l}", 22 + g), c[:, 1:S], ALU.mult, ALU.add))
                        nc.vector.scalar_tensor_tensor(c[:, 2:S], bank[:, 0:S - 2], v(f"conv_w{l}", g), c[:, 2:S],
                                                       ALU.mult, ALU.add).then_inc(*sig("conv", L, g))
                    g = f - lag
                    if 0 <= g < FT:
                        ve.wait_ge(*due("silu", L, g))
                        if g >= 2:
                            ve.wait_ge(*due("hid_lo", L, g - 2))
                        nc.vector.tensor_tensor(hidden[:, g % 2, :], silu[:, g % 2, :], ps(("gu", L, g))[:, 256:512], ALU.mult).then_inc(
                            *sig("hidden", L, g, frees=("gu", L, g)))
                    g = f - lag - 1
                    if 0 <= g < FT:
                        ve.wait_ge(*due("hid_hi", L, g))
                        nc.vector.tensor_tensor(hid_lo[:, g, :], hidden[:, g % 2, :], hid_hi[:, g, :].bitcast(F32), ALU.subtract).then_inc(
                            *sig("hid_lo", L, g))
                    if f <= FT:
                        prepare()
                if L < 2:
                    prepare(8)
                    gain(L, 3)
                    update_post(L, 1, 3)
                else:
                    for p_ in range(4):
                        prepare()
                        add_residual(L, 1, p_)
                        prepare()
            ve.wait_ge(*due("rstd", ("final", 0)))
            for t in range(KT):
                last = nc.vector.scalar_tensor_tensor(raw[:, t, :], x[:, t, :], v("final", t), rstd[:, 0, 0:256], ALU.mult, ALU.mult)
                if t % 2:
                    last.then_inc(*sig("out_ready", t // 2))


def kernel(**inputs):
    import concourse.bacc as bacc
    from concourse.bass_utils import run_bass_kernel_spmd as run

    a = {n: np.asarray(v) for n, v in inputs.items()}
    const, const_at = const_table()
    arrays = {
        "x_t": np.ascontiguousarray(a["x"][0].T.reshape(KT, P, S).transpose(1, 0, 2)),
        "positions": np.ascontiguousarray(a["positions"]),
        "const_table": np.ascontiguousarray(const),
        "vectors": pack_vectors(a),
        "weights": pack_weights(a),
        "bias_rows": np.ascontiguousarray(a["b_in"][:, 640:1280]),
        "sink_rows": np.ascontiguousarray(a["sinks"]),
        "gate_w": np.ascontiguousarray(a["gla_w_gate_2"]),
        "pool_w": np.ascontiguousarray(a["pool_w"]),
    }
    counts = Counts()
    for _ in range(2):
        nc = bacc.Bacc("TRN2", target_bir_lowering=False, num_devices=1)
        t = {n: nc.dram_tensor(n, v.shape, mybir.dt.from_np(v.dtype), kind="ExternalInput").ap() for n, v in arrays.items()}
        out = nc.dram_tensor("out_t", (P, KT, S), F32, kind="ExternalOutput").ap()
        build(nc, counts, t["x_t"], t["positions"], t["const_table"], const_at, t["vectors"], t["weights"], t["bias_rows"],
              t["sink_rows"], t["gate_w"], t["pool_w"], out)
    r = run(nc, [arrays], core_ids=[0])
    got = r.results[0]["out_t"]
    return got.transpose(1, 0, 2).reshape(D, S).T.reshape(1, S, D)
```

```python
from contextlib import ExitStack

import numpy as np

import concourse.bass as bass
from concourse import mybir

F32 = mybir.dt.float32
F32R = mybir.dt.float32r
I32 = mybir.dt.int32
ALU = mybir.AluOpType
ACT = mybir.ActivationFunctionType
AX_X = mybir.AxisListType.X

P = 128
S = 256
D = 1024
KT = D // P
NL = 4
FF = 2816
FT = FF // P
EPS = 1e-6
NEG = -1e30
HEADS = 8
HEAD_DIM = 64
ROT = 16
POOLS = (2, 4, 8, 16)
SLOT = FF
NRAW = 3
NSPLIT = 2
NADA = 24


def const_table():
    parts, at = [], {}

    def put(name, a):
        a = np.asarray(a, np.float32).reshape(P, -1)
        start = sum(b.shape[1] for b in parts)
        at[name] = (start, start + a.shape[1])
        parts.append(a)

    def rot_matrix(period, half):
        r = np.zeros((P, P))
        for m in range(P):
            o = m % period
            if o < half:
                r[m + half, m] = -1.0
            elif o < 2 * half:
                r[m - half, m] = 1.0
        return r

    def rope(dim, base, copies):
        inv = base ** (-(np.arange(0, dim, 2, dtype=np.float32) / dim))
        ang = (np.arange(S, dtype=np.float32)[:, None] * inv[None, :].astype(np.float32)).astype(np.float32)
        c, s = np.cos(ang).T, np.sin(ang).T
        return np.tile(np.concatenate([c, c]), (copies, 1)), np.tile(np.concatenate([s, s]), (copies, 1))

    i = np.arange(P)
    put("ident", np.eye(P))
    put("ones", np.ones((P, P)))
    inv = np.float32(500000.0) ** (-np.arange(0, ROT, 2, dtype=np.float32) / np.float32(ROT))
    freq = np.zeros(P)
    for m in range(P):
        if m % HEAD_DIM < ROT:
            freq[m] = inv[m % HEAD_DIM % (ROT // 2)]
    put("freq", freq)
    put("eps", np.full(P, EPS))
    put("ones64", (i[:, None] // 64 == i[None, :] // 64))
    put("rot16", rot_matrix(HEAD_DIM, ROT // 2))
    put("rot64", rot_matrix(64, 32))
    put("rot32", rot_matrix(32, 16))
    k2 = np.arange(2 * P)
    diff = i[:, None] + P - k2[None, :]
    put("window", np.where((diff >= 0) & (diff < P), 0.0, NEG))
    put("causal2", np.where(diff >= 0, 0.0, NEG))
    t = np.arange(S)
    band = []
    for w in POOLS:
        full = ((t[None, :] - t[:, None] >= 0) & (t[None, :] - t[:, None] < w)) / np.minimum(t + 1.0, w)[None, :] - np.eye(S)
        band += [full[:P, :], full[P:, P:]]
    put("band", np.concatenate(band, 1))
    lower = (t[None, :] >= i[:, None]).astype(float)
    put("glamask", lower)
    decay = []
    for h in range(4):
        g = np.log(1.0 - 2.0 ** (-5.0 - h))
        d = np.where(t[None, :] >= i[:, None], np.exp(g * np.maximum(t[None, :] - i[:, None], 0)), 0.0)
        decay.append(d)
    put("decay", np.concatenate(decay, 1))
    for name, (c, s) in (("mla", rope(64, 10000.0, 2)), ("ret", rope(32, 10000.0, 4))):
        put(name + "cos", c)
        put(name + "sin", s)
    put("headmask", (i[:, None] // 32 == np.arange(4)[None, :]))
    return np.concatenate(parts, 1), at


VECTORS = []
for _l in range(2):
    VECTORS += [(f"ada_b{_l}", 48), (f"g_pre_mix{_l}", 8), (f"g_post_mix{_l}", 8), (f"g_pre_ffn{_l}", 8),
                (f"g_post_ffn{_l}", 8), (f"b_qk{_l}", 5), (f"pool_scale{_l}", 4)]
for _l in range(2):
    VECTORS += [(f"attn_norm{_l}", 8), (f"q_norm{_l}", 3), (f"kv_norm{_l}", 2), (f"mla_out{_l}", 4),
                (f"gla_b{_l}", 1), (f"gla_out{_l}", 2), (f"ret_out{_l}", 2), (f"ffn_norm{_l}", 8),
                (f"conv_w{_l}", 66), (f"conv_b{_l}", 22)]
VECTORS += [("final", 8)]
COL, _n = {}, 0
for _name, _t in VECTORS:
    COL[_name] = _n
    _n += _t
NVEC = (_n + P - 1) // P


ADA_AFTER = {("qk", 0, 0): [(0, 8)], ("qk", 0, 1): [(0, 9)], ("st", 0, 0): [(0, 10), (0, 11)], ("st", 0, 1): [(0, 12), (0, 13)],
             ("wo", 0, 0): [(0, 14)], ("wo", 0, 1): [(0, 15)], ("wo", 0, 2): [(0, 16), (0, 17)], ("wo", 0, 3): [(0, 18), (0, 19)]}
_slots = [("gu", 0, _f) for _f in range(1, 22) if _f % 4 != 0] + [("wd", 0, _i) for _i in range(0, 7)] + [("wo", 1, _i) for _i in (0, 1, 2)]
ADA_AFTER.update({_s: [_u] for _s, _u in zip(_slots, [(0, 20 + _i) for _i in range(4)] + [(1, _i) for _i in range(20)])})
ADA_AFTER.update({("gu", 1, 4 + 4 * _i): [(1, 20 + _i)] for _i in range(4)})


def unit_list():
    units = []

    def add(kind, L, i, kt, cols, *ada):
        units.append(((kind, L, i), kt, cols))
        units.extend((("ada", l, n), KT, 256) for l, n in ada)

    units += [(("ada", 0, n), KT, 256) for n in range(8)]
    for L in range(2):
        for i, cols in ((2, 128), (0, 256), (1, 256)):
            add("qk", L, i, KT, cols, *ADA_AFTER.get(("qk", L, i), ()))
        for i in range(2):
            add("st", L, i, KT, 320, *ADA_AFTER.get(("st", L, i), ()))
        for i in range(4):
            add("wo", L, i, KT, 256, *ADA_AFTER.get(("wo", L, i), ()))
        for f in range(FT):
            add("gu", L, f, KT, 256, *ADA_AFTER.get(("gu", L, f), ()))
        for m in range(KT):
            add("wd", L, m, FT, 128, *ADA_AFTER.get(("wd", L, m), ()))
    for L in range(2, 4):
        for kind, i, kt, cols in (("z0", 0, KT, 256), ("z0", 1, KT, 256), ("z0", 2, KT, 128), ("kr", 0, KT, 128), ("gqk", 0, KT, 256),
                                  ("rqk", 0, KT, 256), ("uq", 0, 3, 768), ("ukv", 0, 2, 1024), ("glr", 0, KT, 128), ("gv", 0, KT, 256),
                                  ("rv", 0, KT, 256), ("gg", 0, KT, 256), ("rg", 0, KT, 256)):
            add(kind, L, i, kt, cols)
        for i in range(4):
            add("wo", L, i, KT, 256)
        for f in range(FT):
            add("gu", L, f, KT, 256)
        for m in range(KT):
            add("wd", L, m, FT, 128)
    return units


UNITS = unit_list()
UNIT_NO = {u[0]: n for n, u in enumerate(UNITS)}
SPLITS = [u[0] for u in UNITS if u[0][0] != "ada"]
SPLIT_NO = {u: n for n, u in enumerate(SPLITS)}


def tiled(w):
    rows, cols = w.shape
    return w.reshape(rows // P, P, cols).transpose(1, 0, 2).reshape(P, -1)


def pack_weights(a):
    heads = [h for j in range(4) for h in (j, j + 4)]
    out = []
    sizes = (384, 256, 64, 128, 128, 256, 16, 256, 128, 128, 256, 256)
    for (kind, L, i), kt, cols in UNITS:
        l = L % 2
        c = slice(256 * i, 256 * (i + 1))
        if kind == "ada":
            out.append(np.concatenate([a["ada_w"][l][:, c][:, P * f:P * (f + 1)].T for f in range(2)], 1).ravel())
            continue
        elif kind == "qk":
            q = a["w_in"][l][:, :512].reshape(D, HEADS, HEAD_DIM)[:, heads].reshape(D, 512)
            w = np.concatenate([q, a["w_in"][l][:, 512:640]], 1)[:, 256 * i:256 * i + cols]
        elif kind == "st":
            w = a["w_in"][l][:, 640 + 320 * i:960 + 320 * i]
        elif kind == "wo" and L < 2:
            att = a["w_out"][l][:512].reshape(HEADS, HEAD_DIM, D)[heads].reshape(512, D)
            w = np.concatenate([att, a["w_out"][l][512:]], 0)[:, c]
        elif kind == "wo":
            w = a["w_out_2"][l][:, c]
        elif kind == "gu":
            one, two = (a["w_gate"][l], a["w_up"][l]) if L < 2 else (a["ffn_w_up_2"][l][:, :FF], a["ffn_w_up_2"][l][:, FF:])
            w = np.concatenate([one[:, P * i:P * (i + 1)], two[:, P * i:P * (i + 1)]], 1)
        elif kind == "wd":
            w = (a["w_down"] if L < 2 else a["ffn_w_down_2"])[l][:, P * i:P * (i + 1)]
        elif kind == "uq":
            w = a["mla_w_uq_2"][l].reshape(384, 4, 192)
            w = np.concatenate([w[:, :, :128].reshape(384, 512), w[:, :, 128:].reshape(384, 256)], 1)
        elif kind == "ukv":
            w = a["mla_w_ukv_2"][l].reshape(256, 4, 256)
            w = np.concatenate([w[:, :, :128].reshape(256, 512), w[:, :, 128:].reshape(256, 512)], 1)
        else:
            cq, ckv, kr, gq, gk, gv, glr, gg, rq, rk, rv, rg = np.split(a["w_in_2"][l], np.cumsum(sizes)[:-1], 1)
            w = {"z0": lambda: np.concatenate([cq, ckv], 1)[:, 256 * i:256 * i + cols], "kr": lambda: np.concatenate([kr, kr], 1),
                 "gqk": lambda: np.concatenate([gq, gk], 1), "rqk": lambda: np.concatenate([rq, rk], 1),
                 "glr": lambda: np.concatenate([glr, np.zeros((D, P - 16), glr.dtype)], 1), "gg": lambda: gg, "rg": lambda: rg,
                 "gv": lambda: gv, "rv": lambda: rv}[kind]()
        w = tiled(w)
        assert w.shape == (P, kt * cols), (kind, w.shape)
        out.append(w.ravel())
    return np.concatenate(out)


def pack_vectors(a):
    heads = [h for j in range(4) for h in (j, j + 4)]
    rows = []
    for name, tiles in VECTORS:
        base, l = (name[:-1], int(name[-1])) if name[-1].isdigit() else (name, 0)
        v = {
            "ada_b": lambda: a["ada_b"][l], "b_qk": lambda: np.concatenate(
                [a["b_in"][l][:512].reshape(HEADS, HEAD_DIM)[heads].ravel(), a["b_in"][l][512:640]]),
            "attn_norm": lambda: a["attn_norm_2"][l], "q_norm": lambda: a["mla_q_norm_2"][l],
            "kv_norm": lambda: a["mla_kv_norm_2"][l], "mla_out": lambda: a["mla_out_norm_2"][l],
            "gla_b": lambda: a["gla_b_gate_2"][l], "gla_out": lambda: a["gla_out_norm_2"][l],
            "ret_out": lambda: a["ret_out_norm_2"][l], "ffn_norm": lambda: a["ffn_norm_2"][l],
            "conv_w": lambda: a["ffn_conv_w_2"][l], "conv_b": lambda: a["ffn_conv_b_2"][l],
            "final": lambda: a["final_norm_2"],
        }.get(base, lambda: a[base][l])()
        rows.append(np.asarray(v).reshape(tiles, P))
    rows = np.concatenate(rows)
    rows = np.concatenate([rows, np.zeros((NVEC * P - len(rows), P), rows.dtype)])
    return np.ascontiguousarray(rows.reshape(NVEC, P, P).transpose(1, 0, 2).reshape(P, NVEC * P))


class Counts:

    def __init__(self):
        self.value = {}
        self.freed_by = {}
        self.last_use = {}


def build(nc, counts, a_x, a_pos, a_const, const_at, a_vec, a_w, a_bias, a_sinks, a_gatew, a_poolw, a_c, out):
    ctx = ExitStack()
    with ctx:
        def sb(name, shape, dt=F32):
            return ctx.enter_context(nc.sbuf_tensor(name, shape, dt))

        psum = [ctx.enter_context(nc.psum_tensor(f"bank{b}", [P, 512], F32)) for b in range(8)]

        sems, so_far = {}, {}

        def sem(name):
            if name not in sems:
                sems[name] = ctx.enter_context(nc.semaphore(name))
                so_far[name] = 0
            return sems[name]

        def sig(name, *key, frees=None, by=1):
            s = sem(name)
            so_far[name] += by
            counts.value[(name, *key)] = so_far[name]
            if frees is not None:
                counts.freed_by[frees] = (name, *key)
            return s, by

        def due(name, *key):
            return sem(name), counts.value.get((name, *key), 1)

        raw_w = sb("raw_w", [P, NRAW, SLOT])
        hi_w = sb("hi_w", [P, NSPLIT, SLOT], F32R)
        lo_w = sb("lo_w", [P, NSPLIT, SLOT], F32R)
        const = sb("const", [P, a_const.shape[1]])
        vcol = sb("vcol", [P, NVEC * P])
        x = sb("x", [P, KT, S])
        raw = sb("raw", [P, KT, S])
        in_hi = sb("in_hi", [P, KT, S], F32R)
        in_lo = sb("in_lo", [P, KT, S], F32R)
        silu = sb("silu", [P, 2, S])
        hidden = sb("hidden", [P, 2, S])
        shared = sb("shared", [P, 1536])
        bias_vu = shared[:, 0:1280].rearrange("p (l n) -> p l n", l=2)
        gates = shared[:, 0:1024].rearrange("p (t s) -> p t s", t=4)
        conv = shared[:, 1024:1536].rearrange("p (b s) -> p b s", b=2)
        rstd = sb("rstd", [P, 2, 512])
        c_row = sb("c_row", [P, D])
        mods = sb("mods", [P, 2, 48])
        gains = sb("gains", [P, 2, 4, KT])
        rope1 = sb("rope1", [P, 2, S])
        sinks = sb("sinks", [P, 2, HEADS])
        gatew = sb("gatew", [16, 2, P])
        poolw = sb("poolw", [P, 2, 4, P])
        tmp2 = sb("tmp", [P, 2, 512])
        tmp = tmp2[:, 0, :]
        smax = sb("smax", [P, 6, 4])
        ssum = sb("ssum", [P, 6, 4])

        def overlay(*tensors):
            with ExitStack() as own:
                return [own.enter_context(nc.sbuf_tensor(name, [P, n], dt)) for name, n, dt in tensors]

        start, = overlay(("start", 2560, F32))
        vrow = start[:, 0:NVEC * P]
        pos_i = start[:, 1024:1280].bitcast(I32)
        ang = start[:, 1280:1536]
        turns = start[:, 1536:2048].rearrange("p (i s) -> p i s", i=2)
        whole, part = start[:, 2048:2304], start[:, 2304:2560]

        hid_hi, hid_lo = (t[:, :].rearrange("p (t s) -> p t s", t=FT) for t in overlay(("hid_hi", FT * S, F32R), ("hid_lo", FT * S, F32R)))

        qk, tok, prob, probT, pooled = overlay(("qk", 1280, F32), ("tok", 1280, F32), ("prob", 6 * 516, F32),
                                               ("probT", 6 * 512, F32), ("pooled", 1024, F32))
        qk = qk[:, :].rearrange("p (t s) -> p t s", t=5)
        tok = tok[:, :].rearrange("p (b n) -> p b n", b=2)
        prob = prob[:, :].rearrange("p (b n) -> p b n", b=6)
        probT = probT[:, :].rearrange("p (b n) -> p b n", b=6)
        pooled = pooled[:, :].rearrange("p (g s) -> p g s", g=4)

        cqkv, cn_hi, cn_lo, mla, vgr, gr = overlay(("cqkv", 1280, F32), ("cn_hi", 1280, F32R), ("cn_lo", 1280, F32R), ("mla", 2816, F32),
                                                   ("vgr", 1024, F32), ("gr", 3336, F32))
        _, prob2, probT2 = overlay(("cqkv_under", 1280, F32), ("prob2", 1024, F32), ("probT2", 1536, F32))
        kn = cqkv[:, 0:1024].rearrange("p (t s) -> p t s", t=4)
        cqkv = cqkv[:, :].rearrange("p (t s) -> p t s", t=5)
        cn_hi = cn_hi[:, :].rearrange("p (t s) -> p t s", t=5)
        cn_lo = cn_lo[:, :].rearrange("p (t s) -> p t s", t=5)
        prob2 = prob2[:, :].rearrange("p (b n) -> p b n", b=2)
        probT2 = probT2[:, :].rearrange("p (b n) -> p b n", b=3)
        head_sq = mla[:, 0:2048].rearrange("p (b n) -> p b n", b=4)
        qh = mla[:, 0:1792].rearrange("p (t s) -> p t s", t=7)
        vm = mla[:, 1792:2816].rearrange("p (b n) -> p b n", b=2)
        vgr = vgr[:, :].rearrange("p (b n) -> p b n", b=2)
        gq, gk, rq, rk = (gr[:, 256 * n:256 * (n + 1)] for n in range(4))
        lsum = gr[:, 1024:1280]
        attT = gr[:, 1280:2816].rearrange("p (h n) -> p h n", h=4)
        expk = gr[:, 2816:3072]
        glr = gr[0:16, 3072:3328]
        mid = gr[:, 3328:3336]
        expq = poolw[:, :, :, :].rearrange("p l g d -> p (l g d)").rearrange("p (j s) -> p j s", j=4)
        kbd = c_row[:, :].rearrange("p (h s) -> p h s", h=4)
        kr2 = silu

        def k(name, a=0, b=None):
            lo, hi = const_at[name]
            return const[:, lo + a:(hi if b is None else lo + b)]

        def v(name, i=0, n=1):
            return vcol[:, COL[name] + i:COL[name] + i + n]

        def bcast(ap, n):
            return ap.rearrange("p (o s) -> p o s", o=1).to_broadcast([ap.shape[0], n, ap.shape[1]])

        const_head = const_at["ones64"][0]

        def raw_view(unit):
            n = UNIT_NO[unit]
            return raw_w[:, n % NRAW, 0:UNITS[n][1] * UNITS[n][2]]

        def halves(unit):
            _, kt, cols = UNITS[UNIT_NO[unit]]
            w = kt * cols // 2
            return [slice(0, w), slice(w, 2 * w)]

        block = ctx.enter_context(nc.Block())

        bank_of, occupant = {}, [None] * 8

        def ps(job):
            return psum[bank_of[job]]

        @block.tensor
        def _(pe):
            n_jobs, kept = [0], set()

            def take(job, keep=False):
                while n_jobs[0] % 8 in kept:
                    n_jobs[0] += 1
                b = n_jobs[0] % 8
                n_jobs[0] += 1
                if keep:
                    kept.add(b)
                if occupant[b] is not None and occupant[b] in counts.freed_by:
                    pe.wait_ge(*due(*counts.freed_by[occupant[b]]))
                occupant[b] = job
                bank_of[job] = b
                return psum[b]

            stream = [0]

            def weights(unit, job):
                if SPLIT_NO[unit] >= stream[0]:
                    assert SPLITS[stream[0]] == unit, unit
                    stream[0] += 1
                pe.wait_ge(*due("lo_w", unit, 1))
                counts.last_use[unit] = job
                _, kt, cols = UNITS[UNIT_NO[unit]]
                n = SPLIT_NO[unit] % NSPLIT
                return tuple(w[:, n, 0:kt * cols].rearrange("p (t c) -> p t c", t=kt) for w in (hi_w, lo_w))

            def exact(o, st, mv, start, stop, **kw):
                nc.tensor.matmul(o, st[1], mv[0], start=start, stop=False, **kw)
                nc.tensor.matmul(o, st[0], mv[1], start=False, stop=False, **kw)
                return nc.tensor.matmul(o, st[0], mv[0], start=False, stop=stop, **kw)

            def group(o, pairs):
                for i, (w, r) in enumerate(pairs):
                    last = nc.tensor.matmul(o, w, r, start=(i == 0), stop=(i == len(pairs) - 1))
                return last

            def half(bank, i):
                return bank[:, 256 * i:256 * (i + 1)]

            def sums(N, tiles, ones, src, wait):
                job = ("sums", *N)
                b = take(job)
                for i, t in enumerate(tiles):
                    wait(t)
                    last = nc.tensor.matmul(b[:, 0:256], ones, src[:, t, :], start=(i == 0), stop=(i == len(tiles) - 1))
                last.then_inc(*sig(*job))

            def norm_sums(N):
                sums(N, range(KT), k("ones"), raw, lambda t: pe.wait_ge(*due("squared", N, t // 2)) if t % 2 == 0 else None)

            both = (in_hi, in_lo)

            def product(job, unit, src, wait=None, c0=0, n=2, at=0, first=True, last=True):
                w = weights(unit, job)
                kts = UNITS[UNIT_NO[unit]][1]
                b = take(job, keep=job[0] == "gate" or job[0] == "y" and job[1] < 2) if first else ps(job)
                order = [(i, t) for i in range(n) for t in range(kts)] if wait is None else [(i, t) for t in range(kts) for i in range(n)]
                for i, t in order:
                    if wait is not None and i == 0:
                        wait(t)
                    c = c0 + P * i
                    kw = {} if wait is None or n == 1 else {"skip_group_check": True}
                    done = exact(half(b, at + i), [v_[:, t, c:c + P] for v_ in w], [v_[:, t, :] for v_ in src],
                                 start=(t == 0 and (i == 0 or wait is None)), stop=(t == kts - 1), **kw)
                if last:
                    done.then_inc(*sig(*job))
                else:
                    done.then_inc(*sig("part", unit))
                    counts.last_use[unit] = ("part", unit)

            def part_product(job, unit, tiles, wait, first, last):
                w = weights(unit, job)
                b = take(job, keep=job[1] < 2) if first else ps(job)
                for t in tiles:
                    wait(t)
                    for i in range(2):
                        done = exact(half(b, i), [v_[:, t, P * i:P * (i + 1)] for v_ in w], [in_hi[:, t, :], in_lo[:, t, :]],
                                     start=(first and t == tiles[0] and i == 0), stop=(last and t == tiles[-1]), skip_group_check=True)
                if last:
                    done.then_inc(*sig(*job))

            def token_product(job, unit, src, tb, c0, cols, o0, last, tiles):
                w = weights(unit, job)
                for n, t in enumerate(tiles):
                    done = exact(ps(job)[:, o0:o0 + cols], [v_[:, t, P * tb:P * (tb + 1)] for v_ in src],
                                 [v_[:, n, c0:c0 + cols] for v_ in w], start=(n == 0), stop=(n == len(tiles) - 1))
                if last:
                    done.then_inc(*sig(*job))
                elif tb == 1:
                    done.then_inc(*sig("part", unit))
                    counts.last_use[unit] = ("part", unit)

            def transposes(job, srcs):
                b = take(job)
                for i, s_ in enumerate(srcs):
                    last = nc.tensor.transpose(b[:, P * i:P * (i + 1)], s_, k("ident"))
                last.then_inc(*sig(*job))

            pe.wait_ge(*due("const_in", 0))
            pe.wait_ge(*due("vec_in", 0))
            transposes(("vec",), [vrow[:, P * g:P * (g + 1)] for g in range(NVEC)])

            for L in range(NL):
                h_wait = lambda t: pe.wait_ge(*due("in_lo", ("mix", L), t))
                if L == 0:
                    norm_sums(("mix", L))
                if L < 2:
                    def turn_qk(i):
                        pe.wait_ge(*due("qk_raw", L, i))
                        n = 512 if i < 2 else 256
                        b = take(("qk_rot", L, i))
                        nc.tensor.matmul(b[:, 0:n], k("rot16"), qk[:, 2 * i:2 * i + n // 256, :], start=True, stop=True).then_inc(*sig("qk_rot", L, i))

                    def tokens(u, tb):
                        take(("st", L, u, tb))
                        token_product(("st", L, u, tb), ("st", L, u), both, tb, 0, 320, 0, True, range(KT))

                    product(("qk", L, 2), ("qk", L, 2), both, h_wait, n=1)
                    product(("qk", L, 0), ("qk", L, 0), both)
                    if L == 0:
                        pe.wait_ge(*due("const_rest", 0))
                    turn_qk(2)
                    product(("qk", L, 1), ("qk", L, 1), both)
                    turn_qk(0)
                    tokens(0, 0)
                    turn_qk(1)
                    pe.wait_ge(*due("qk_done", L, 2))
                    for g in range(2):
                        rows = slice(64 * g, 64 * g + 64)
                        for jp in range(2):
                            pe.wait_ge(*due("qk_done", L, jp))
                            job = ("score", L, 2 * g + jp)
                            b = take(job)
                            for j in range(2):
                                last = group(half(b, j), [(qk[rows, 2 * jp + j, P:2 * P], qk[rows, 4, :])])
                            last.then_inc(*sig(*job))
                    tokens(0, 1)
                    for g in range(2):
                        rows = slice(64 * g, 64 * g + 64)
                        job = ("score", L, 4 + g)
                        b = take(job)
                        for j in range(4):
                            last = group(b[:, P * j:P * (j + 1)], [(qk[rows, j, 0:P], qk[rows, 4, 0:P])])
                        last.then_inc(*sig(*job))
                    tokens(1, 0)
                    tokens(1, 1)

                    def turn_prob(n):
                        pe.wait_ge(*due("prob", L, n))
                        p_ = prob[:, n, :]
                        cut = (lambda i: p_[:, 257 * (i // 2) + P * (i % 2):][:, 0:P]) if n < 4 else (lambda i: p_[:, 128 * i + i:][:, 0:P])
                        transposes(("probT", L, n), [cut(i) for i in range(4)])

                    turn_prob(0)
                    turn_prob(1)
                    for i in range(2):
                        pe.wait_ge(*due("tok", L, 1, 1))
                        job = ("pool", L, i)
                        b = take(job)
                        for g in range(2):
                            gi = 2 * i + g
                            o = half(b, g)
                            nc.tensor.matmul(o, tok[:, 0, 128 + P * gi:256 + P * gi], k("band", 384 * gi, 384 * gi + 256), start=True, stop=False)
                            last = nc.tensor.matmul(o[:, P:2 * P], tok[:, 1, 128 + P * gi:256 + P * gi], k("band", 384 * gi + 256, 384 * gi + 384), start=False, stop=True)
                        last.then_inc(*sig(*job))
                    turn_prob(2)
                    pe.wait_ge(*due("poolw_in", 0))
                    for i in range(2):
                        job = ("poolw", L, i)
                        pe.wait_ge(*due("pooled", L, i))
                        b = take(job)
                        for g in range(2):
                            last = group(half(b, g), [(poolw[:, L, 2 * i + g, :], pooled[:, 2 * i + g, :])])
                        last.then_inc(*sig(*job))
                    for n in range(3, 6):
                        turn_prob(n)
                    def attention(jp):
                        job = ("attn", L, jp)
                        b = take(job)
                        for n in (jp, 2 + jp, 4, 5):
                            pe.wait_ge(*due("probT_in", L, n))
                        for j in range(2):
                            for g in range(2):
                                val = lambda kb: tok[:, kb, 64 * g:64 * g + 64]
                                o = b[64 * g:64 * g + 64, 256 * j:256 * (j + 1)]
                                t1 = probT[:, 2 * g + jp, 256 * j:256 * (j + 1)]
                                t0 = probT[:, 4 + g, P * (2 * jp + j):P * (2 * jp + j + 1)]
                                group(o[:, 0:P], [(val(0), t0)])
                                last = group(o[:, P:2 * P], [(val(0), t1[:, 0:P]), (val(1), t1[:, P:2 * P])])
                        last.then_inc(*sig(*job))
                else:
                    product(("z0", L, 0), ("z0", L, 0), both, h_wait)
                    product(("z0", L, 1), ("z0", L, 1), both)
                    product(("z0", L, 2), ("z0", L, 2), both, n=1)
                    product(("kr", L), ("kr", L, 0), both, n=1)
                    for n, tiles in enumerate(((0, 1, 2), (3, 4))):
                        sums(("c", L, n), tiles, k("ones"), raw, lambda t: pe.wait_ge(*due("csq", L, t // 2)))
                    product(("gqk", L), ("gqk", L, 0), both)
                    pe.wait_ge(*due("kr_raw", L))
                    b = take(("kr_rot", L))
                    nc.tensor.matmul(b[:, 0:256], k("rot64"), qh[:, 6, :], start=True, stop=True).then_inc(*sig("kr_rot", L))
                    product(("rqk", L), ("rqk", L, 0), both)
                    cn = (cn_hi, cn_lo)
                    product(("qr", L), ("uq", L, 0), cn, lambda t: pe.wait_ge(*due("cn_lo", L, t)), c0=512)
                    pe.wait_ge(*due("rqk_raw", L))
                    b = take(("rqk_rot", L))
                    nc.tensor.matmul(b[:, :], k("rot32"), gr[:, 512:1024], start=True, stop=True).then_inc(*sig("rqk_rot", L))
                    product(("qn", L, 0), ("uq", L, 0), cn, c0=0)
                    product(("qn", L, 1), ("uq", L, 0), cn, c0=256)
                    pe.wait_ge(*due("qr_raw", L))
                    b = take(("qr_rot", L))
                    nc.tensor.matmul(b[:, :], k("rot64"), qh[:, 4:6, :], start=True, stop=True).then_inc(*sig("qr_rot", L))
                    ckv = tuple(v_[:, 3:5, :] for v_ in cn)
                    product(("kn", L, 0), ("ukv", L, 0), ckv, lambda t: pe.wait_ge(*due("cn_lo", L, 3 + t)), c0=0)
                    product(("kn", L, 1), ("ukv", L, 0), ckv, c0=256)
                    for tb in range(2):
                        take(("vm", L, tb))
                        token_product(("vm", L, tb), ("ukv", L, 0), ckv, tb, 512, 512, 0, True, range(2))
                    product(("glr", L), ("glr", L, 0), both, n=1)
                    pe.wait_ge(*due("kn_in", L, 1))
                    pe.wait_ge(*due("qn_in", L, 1))
                    pe.wait_ge(*due("qr_in", L))
                    pe.wait_ge(*due("kr2", L))
                    for n in range(3):
                        job = ("score", L, n)
                        b = take(job)
                        for i in range(2 if n < 2 else 4):
                            hd = 2 * n + i if n < 2 else i
                            qs, ks, o = (slice(P, 2 * P), slice(0, 256), half(b, i)) if n < 2 else (slice(0, P), slice(0, P), b[:, P * i:P * (i + 1)])
                            last = group(o, [(qh[:, hd, qs], kn[:, hd, ks]), (qh[:, 4 + hd // 2, qs], kr2[:, hd % 2, ks])])
                        last.then_inc(*sig(*job))
                    pe.wait_ge(*due("gatew_in", 0))
                    pe.wait_ge(*due("glr_in", L))
                    b = take(("ggate", L))
                    nc.tensor.matmul(b[:, 0:256], gatew[:, L - 2, :], glr, start=True, stop=True).then_inc(*sig("ggate", L))

                    def token_values(unit):
                        take((unit, L))
                        for tb in range(2):
                            token_product((unit, L), (unit, L, 0), both, tb, 0, 256, 256 * tb, tb == 1, range(KT))

                    def turn_prob(n):
                        pe.wait_ge(*due("prob", L, n))
                        transposes(("probT", L, n), [prob2[:, n % 2, P * i:P * (i + 1)] for i in range(4)])

                    def head_outputs(job, scores, c0):
                        b = take(job)
                        for hd in range(4):
                            pe.wait_ge(*due(scores, L, hd))
                            o = b[64 * (hd % 2):64 * (hd % 2) + 64, 256 * (hd // 2):256 * (hd // 2) + 256]
                            val = lambda jb: vgr[:, jb, c0 + 64 * hd:c0 + 64 * hd + 64]
                            nc.tensor.matmul(o, val(0), attT[:, hd, 0:256], start=True, stop=False)
                            last = nc.tensor.matmul(o[:, P:2 * P], val(1), attT[:, hd, 256:384], start=False, stop=True)
                        last.then_inc(*sig(*job))

                    token_values("gv")
                    pe.wait_ge(*due("rkbd", L))
                    for hd in range(4):
                        job = ("rscore", L, hd)
                        b = take(job)
                        group(b[:, 0:256], [(kbd[:, hd, 0:P], rq)])
                        group(b[:, 256:384], [(kbd[:, hd, P:2 * P], rq[:, P:2 * P])]).then_inc(*sig(*job))
                    turn_prob(0)
                    token_values("rv")
                    pe.wait_ge(*due("rv_in", L))
                    head_outputs(("rout", L), "ratt", 256)
                    turn_prob(1)
                    pe.wait_ge(*due("gkbd", L))
                    for hd in range(4):
                        job = ("gscore", L, hd)
                        b = take(job)
                        for J in range(4):
                            o = b[64 * (J % 2):64 * (J % 2) + 64, 0:256] if J < 2 else b[64 * (J % 2):64 * (J % 2) + 64, 256:384]
                            last = group(o, [(kbd[:, hd, 64 * J:64 * J + 64], expq[:, J, P * (J // 2):])])
                        last.then_inc(*sig(*job))
                    turn_prob(2)
                    pe.wait_ge(*due("vm_in", L, 1))
                    for n in range(2):
                        job = ("attn", L, n)
                        b = take(job)
                        for m in (n, 2):
                            pe.wait_ge(*due("probT_in", L, m))
                        for i in range(2):
                            hd = 2 * n + i
                            val = lambda kb: vm[:, kb, P * hd:P * (hd + 1)]
                            t1 = probT2[:, n, 256 * i:256 * (i + 1)]
                            t0 = probT2[:, 2, P * hd:P * (hd + 1)]
                            group(half(b, i)[:, 0:P], [(val(0), t0)])
                            last = group(half(b, i)[:, P:2 * P], [(val(0), t1[:, 0:P]), (val(1), t1[:, P:2 * P])])
                        last.then_inc(*sig(*job))
                    head_outputs(("gout", L), "gatt", 0)
                    product(("gate", L, 0), ("gg", L, 0), both)
                    for m, (n, ones) in enumerate(((0, "ones"), (1, "ones"), (3, "ones64"), (2, "ones64"))):
                        pe.wait_ge(*due("hsq", L, n))
                        b = take(("hsum", L, n))
                        nc.tensor.matmul(b[:, :], k(ones), head_sq[:, m, :], start=True, stop=True).then_inc(*sig("hsum", L, n))
                    product(("gate", L, 1), ("rg", L, 0), both)
                    kept.clear()

                def summed(N, jobs, finish=True):
                    job = ("sums", *N)
                    for p_ in range(4):
                        jobs(p_)
                        if p_ == 1:
                            b = take(job, keep=True)
                        if p_ >= 1:
                            square_sums(N, b, p_ - 1)
                    if finish:
                        square_sums(N, b, 3).then_inc(*sig(*job))
                    return b

                def square_sums(N, b, p_):
                    pe.wait_ge(*due("squared", N, p_))
                    for t in (2 * p_, 2 * p_ + 1):
                        done = nc.tensor.matmul(b[:, 0:256], k("ones"), raw[:, t, :], start=(t == 0), stop=(t == KT - 1))
                    return done

                cat_wait = lambda t: pe.wait_ge(*due("cat_lo", L, t))

                def mixed(p_):
                    early, late = ((4, 5, 6, 7), (0, 1, 2, 3)) if L < 2 else ((0, 1, 2, 3), (4, 5, 6, 7))
                    if p_ == 0:
                        for q in range(2):
                            part_product(("y", L, 0, q), ("wo", L, q), early, cat_wait, True, False)
                            if L < 2:
                                attention(q)
                    if p_ < 2:
                        part_product(("y", L, 0, p_), ("wo", L, p_), late, cat_wait, False, True)
                    else:
                        product(("y", L, 0, p_), ("wo", L, p_), both)

                sums_bank = summed(("post_mix" if L < 2 else "ffn", L), mixed, finish=L < 2)
                if L < 2:
                    norm_sums(("ffn", L))
                if L < 2:
                    kept.clear()
                for f in range(FT):
                    product(("gu", L, f), ("gu", L, f), both, (lambda t: pe.wait_ge(*due("in_lo", ("ffn", L), t))) if f == 0 else None)
                    if f == 0 and L >= 2:
                        square_sums(("ffn", L), sums_bank, 3).then_inc(*sig("sums", "ffn", L))
                        kept.clear()

                def down(p_):
                    hid = (hid_hi, hid_lo)
                    product(("y", L, 1, p_), ("wd", L, 2 * p_), hid, (lambda t: pe.wait_ge(*due("hid_lo", L, t))) if p_ == 0 else None,
                            n=1, last=False)
                    product(("y", L, 1, p_), ("wd", L, 2 * p_ + 1), hid, n=1, at=1, first=False)

                summed(("post_ffn", L) if L < 2 else ("mix", L + 1) if L + 1 < NL else ("final", 0), down)
                if L < 2:
                    norm_sums(("mix", L + 1))
                kept.clear()

        @block.sync
        def _(sp):
            off = 0
            for n, (unit, kt, cols) in enumerate(UNITS):
                if unit == SPLITS[3]:
                    sp.dma_start(const[:, const_head:], a_const[:, const_head:]).then_inc(*sig("const_rest", 0, by=16))
                if n >= NRAW:
                    old = UNITS[n - NRAW][0]
                    sp.wait_ge(*due(*(("ada", old) if old[0] == "ada" else ("lo_w", old, 1))))
                sp.dma_start(raw_view(unit), a_w[off:off + P * kt * cols].rearrange("(p w) -> p w", p=P)).then_inc(
                    *sig(f"raw_w{n % NRAW}", unit, by=16))
                off += P * kt * cols
            for p_ in range(4):
                sp.wait_ge(*due("out_ready", p_))
                sp.dma_start(out[:, 2 * p_:2 * p_ + 2, :], raw[:, 2 * p_:2 * p_ + 2, :]).then_inc(*sig("stored", p_, by=16))
            sp.wait_ge(*due("stored", 3))

        @block.gpsimd
        def _(pool):
            steps = [0]

            def step(ins):
                steps[0] += 1
                ins.then_inc(*sig("pool_step", steps[0]))
                pool.wait_ge(*due("pool_step", steps[0]))

            magic, two_pi = 12582912.0, 6.283185307179586
            parts = (6.28125, 0.0019350051879882812, 3.019915982e-07)
            pool.wait_ge(*due("pos_in", 0))
            pool.wait_ge(*due("const_in", 0))
            step(nc.gpsimd.tensor_copy(ang[:, :], pos_i[:, :]))
            step(nc.gpsimd.tensor_scalar(ang[:, :], ang[:, :], k("freq"), None, ALU.mult))
            for i, quarter in ((0, 0.25), (1, 0.0)):
                step(nc.gpsimd.tensor_scalar(whole, ang[:, :], 1.0 / two_pi, quarter, ALU.mult, ALU.add))
                step(nc.gpsimd.tensor_scalar(whole, whole, magic, None, ALU.add))
                step(nc.gpsimd.tensor_scalar(whole, whole, magic, None, ALU.subtract))
                for n, c in enumerate(parts):
                    step(nc.gpsimd.tensor_scalar(part, whole, c, None, ALU.mult))
                    step(nc.gpsimd.tensor_tensor(turns[:, i, :], ang[:, :] if n == 0 else turns[:, i, :], part, ALU.subtract))
                step(nc.gpsimd.tensor_scalar(turns[:, i, :], turns[:, i, :], quarter * two_pi, -3.1415925, ALU.add, ALU.max))
                nc.gpsimd.tensor_scalar(turns[:, i, :], turns[:, i, :], 3.1415925, None, ALU.min).then_inc(*sig("turns", i))
            pool.wait_ge(*due("ada", ("ada", 0, 6)))
            pool.dma_start(bias_vu[:, :, :], a_bias.rearrange("(o l) n -> o l n", o=1).to_broadcast([P, 2, 640])).then_inc(*sig("bias_in", 0, by=16))
            pool.dma_start(sinks[:, :, :], a_sinks.rearrange("(o l) n -> o l n", o=1).to_broadcast([P, 2, HEADS])).then_inc(*sig("sinks_in", 0, by=16))
            pool.dma_start(poolw[:, :, :, :], a_poolw.rearrange("l g c d -> c l g d")).then_inc(*sig("poolw_in", 0, by=16))
            pool.dma_start(gatew[:, :, :], a_gatew.rearrange("l g n -> g l n")).then_inc(*sig("gatew_in", 0, by=16))

        @block.scalar
        def _(sc):
            sc.dma_start(c_row[:, :], a_c.to_broadcast([P, D])).then_inc(*sig("c_in", 0, by=16))
            sc.dma_start(vrow[:, :], a_vec).then_inc(*sig("vec_in", 0, by=16))
            sc.dma_start(const[:, 0:const_head], a_const[:, 0:const_head]).then_inc(*sig("const_in", 0, by=16))
            sc.dma_start(pos_i[:, :], a_pos.to_broadcast([P, S])).then_inc(*sig("pos_in", 0, by=16))
            sc.dma_start(x[:, :, :], a_x).then_inc(*sig("x_in", 0, by=16))
            sc.preload_act_table_set("silu_and_others")
            sc.wait_ge(*due("c_in", 0))
            nc.scalar.activation(c_row[:, :], c_row[:, :], ACT.Silu).then_inc(*sig("c_act", 0))
            splits = [0]

            def prepare(n=1, parts=(0, 1)):
                for unit in SPLITS[splits[0]:splits[0] + n]:
                    m = splits[0]
                    splits[0] += parts[-1]
                    sc.wait_ge(*due(f"raw_w{UNIT_NO[unit] % NRAW}", unit))
                    if m >= NSPLIT:
                        sc.wait_ge(*due(*counts.last_use.get(SPLITS[m - NSPLIT], ("none",))))
                    for i in parts:
                        cut = halves(unit)[i]
                        nc.scalar.activation(hi_w[:, m % NSPLIT, cut], raw_view(unit)[:, cut], ACT.Identity).then_inc(*sig("hi_w", unit, i))

            def square(N, p_, src_due):
                sc.wait_ge(*src_due)
                if N[0] in ("post_mix", "post_ffn"):
                    src = ps(("y", N[1], 0 if N[0] == "post_mix" else 1, p_))[:, :]
                    dst = raw[:, 2 * p_:2 * p_ + 2, :].rearrange("p t s -> p (t s)")
                else:
                    src, dst = x[:, 2 * p_:2 * p_ + 2, :], raw[:, 2 * p_:2 * p_ + 2, :]
                nc.scalar.activation(dst, src, ACT.Square).then_inc(*sig("squared", N, p_))

            def root(job, name, key, scale, width, dst):
                sc.wait_ge(*due(*job))
                nc.scalar.activation(dst, ps(job)[:, 0:width], ACT.Ln, bias=k("eps"), scale=scale).then_inc(*sig("mean_log", job, frees=job))
                sc.wait_ge(*due("mean_log", job))
                nc.scalar.activation(dst, dst, ACT.Exp, scale=-0.5).then_inc(*sig(name, *key))

            def norm(N, src_due, before=(0, 0, 0, 0), after=(0, 0, 0, 0), split=False):
                for p_ in range(4):
                    prepare(before[p_])
                    last = split and p_ == 3
                    if last:
                        prepare(after[p_], (0,))
                    square(N, p_, src_due(p_))
                    if last:
                        prepare(after[p_], (1,))
                    if p_ == 3:
                        root(("sums", *N), "rstd", (N,), 1.0 / D, 256, rstd[:, 0, 0:256])
                    if not last:
                        prepare(after[p_])

            def round_in(N, shift=None):
                for t in range(KT):
                    sc.wait_ge(*due("scaled", N, t))
                    kw = {} if shift is None else {"bias": shift[:, t:t + 1]}
                    nc.scalar.activation(in_hi[:, t, :], raw[:, t, :], ACT.Identity, **kw).then_inc(*sig("in_hi", N, t))

            def round_cat(L, tiles):
                for t in tiles:
                    sc.wait_ge(*due("cat_raw", L, t))
                    nc.scalar.activation(in_hi[:, t, :], raw[:, t, :], ACT.Identity).then_inc(*sig("cat_hi", L, t))

            def copy(job, dst, src, name, *key, **kw):
                sc.wait_ge(*due(*job))
                return nc.scalar.activation(dst, src, ACT.Identity, **kw).then_inc(*sig(name, *key, frees=job))

            def head_root(L, m, n):
                if m >= 2:
                    sc.wait_ge(*due("cat_raw", L, 2 * m - 3))
                root(("hsum", L, n), "h_rstd", (L, n), 1.0 / (64 if n >= 2 else 128), 512, rstd[:, m % 2, :])

            sc.preload_act_table_set("natural_log_exp_and_others")
            for L in range(NL):
                l = L % 2
                if L == 0:
                    norm(("mix", L), lambda p_: due("x_in", 0))
                    prepare()
                if L < 2:
                    round_in(("mix", L), mods[:, L, 0:8])
                    if L == 0:
                        prepare()
                        sc.preload_act_table_set("trig_and_small")
                        sc.wait_ge(*due("turns", 1))
                        nc.scalar.activation(rope1[:, :, :], turns[:, :, :], ACT.Sin).then_inc(*sig("rope1", 0))
                        sc.preload_act_table_set("natural_log_exp_and_others")
                    for i in (2, 0, 1):
                        for j in range(2 if i < 2 else 1):
                            sc.wait_ge(*due("qk", L, i))
                            last = nc.scalar.activation(qk[:, 2 * i + j, :], ps(("qk", L, i))[:, 256 * j:256 * (j + 1)], ACT.Identity,
                                                        bias=v(f"b_qk{l}", 2 * i + j))
                        last.then_inc(*sig("qk_raw", L, i, frees=("qk", L, i)))
                        prepare()
                    for n in range(6):
                        nh = 2 if n < 4 else 4
                        w = 257 if n < 4 else 129
                        sc.wait_ge(*due("smax", L, n))
                        for i in range(nh):
                            last = nc.scalar.activation(prob[:, n, w * i:w * i + w], prob[:, n, w * i:w * i + w], ACT.Exp,
                                                        bias=smax[:, n, i:i + 1], accum_out=ssum[:, n, i:i + 1])
                        last.then_inc(*sig("exp", L, n))
                        if n == 1:
                            prepare()
                        if n == 4:
                            for i in range(2):
                                copy(("pool", L, i), pooled[:, 2 * i:2 * i + 2, :].rearrange("p t s -> p (t s)"), ps(("pool", L, i))[:, :], "pooled", L, i)
                        if n >= 3:
                            copy(("probT", L, n - 3), probT[:, n - 3, :], ps(("probT", L, n - 3))[:, :], "probT_in", L, n - 3)
                    round_cat(L, range(4, 8))
                    for n in range(3, 5):
                        copy(("probT", L, n), probT[:, n, :], ps(("probT", L, n))[:, :], "probT_in", L, n)
                    prepare()
                    for n in range(5, 6):
                        copy(("probT", L, n), probT[:, n, :], ps(("probT", L, n))[:, :], "probT_in", L, n)
                    for jp in range(2):
                        sc.wait_ge(*due("attn", L, jp))
                        nc.scalar.activation(in_hi[:, 2 * jp:2 * jp + 2, :], ps(("attn", L, jp))[:, :], ACT.Identity).then_inc(*sig("attn_hi", L, jp))
                else:
                    round_in(("mix", L))
                    for i in range(3):
                        n = 2 if i < 2 else 1
                        copy(("z0", L, i), cqkv[:, 2 * i:2 * i + n, :].rearrange("p t s -> p (t s)"), ps(("z0", L, i))[:, 0:256 * n], "c_raw", L, i)
                        prepare()
                    copy(("kr", L), qh[:, 6, :], ps(("kr", L))[:, 0:256], "kr_raw", L)
                    prepare()
                    root(("sums", "c", L, 0), "c_rstd", (L, 0), 1.0 / 384, 256, rstd[:, 1, 0:256])
                    root(("sums", "c", L, 1), "c_rstd", (L, 1), 1.0 / 256, 256, rstd[:, 1, 256:512])
                    for t in range(5):
                        sc.wait_ge(*due("cn_raw", L, t))
                        nc.scalar.activation(cn_hi[:, t, :], cqkv[:, t, :], ACT.Identity).then_inc(*sig("cn_hi", L, t))
                    sc.wait_ge(*due("gqk", L))
                    nc.scalar.activation(gq, ps(("gqk", L))[:, 0:256], ACT.Identity, scale=32.0 ** -0.5)
                    nc.scalar.activation(gk, ps(("gqk", L))[:, 256:512], ACT.Identity).then_inc(*sig("gqk_raw", L, frees=("gqk", L)))
                    prepare()
                    copy(("rqk", L), gr[:, 512:1024], ps(("rqk", L))[:, :], "rqk_raw", L)
                    prepare()
                    copy(("qr", L), qh[:, 4:6, :].rearrange("p t s -> p (t s)"), ps(("qr", L))[:, :], "qr_raw", L)
                    for i in range(2):
                        copy(("qn", L, i), qh[:, 2 * i:2 * i + 2, :].rearrange("p t s -> p (t s)"), ps(("qn", L, i))[:, :], "qn_in", L, i)
                    prepare()
                    for i in range(2):
                        copy(("kn", L, i), kn[:, 2 * i:2 * i + 2, :].rearrange("p t s -> p (t s)"), ps(("kn", L, i))[:, :], "kn_in", L, i)
                    for tb in range(2):
                        copy(("vm", L, tb), vm[:, tb, :], ps(("vm", L, tb))[:, :], "vm_in", L, tb)
                    prepare()
                    copy(("glr", L), glr, ps(("glr", L))[0:16, 0:256], "glr_in", L)
                    prepare()

                    def exp(n):
                        nh, w = (2, 256) if n < 2 else (4, 128)
                        sc.wait_ge(*due("smax", L, n))
                        for i in range(nh):
                            last = nc.scalar.activation(prob2[:, n % 2, w * i:w * (i + 1)], prob2[:, n % 2, w * i:w * (i + 1)], ACT.Exp,
                                                        bias=smax[:, n % 2, i:i + 1], accum_out=ssum[:, n % 2, i:i + 1])
                        last.then_inc(*sig("exp", L, n))

                    def values(unit, c0):
                        copy((unit, L), vgr[:, :, c0:c0 + 256], ps((unit, L))[:, :].rearrange("p (b n) -> p b n", b=2), unit + "_in", L)

                    def probT_in(n):
                        copy(("probT", L, n), probT2[:, n, :], ps(("probT", L, n))[:, :], "probT_in", L, n)

                    def head_in(job, n):
                        copy(job, raw[:, 2 * n:2 * n + 2, :].rearrange("p t s -> p (t s)"), ps(job)[:, :], "o_in", L, n)

                    exp(0)
                    exp(1)
                    sc.wait_ge(*due("ggate_in", L))
                    nc.scalar.activation(expk, lsum, ACT.Abs).then_inc(*sig("lsig", L, 0))
                    sc.wait_ge(*due("lsig", L, 0))
                    nc.scalar.activation(expk, expk, ACT.Exp, scale=-1.0).then_inc(*sig("lsig", L, 1))
                    sc.wait_ge(*due("lsig", L, 1))
                    nc.scalar.activation(expk, expk, ACT.Ln, bias=1.0).then_inc(*sig("lsig", L, 2))
                    values("gv", 0)
                    prepare()
                    probT_in(0)
                    exp(2)
                    sc.wait_ge(*due("gmid", L))
                    for J in range(4):
                        nc.scalar.activation(expq[:, J, 64 * J:256], lsum[:, 64 * J:256], ACT.Exp, bias=mid[:, 4 + J:5 + J], scale=1.0 / 16)
                        last = nc.scalar.activation(expk[:, 64 * J:64 * J + 64], lsum[:, 64 * J:64 * J + 64], ACT.Exp, bias=mid[:, J:J + 1], scale=-1.0 / 16)
                    last.then_inc(*sig("gexp", L))
                    values("rv", 256)
                    prepare()
                    head_in(("rout", L), 3)
                    probT_in(1)
                    probT_in(2)
                    head_in(("attn", L, 0), 0)
                    head_in(("attn", L, 1), 1)
                    head_in(("gout", L), 2)
                    order = (0, 1, 3, 2)
                    for m, n in enumerate(order):
                        sc.wait_ge(*due("o_in", L, n))
                        nc.scalar.activation(head_sq[:, m, :], raw[:, 2 * n:2 * n + 2, :], ACT.Square).then_inc(*sig("hsq", L, n))
                    prepare()
                    head_root(L, 0, 0)
                    head_root(L, 1, 1)
                    head_root(L, 2, 3)
                    head_root(L, 3, 2)
                    sc.wait_ge(*due("gate", L, 1))
                    round_cat(L, (0, 1, 2, 3))
                    prepare()
                    sc.preload_act_table_set("silu_and_others")
                    for i in range(2):
                        sc.wait_ge(*due("gate", L, i))
                        nc.scalar.activation(gates[:, 2 * i:2 * i + 2, :].rearrange("p t s -> p (t s)"), ps(("gate", L, i))[:, :], ACT.Silu).then_inc(
                            *sig("gates", L, i, frees=("gate", L, i)))
                    sc.preload_act_table_set("natural_log_exp_and_others")
                    round_cat(L, (6, 7, 4, 5))
                if L < 2:
                    norm(("post_mix", L), lambda p_: due("y", L, 0, p_), after=(1, 1, L, 1))
                    norm(("ffn", L), lambda p_: due("x", L, 0, p_))
                    round_in(("ffn", L), mods[:, L, 24:32])
                    prepare(1 - L)
                else:
                    for p_ in range(3):
                        square(("ffn", L), p_, due("x", L, 0, p_))
                        prepare()
                    sc.wait_ge(*due("y", L, 0, 3))
                    for t in range(KT):
                        sc.wait_ge(*due("x", L, 0, t // 2))
                        nc.scalar.activation(in_hi[:, t, :], x[:, t, :], ACT.Identity, scale=v(f"ffn_norm{l}", t)).then_inc(
                            *sig("in_hi", ("ffn", L), t))
                    square(("ffn", L), 3, due("x", L, 0, 3))
                    prepare(2)
                    root(("sums", "ffn", L), "rstd", (("ffn", L),), 1.0 / D, 256, rstd[:, 0, 0:256])
                sc.preload_act_table_set("silu_and_others")
                lag = 1 if L < 2 else 2
                for f in range(1, FT + lag + 2):
                    if L >= 2 and 1 < f <= FT:
                        prepare()
                    if L >= 2 and f - 1 < FT:
                        g = f - 1
                        sc.wait_ge(*due("gu_scaled", L, g))
                        if g >= 2:
                            sc.wait_ge(*due("silu", L, g - 2))
                        nc.scalar.activation(conv[:, g % 2, :], tmp2[:, g % 2, 0:256], ACT.Identity, bias=v(f"conv_b{l}", g),
                                             scale=v(f"conv_w{l}", 44 + g)).then_inc(*sig("conv0", L, g))
                    g = f - lag
                    if 0 <= g < FT:
                        sc.wait_ge(*due(*(("gu", L, g) if L < 2 else ("conv", L, g))))
                        if g >= 2:
                            sc.wait_ge(*due("hidden", L, g - 2))
                        src = ps(("gu", L, g))[:, 0:256] if L < 2 else conv[:, g % 2, :]
                        nc.scalar.activation(silu[:, g % 2, :], src, ACT.Silu).then_inc(*sig("silu", L, g))
                    g = f - lag - 1
                    if 0 <= g < FT:
                        sc.wait_ge(*due("hidden", L, g))
                        nc.scalar.activation(hid_hi[:, g, :], hidden[:, g % 2, :], ACT.Identity).then_inc(*sig("hid_hi", L, g))
                    if L < 2 and f <= FT:
                        prepare()
                sc.preload_act_table_set("natural_log_exp_and_others")
                N, src = (("post_ffn", L), (lambda p_: due("y", L, 1, p_))) if L < 2 else \
                    (("mix", L + 1) if L + 1 < NL else ("final", 0), lambda p_: due("x", L, 1, p_))
                norm(N, src, before=(1, 1, 1, 1), after=(1, 1, 1, 1), split=L >= 2)
                if L < 2:
                    norm(("mix", L + 1), lambda p_: due("x", L, 1, p_))

        @block.vector
        def _(ve):
            steps = [0]

            def step(ins):
                steps[0] += 1
                ins.then_inc(*sig("ve_step", steps[0]))
                ve.wait_ge(*due("ve_step", steps[0]))

            flat = lambda ap: ap.rearrange("p t s -> p (t s)")
            splits = [0]
            ada_todo = [u[0] for u in UNITS[:UNIT_NO[SPLITS[0]]]]

            def prepare(n=1, ada=True):
                for unit in SPLITS[splits[0]:splits[0] + n]:
                    m = splits[0]
                    splits[0] += 1
                    for i, cut in enumerate(halves(unit)):
                        ve.wait_ge(*due("hi_w", unit, i))
                        nc.vector.tensor_tensor(lo_w[:, m % NSPLIT, cut], raw_view(unit)[:, cut], hi_w[:, m % NSPLIT, cut].bitcast(F32),
                                                ALU.subtract).then_inc(*sig("lo_w", unit, i))
                    n = UNIT_NO[unit] + 1
                    while n < len(UNITS) and UNITS[n][0][0] == "ada":
                        ada_todo.append(UNITS[n][0])
                        n += 1
                    if ada:
                        ada_work()

            def ada_work(most=None):
                for _ in range(len(ada_todo) if most is None else most):
                    unit = ada_todo.pop(0)
                    _, l, n = unit
                    ve.wait_ge(*due(f"raw_w{UNIT_NO[unit] % NRAW}", unit))
                    w = raw_view(unit).rearrange("p (f k) -> p f k", f=2)
                    for f in range(2):
                        last = nc.vector.scalar_tensor_tensor(w[:, f, :], w[:, f, :], 1.0, c_row[:, :], ALU.mult, ALU.mult,
                                                              accum_out=mods[:, l, 2 * n + f:2 * n + f + 1])
                    last.then_inc(*sig("ada", unit))

            def apply(N, g, shift=None):
                ve.wait_ge(*due("rstd", N))
                for t in range(KT + 2):
                    if t < KT:
                        nc.vector.scalar_tensor_tensor(raw[:, t, :], x[:, t, :], g(t), rstd[:, 0, 0:256], ALU.mult, ALU.mult).then_inc(
                            *sig("scaled", N, t))
                    if t >= 2:
                        u = t - 2
                        ve.wait_ge(*due("in_hi", N, u))
                        hi = in_hi[:, u, :].bitcast(F32)
                        if shift is None:
                            ins = nc.vector.tensor_tensor(in_lo[:, u, :], raw[:, u, :], hi, ALU.subtract)
                        else:
                            ins = nc.vector.scalar_tensor_tensor(in_lo[:, u, :], raw[:, u, :], shift[:, u:u + 1], hi, ALU.add, ALU.subtract)
                        ins.then_inc(*sig("in_lo", N, u))

            def cat_lo(L, tiles):
                for t in tiles:
                    ve.wait_ge(*due("cat_hi", L, t))
                    nc.vector.tensor_tensor(in_lo[:, t, :], raw[:, t, :], in_hi[:, t, :].bitcast(F32), ALU.subtract).then_inc(
                        *sig("cat_lo", L, t))

            def add_residual(L, which, p_):
                ve.wait_ge(*due("y", L, which, p_))
                xs = flat(x[:, 2 * p_:2 * p_ + 2, :])
                nc.vector.tensor_tensor(xs, xs, ps(("y", L, which, p_))[:, :], ALU.add).then_inc(
                    *sig("x", L, which, p_, frees=("y", L, which, p_)))

            def update_post(L, which, gain):
                N = ("post_mix" if which == 0 else "post_ffn", L)
                ve.wait_ge(*due("rstd", N))
                for p_ in range(4):
                    scaled = tmp2[:, p_ % 2, :]
                    if p_ >= 2:
                        ve.wait_ge(*due("x", L, which, p_ - 2))
                    for j in range(2):
                        t = 2 * p_ + j
                        last = nc.vector.scalar_tensor_tensor(scaled[:, 256 * j:256 * (j + 1)], ps(("y", L, which, p_))[:, 256 * j:256 * (j + 1)],
                                                              gains[:, L, gain, t:t + 1], rstd[:, 0, 0:256], ALU.mult, ALU.mult)
                    step(last)
                    xs = flat(x[:, 2 * p_:2 * p_ + 2, :])
                    nc.vector.tensor_tensor(xs, xs, scaled, ALU.add).then_inc(*sig("x", L, which, p_, frees=("y", L, which, p_)))

            def softmax(L, n, nh, w, w1, scale, mask, buf, sink, bufs):
                job = ("score", L, n)
                ve.wait_ge(*due(*job))
                if n >= bufs:
                    ve.wait_ge(*due("probT", L, n - bufs))
                pr = buf[:, n % bufs, 0:nh * w1].rearrange("p (h k) -> p h k", h=nh)
                if sink is not None:
                    nc.vector.tensor_copy(pr[:, :, w], sink)
                nc.vector.scalar_tensor_tensor(pr[:, :, 0:w], ps(job)[:, 0:nh * w].rearrange("p (h k) -> p h k", h=nh), scale,
                                               bcast(mask, nh), ALU.mult, ALU.add).then_inc(*sig("scored", L, n, frees=job))
                ve.wait_ge(*due("scored", L, n))
                step(nc.vector.tensor_reduce(smax[:, n % bufs, 0:nh], pr, AX_X, ALU.max))
                nc.vector.tensor_scalar(smax[:, n % bufs, 0:nh], smax[:, n % bufs, 0:nh], -1.0, None, ALU.mult).then_inc(*sig("smax", L, n))

            def normalize(L, n, nh, w, w1, buf, bufs):
                ve.wait_ge(*due("exp", L, n))
                step(nc.vector.reciprocal(ssum[:, n % bufs, 0:nh], ssum[:, n % bufs, 0:nh]))
                pr = buf[:, n % bufs, 0:nh * w1].rearrange("p (h k) -> p h k", h=nh)
                nc.vector.tensor_tensor(pr[:, :, 0:w], pr[:, :, 0:w], ssum[:, n % bufs, 0:nh].rearrange("p (h o) -> p h o", o=1).to_broadcast([P, nh, w]),
                                        ALU.mult).then_inc(*sig("prob", L, n))

            def rotate(q, rot, cos, sin, n, name, *key, frees):
                w = 256 * n
                r3 = q.rearrange("p (t s) -> p t s", t=n)
                step(nc.vector.tensor_tensor(tmp[:, 0:w].rearrange("p (t s) -> p t s", t=n), rot.rearrange("p (t s) -> p t s", t=n),
                                             bcast(sin, n), ALU.mult))
                step(nc.vector.tensor_tensor(r3, r3, bcast(cos, n), ALU.mult))
                nc.vector.tensor_tensor(q, q, tmp[:, 0:w], ALU.add).then_inc(*sig(name, *key, frees=frees))
                ve.wait_ge(*due(name, *key))

            def gain(L, which):
                start, col, g, op = ((0, 8, "g_pre_mix", None), (16, 16, "g_post_mix", ALU.mult), (24, 32, "g_pre_ffn", None),
                                     (40, 40, "g_post_ffn", ALU.mult))[which]
                ve.wait_ge(*due("ada", ("ada", L, (col + 8) // 2 - 1)))
                both_ = mods[:, L, start:col + 8]
                step(nc.vector.tensor_tensor(both_, both_, v(f"ada_b{L}", start, col + 8 - start), ALU.add))
                m, o, w = mods[:, L, col:col + 8], gains[:, L, which, :], v(f"{g}{L}", 0, 8)
                if op is None:
                    step(nc.vector.scalar_tensor_tensor(o, m, 1.0, w, ALU.add, ALU.mult))
                else:
                    step(nc.vector.tensor_tensor(o, m, w, op))

            ve.wait_ge(*due("c_act", 0))
            ada_work(2)
            ve.wait_ge(*due("vec"))
            nc.vector.tensor_copy(vcol[:, :], ps(("vec",))[:, 0:NVEC * P]).then_inc(*sig("vcol", 0, frees=("vec",)))
            ve.wait_ge(*due("vcol", 0))
            ada_work()
            for L in range(NL):
                l = L % 2
                if L == 0:
                    prepare()
                if L < 2:
                    gain(L, 0)
                    if L == 0:
                        ve.wait_ge(*due("x_in", 0))
                    apply(("mix", L), lambda t: gains[:, L, 0, t:t + 1], mods[:, L, 0:8])
                    def turn_qk(i):
                        n = 2 if i < 2 else 1
                        ve.wait_ge(*due("qk_rot", L, i))
                        rotate(flat(qk[:, 2 * i:2 * i + n, :]), ps(("qk_rot", L, i))[:, 0:256 * n], rope1[:, 0, :], rope1[:, 1, :], n,
                               "qk_done", L, i, frees=("qk_rot", L, i))

                    prepare(2 if L == 0 else 1)
                    if L == 0:
                        ve.wait_ge(*due("rope1", 0))
                        ve.wait_ge(*due("bias_in", 0))
                        ve.wait_ge(*due("sinks_in", 0))
                        ve.wait_ge(*due("const_rest", 0))
                    turn_qk(2)
                    prepare()
                    turn_qk(0)
                    turn_qk(1)
                    prepare()

                    def tokens(u, tb):
                        ve.wait_ge(*due("st", L, u, tb))
                        c = slice(320 * u, 320 * (u + 1))
                        nc.vector.tensor_tensor(tok[:, tb, c], ps(("st", L, u, tb))[:, 0:320], bias_vu[:, l, c], ALU.add).then_inc(
                            *sig("tok", L, u, tb, frees=("st", L, u, tb)))

                    tokens(0, 0)
                    for n in range(7):
                        if n < 6:
                            if n < 4:
                                g, jp = n // 2, n % 2
                                softmax(L, n, 2, 256, 257, 0.125, k("window"), prob, sinks[:, l, 4 * g + 2 * jp:4 * g + 2 * jp + 2], 6)
                            else:
                                softmax(L, n, 4, 128, 129, 0.125, k("causal2", P, 2 * P), prob, sinks[:, l, 4 * (n - 4):4 * (n - 4) + 4], 6)
                        if n >= 1:
                            m = n - 1
                            normalize(L, m, *((2, 256, 257) if m < 4 else (4, 128, 129)), prob, 6)
                        if n == 1:
                            tokens(0, 1)
                        if n == 3:
                            tokens(1, 0)
                            tokens(1, 1)
                        if n == 2:
                            prepare(ada=False)
                    for i in range(2):
                        ve.wait_ge(*due("poolw", L, i))
                        for g in range(2):
                            t = 4 + 2 * i + g
                            nc.vector.tensor_scalar(raw[:, t, :], ps(("poolw", L, i))[:, 256 * g:256 * (g + 1)],
                                                    v(f"pool_scale{l}", 2 * i + g), None, ALU.mult).then_inc(
                                *sig("cat_raw", L, t, frees=("poolw", L, i)))
                    cat_lo(L, range(4, 8))
                    prepare()
                    for jp in range(2):
                        ve.wait_ge(*due("attn_hi", L, jp))
                        for j in range(2):
                            t = 2 * jp + j
                            nc.vector.tensor_tensor(in_lo[:, t, :], ps(("attn", L, jp))[:, 256 * j:256 * (j + 1)], in_hi[:, t, :].bitcast(F32),
                                                    ALU.subtract).then_inc(*sig("cat_lo", L, t, frees=("attn", L, jp)))
                    prepare(2 + L)
                    gain(L, 1)
                    update_post(L, 0, 1)
                    prepare(ada=False)
                    gain(L, 2)
                    apply(("ffn", L), lambda t: gains[:, L, 2, t:t + 1], mods[:, L, 24:32])
                    ada_work()
                    prepare(1 - L)
                else:
                    apply(("mix", L), lambda t: v(f"attn_norm{l}", t))
                    for i in range(3):
                        n = 2 if i < 2 else 1
                        ve.wait_ge(*due("c_raw", L, i))
                        c = cqkv[:, 2 * i:2 * i + n, :]
                        nc.vector.tensor_tensor(raw[:, 2 * i:2 * i + n, :], c, c, ALU.mult).then_inc(*sig("csq", L, i))
                        prepare()
                    prepare()
                    for n, tiles in enumerate(((0, 1, 2), (3, 4))):
                        ve.wait_ge(*due("c_rstd", L, n))
                        for t in tiles:
                            g = v(f"q_norm{l}", t) if n == 0 else v(f"kv_norm{l}", t - 3)
                            nc.vector.scalar_tensor_tensor(cqkv[:, t, :], cqkv[:, t, :], g, rstd[:, 1, 256 * n:256 * n + 256],
                                                           ALU.mult, ALU.mult).then_inc(*sig("cn_raw", L, t))
                    for t in range(5):
                        ve.wait_ge(*due("cn_hi", L, t))
                        nc.vector.tensor_tensor(cn_lo[:, t, :], cqkv[:, t, :], cn_hi[:, t, :].bitcast(F32), ALU.subtract).then_inc(
                            *sig("cn_lo", L, t))
                    ve.wait_ge(*due("kr_rot", L))
                    rotate(qh[:, 6, :], ps(("kr_rot", L))[:, 0:256], k("mlacos"), k("mlasin"), 1, "kr_in", L, frees=("kr_rot", L))
                    for i in range(2):
                        last = nc.vector.tensor_scalar(kr2[:, i, :], qh[:, 6, :], k("ones64", 127 * i, 127 * i + 1), None, ALU.mult)
                    last.then_inc(*sig("kr2", L))
                    prepare(2)
                    ve.wait_ge(*due("rqk_rot", L))
                    rotate(gr[:, 512:1024], ps(("rqk_rot", L))[:, :], k("retcos"), k("retsin"), 2, "rqk_in", L, frees=("rqk_rot", L))
                    for hd in range(4):
                        last = nc.vector.tensor_scalar(kbd[:, hd, :], rk, k("headmask", hd, hd + 1), 32.0 ** -0.5, ALU.mult, ALU.mult)
                    last.then_inc(*sig("rkbd", L))
                    ve.wait_ge(*due("qr_rot", L))
                    rotate(flat(qh[:, 4:6, :]), ps(("qr_rot", L))[:, :], k("mlacos"), k("mlasin"), 2, "qr_in", L, frees=("qr_rot", L))
                    prepare(2)
                    args = lambda n: (2, 256, 256) if n < 2 else (4, 128, 128)
                    sc_ = 192.0 ** -0.5
                    softmax(L, 0, *args(0), sc_, k("causal2"), prob2, None, 2)
                    softmax(L, 1, *args(1), sc_, k("causal2"), prob2, None, 2)
                    ve.wait_ge(*due("ggate", L))
                    nc.vector.tensor_scalar(lsum, ps(("ggate", L))[:, 0:256], v(f"gla_b{l}"), None, ALU.add).then_inc(*sig("ggate_in", L, frees=("ggate", L)))
                    normalize(L, 0, *args(0), prob2, 2)
                    prepare()
                    ve.wait_ge(*due("lsig", L, 2))
                    step(nc.vector.scalar_tensor_tensor(tmp[:, 0:256], lsum, 0.0, expk, ALU.min, ALU.subtract))
                    step(nc.vector.tensor_tensor_scan(lsum, k("ones", 0, 1).to_broadcast([P, S]), tmp[:, 0:256], 0.0, ALU.mult, ALU.add))
                    middle = lsum.rearrange("p (j s) -> p j s", j=4)[:, :, 31]
                    nc.vector.tensor_scalar(mid[:, 0:4], middle, 1.0 / 16, None, ALU.mult)
                    nc.vector.tensor_scalar(mid[:, 4:8], middle, -1.0 / 16, None, ALU.mult).then_inc(*sig("gmid", L))
                    for hd in range(4):
                        ve.wait_ge(*due("rscore", L, hd))
                        nc.vector.tensor_tensor(attT[:, hd, 0:256], ps(("rscore", L, hd))[:, 0:256], k("decay", 256 * hd, 256 * hd + 256), ALU.mult)
                        nc.vector.tensor_tensor(attT[:, hd, 256:384], ps(("rscore", L, hd))[:, 256:384], k("decay", 256 * hd, 256 * hd + 128),
                                                ALU.mult).then_inc(*sig("ratt", L, hd, frees=("rscore", L, hd)))
                    softmax(L, 2, *args(2), sc_, k("causal2", P, 2 * P), prob2, None, 2)
                    normalize(L, 1, *args(1), prob2, 2)
                    prepare()
                    ve.wait_ge(*due("gexp", L))
                    ve.wait_ge(*due("gqk_raw", L))
                    for J in range(4):
                        nc.vector.tensor_tensor(expq[:, J, 64 * J:256], expq[:, J, 64 * J:256], gq[:, 64 * J:256], ALU.mult)
                        if J % 2:
                            nc.vector.memset(expq[:, J, 64 * J - 64:64 * J], 0.0)
                    for hd in range(4):
                        if hd == 0:
                            ve.wait_ge(*due("rscore", L, 3))
                        last = nc.vector.scalar_tensor_tensor(kbd[:, hd, :], gk, k("headmask", hd, hd + 1), expk, ALU.mult, ALU.mult)
                    last.then_inc(*sig("gkbd", L))
                    normalize(L, 2, *args(2), prob2, 2)
                    ve.wait_ge(*due("rout", L))
                    for hd in range(4):
                        ve.wait_ge(*due("gscore", L, hd))
                        nc.vector.tensor_tensor(attT[:, hd, 0:256], ps(("gscore", L, hd))[:, 0:256], k("glamask"), ALU.mult)
                        nc.vector.tensor_tensor(attT[:, hd, 256:384], ps(("gscore", L, hd))[:, 256:384], k("glamask", 0, P),
                                                ALU.mult).then_inc(*sig("gatt", L, hd, frees=("gscore", L, hd)))
                    prepare(2)

                    def head_norm(m, n):
                        ve.wait_ge(*due("h_rstd", L, n))
                        for j in range(2):
                            t = 2 * n + j
                            g = v(f"ret_out{l}", j) if n == 3 else v(f"gla_out{l}", j) if n == 2 else v(f"mla_out{l}", t)
                            nc.vector.scalar_tensor_tensor(raw[:, t, :], raw[:, t, :], g, rstd[:, m % 2, 256 * j:256 * (j + 1)],
                                                           ALU.mult, ALU.mult).then_inc(*sig("cat_raw" if n < 2 else "h_normed", L, t))

                    head_norm(0, 0)
                    head_norm(1, 1)
                    head_norm(2, 3)
                    head_norm(3, 2)
                    cat_lo(L, (0, 1, 2, 3))
                    prepare()
                    for n in (3, 2):
                        ve.wait_ge(*due("h_normed", L, 5))
                        ve.wait_ge(*due("gates", L, n - 2))
                        for t in (2 * n, 2 * n + 1):
                            nc.vector.tensor_tensor(raw[:, t, :], raw[:, t, :], gates[:, t - 4, :], ALU.mult).then_inc(*sig("cat_raw", L, t))
                    cat_lo(L, (6, 7, 4, 5))
                    for p_ in range(4):
                        add_residual(L, 0, p_)
                        if p_ < 3:
                            prepare()
                    for t in range(KT):
                        ve.wait_ge(*due("in_hi", ("ffn", L), t))
                        nc.vector.scalar_tensor_tensor(in_lo[:, t, :], x[:, t, :], v(f"ffn_norm{l}", t), in_hi[:, t, :].bitcast(F32),
                                                       ALU.mult, ALU.subtract).then_inc(*sig("in_lo", ("ffn", L), t))
                    prepare(2)
                lag = 1 if L < 2 else 2
                for f in range(1, FT + lag + 2):
                    if L >= 2 and f - 1 < FT:
                        g = f - 1
                        if g == 0:
                            ve.wait_ge(*due("rstd", ("ffn", L)))
                        ve.wait_ge(*due("gu", L, g))
                        nc.vector.tensor_tensor(tmp2[:, g % 2, :].rearrange("p (h s) -> p h s", h=2),
                                                ps(("gu", L, g))[:, :].rearrange("p (h s) -> p h s", h=2),
                                                rstd[:, 0:1, 0:256].to_broadcast([P, 2, S]), ALU.mult).then_inc(
                            *sig("gu_scaled", L, g, frees=("gu", L, g)))
                        if g > 0:
                            prepare()
                    g = f - lag
                    if 0 <= g < FT:
                        ve.wait_ge(*due("silu", L, g))
                        if g >= 2:
                            ve.wait_ge(*due("hid_lo", L, g - 2))
                        if L < 2:
                            nc.vector.tensor_tensor(hidden[:, g % 2, :], silu[:, g % 2, :], ps(("gu", L, g))[:, 256:512], ALU.mult).then_inc(
                                *sig("hidden", L, g, frees=("gu", L, g)))
                        else:
                            nc.vector.tensor_tensor(hidden[:, g % 2, :], silu[:, g % 2, :], tmp2[:, g % 2, 256:512], ALU.mult).then_inc(
                                *sig("hidden", L, g))
                    g = f - lag - 1
                    if 0 <= g < FT:
                        ve.wait_ge(*due("hid_hi", L, g))
                        nc.vector.tensor_tensor(hid_lo[:, g, :], hidden[:, g % 2, :], hid_hi[:, g, :].bitcast(F32), ALU.subtract).then_inc(
                            *sig("hid_lo", L, g))
                    if L >= 2 and f - 1 < FT:
                        g = f - 1
                        rows, c = tmp2[:, g % 2, :], conv[:, g % 2, :]
                        ve.wait_ge(*due("conv0", L, g))
                        step(nc.vector.scalar_tensor_tensor(c[:, 1:S], rows[:, 0:S - 1], v(f"conv_w{l}", 22 + g), c[:, 1:S], ALU.mult, ALU.add))
                        nc.vector.scalar_tensor_tensor(c[:, 2:S], rows[:, 0:S - 2], v(f"conv_w{l}", g), c[:, 2:S],
                                                       ALU.mult, ALU.add).then_inc(*sig("conv", L, g))
                    if L < 2 and f <= FT:
                        prepare()
                if L < 2:
                    prepare(7)
                    gain(L, 3)
                    update_post(L, 1, 3)
                    prepare()
                else:
                    for p_ in range(4):
                        prepare()
                        add_residual(L, 1, p_)
                        prepare()
            ve.wait_ge(*due("rstd", ("final", 0)))
            for t in range(KT):
                last = nc.vector.scalar_tensor_tensor(raw[:, t, :], x[:, t, :], v("final", t), rstd[:, 0, 0:256], ALU.mult, ALU.mult)
                if t % 2:
                    last.then_inc(*sig("out_ready", t // 2))


def kernel(**inputs):
    import concourse.bacc as bacc
    from concourse.bass_utils import run_bass_kernel_spmd as run

    a = {n: np.asarray(v) for n, v in inputs.items()}
    const, const_at = const_table()
    arrays = {
        "x_t": np.ascontiguousarray(a["x"][0].T.reshape(KT, P, S).transpose(1, 0, 2)),
        "positions": np.ascontiguousarray(a["positions"]),
        "const_table": np.ascontiguousarray(const),
        "vectors": pack_vectors(a),
        "weights": pack_weights(a),
        "bias_rows": np.ascontiguousarray(a["b_in"][:, 640:1280]),
        "sink_rows": np.ascontiguousarray(a["sinks"]),
        "gate_w": np.ascontiguousarray(a["gla_w_gate_2"]),
        "c": np.ascontiguousarray(a["c"]),
        "pool_w": np.ascontiguousarray(a["pool_w"]),
    }
    counts = Counts()
    for _ in range(2):
        nc = bacc.Bacc("TRN2", target_bir_lowering=False, num_devices=1)
        t = {n: nc.dram_tensor(n, v.shape, mybir.dt.from_np(v.dtype), kind="ExternalInput").ap() for n, v in arrays.items()}
        out = nc.dram_tensor("out_t", (P, KT, S), F32, kind="ExternalOutput").ap()
        build(nc, counts, t["x_t"], t["positions"], t["const_table"], const_at, t["vectors"], t["weights"], t["bias_rows"],
              t["sink_rows"], t["gate_w"], t["pool_w"], t["c"], out)
    r = run(nc, [arrays], core_ids=[0])
    got = r.results[0]["out_t"]
    return got.transpose(1, 0, 2).reshape(D, S).T.reshape(1, S, D)
```
